# Optimizing a Trainium2 kernel written in Bass

```python
import jax, jax.numpy as jnp
from jax import lax
import numpy as np

D_MODEL = 1024
BATCH = 1
SEQ = 512
DEPTH = 2

GRID_W = 64

N_FOURIER_GROUPS = 4
FOURIER_GROUP_DIM = 128
D_FOURIER = N_FOURIER_GROUPS * FOURIER_GROUP_DIM

N_Q_HEADS = 8
N_KV_HEADS = 2
HEAD_DIM = 64
D_ATTN = N_Q_HEADS * HEAD_DIM
D_KV = N_KV_HEADS * HEAD_DIM
ROPE_AXIS_DIM = HEAD_DIM // 2
ROPE_THETA = 10000.0
Q_BLOCK = 128

D_GATE = D_MODEL
SPLITS = [D_FOURIER,
          D_FOURIER + D_ATTN,
          D_FOURIER + D_ATTN + D_KV,
          D_FOURIER + D_ATTN + 2 * D_KV,
          D_FOURIER + D_ATTN + 2 * D_KV + D_GATE]
D_IN_PROJ = D_FOURIER + D_ATTN + 2 * D_KV + 2 * D_GATE

PEER_HEADS = 8
PEER_N_KEYS = 128
PEER_N_EXPERTS = PEER_N_KEYS * PEER_N_KEYS
PEER_TOPK = 16
PEER_QUERY_DIM = 256
PEER_HALF = PEER_QUERY_DIM // 2
PEER_TOKEN_BLOCK = 128

DEEPNORM_ALPHA = (2.0 * DEPTH) ** 0.25
DEEPNORM_BETA = (8.0 * DEPTH) ** -0.25

LN_EPS = 1e-5
RMS_EPS = 1e-6

kernel_name = "hybrid_fnet_gqa_peer_deepnorm_encoder"

def layer_norm(x, g, b):
    xf = x.astype(jnp.float32)
    mu = jnp.mean(xf, axis=-1, keepdims=True)
    xc = xf - mu
    var = jnp.mean(xc * xc, axis=-1, keepdims=True)
    return (xc * lax.rsqrt(var + LN_EPS) * g + b).astype(x.dtype)

def rms_norm(x, g):
    xf = x.astype(jnp.float32)
    ms = jnp.mean(xf * xf, axis=-1, keepdims=True)
    return (xf * lax.rsqrt(ms + RMS_EPS) * g).astype(x.dtype)

def axial_rope_tables(seq_len, dtype):
    rows = seq_len // GRID_W
    row_id = jnp.repeat(jnp.arange(rows, dtype=jnp.float32), GRID_W)
    col_id = jnp.tile(jnp.arange(GRID_W, dtype=jnp.float32), rows)
    inv_freq = 1.0 / (ROPE_THETA ** (jnp.arange(0, ROPE_AXIS_DIM, 2, dtype=jnp.float32) / ROPE_AXIS_DIM))
    ang_r = row_id[:, None] * inv_freq[None, :]
    ang_c = col_id[:, None] * inv_freq[None, :]
    ang = jnp.concatenate([ang_r, ang_r, ang_c, ang_c], axis=-1)
    return jnp.cos(ang).astype(dtype), jnp.sin(ang).astype(dtype)

def apply_axial_rope(x, cos, sin):
    xr = x.reshape(*x.shape[:-1], 2, 2, ROPE_AXIS_DIM // 2)
    rot = jnp.concatenate([-xr[..., 1:2, :], xr[..., 0:1, :]], axis=-2).reshape(x.shape)
    return x * cos[None, :, None, :] + rot * sin[None, :, None, :]

def fourier_mix(xf):
    b, s, _ = xf.shape
    xg = xf.reshape(b, s, N_FOURIER_GROUPS, FOURIER_GROUP_DIM).astype(jnp.float32)
    y = jnp.fft.fft2(xg, axes=(1, 3), norm="ortho").real
    return y.reshape(b, s, D_FOURIER).astype(xf.dtype)

def block_attention(q, k, v):
    b, s = q.shape[:2]
    nblk = s // Q_BLOCK
    grp = N_Q_HEADS // N_KV_HEADS
    qb = q.reshape(b, nblk, Q_BLOCK, N_KV_HEADS, grp, HEAD_DIM).transpose(1, 0, 3, 4, 2, 5)
    kt = k.transpose(0, 2, 1, 3)
    vt = v.transpose(0, 2, 1, 3)
    scale = HEAD_DIM ** -0.5

    def one_block(qblk):
        sc = jnp.einsum('bkgqd,bksd->bkgqs', qblk, kt).astype(jnp.float32) * scale
        p = jax.nn.softmax(sc, axis=-1)
        return jnp.einsum('bkgqs,bksd->bkgqd', p.astype(vt.dtype), vt)

    o = lax.map(one_block, qb)
    return o.transpose(1, 0, 4, 2, 3, 5).reshape(b, s, D_ATTN)

def peer_ffn(x, w_query, sub_keys, u_tab, v_tab):
    b, s, d = x.shape
    xt = x.reshape((b * s) // PEER_TOKEN_BLOCK, PEER_TOKEN_BLOCK, d)

    def one_block(xc):
        q = (xc @ w_query).reshape(-1, PEER_HEADS, 2, PEER_HALF)
        s1 = jnp.einsum('thd,hkd->thk', q[:, :, 0], sub_keys[:, 0]).astype(jnp.float32)
        s2 = jnp.einsum('thd,hkd->thk', q[:, :, 1], sub_keys[:, 1]).astype(jnp.float32)
        v1, i1 = lax.top_k(s1, PEER_TOPK)
        v2, i2 = lax.top_k(s2, PEER_TOPK)
        cand = (v1[..., :, None] + v2[..., None, :]).reshape(*v1.shape[:-1], PEER_TOPK * PEER_TOPK)
        cidx = (i1[..., :, None] * PEER_N_KEYS + i2[..., None, :]).reshape(*i1.shape[:-1], PEER_TOPK * PEER_TOPK)
        sv, pos = lax.top_k(cand, PEER_TOPK)
        eidx = jnp.take_along_axis(cidx, pos, axis=-1)
        gate = jax.nn.softmax(sv, axis=-1)
        u = u_tab[eidx]
        act = jax.nn.gelu(jnp.einsum('thkd,td->thk', u, xc), approximate=False)
        w = gate.astype(act.dtype) * act
        vv = v_tab[eidx]
        return jnp.einsum('thk,thkd->td', w, vv)

    return lax.map(one_block, xt).reshape(b, s, d)

def setup_inputs(seed: int = 0) -> dict:
    key = jax.random.key(seed)
    ks = jax.random.split(key, 20)
    nrm = jax.random.normal
    f32 = jnp.float32
    x = nrm(ks[0], (BATCH, SEQ, D_MODEL), f32)
    ln0_g = 1.0 + 0.02 * nrm(ks[1], (D_MODEL,), f32)
    ln0_b = 0.02 * nrm(ks[2], (D_MODEL,), f32)
    w_in = nrm(ks[3], (DEPTH, D_MODEL, D_IN_PROJ), f32) * D_MODEL ** -0.5
    b_gate = 0.01 * nrm(ks[4], (DEPTH, 2, D_MODEL), f32)
    q_norm_g = 1.0 + 0.02 * nrm(ks[5], (DEPTH, HEAD_DIM), f32)
    k_norm_g = 1.0 + 0.02 * nrm(ks[6], (DEPTH, HEAD_DIM), f32)
    w_branch_fourier = nrm(ks[7], (DEPTH, D_FOURIER, D_MODEL), f32) * D_FOURIER ** -0.5
    w_branch_attn = nrm(ks[8], (DEPTH, D_ATTN, D_MODEL), f32) * D_ATTN ** -0.5
    w_out = nrm(ks[9], (DEPTH, D_MODEL, D_MODEL), f32) * (DEEPNORM_BETA * D_MODEL ** -0.5)
    ln1_g = 1.0 + 0.02 * nrm(ks[10], (DEPTH, D_MODEL), f32)
    ln1_b = 0.02 * nrm(ks[11], (DEPTH, D_MODEL), f32)
    peer_w_query = nrm(ks[12], (DEPTH, D_MODEL, PEER_HEADS * PEER_QUERY_DIM), f32) * D_MODEL ** -0.5
    peer_sub_keys = nrm(ks[13], (DEPTH, PEER_HEADS, 2, PEER_N_KEYS, PEER_HALF), f32) * PEER_HALF ** -0.5
    peer_u = nrm(ks[14], (DEPTH, PEER_N_EXPERTS, D_MODEL), f32) * D_MODEL ** -0.5
    peer_v = nrm(ks[15], (DEPTH, PEER_N_EXPERTS, D_MODEL), f32) * (DEEPNORM_BETA * PEER_HEADS ** -0.5)
    ln2_g = 1.0 + 0.02 * nrm(ks[16], (DEPTH, D_MODEL), f32)
    ln2_b = 0.02 * nrm(ks[17], (DEPTH, D_MODEL), f32)
    return {"x": x, "ln0_g": ln0_g, "ln0_b": ln0_b, "w_in": w_in, "b_gate": b_gate,
            "q_norm_g": q_norm_g, "k_norm_g": k_norm_g,
            "w_branch_fourier": w_branch_fourier, "w_branch_attn": w_branch_attn,
            "w_out": w_out, "ln1_g": ln1_g, "ln1_b": ln1_b,
            "peer_w_query": peer_w_query, "peer_sub_keys": peer_sub_keys,
            "peer_u": peer_u, "peer_v": peer_v, "ln2_g": ln2_g, "ln2_b": ln2_b}

def reference(x, ln0_g, ln0_b, w_in, b_gate, q_norm_g, k_norm_g, w_branch_fourier,
              w_branch_attn, w_out, ln1_g, ln1_b, peer_w_query, peer_sub_keys,
              peer_u, peer_v, ln2_g, ln2_b):
    b, s, _ = x.shape
    x = layer_norm(x, ln0_g, ln0_b)
    cos, sin = axial_rope_tables(s, x.dtype)
    for l in range(DEPTH):
        h = x @ w_in[l]
        xf, q, k, v, g_f, g_a = jnp.split(h, SPLITS, axis=-1)
        y_f = fourier_mix(xf) @ w_branch_fourier[l]
        q = apply_axial_rope(rms_norm(q.reshape(b, s, N_Q_HEADS, HEAD_DIM), q_norm_g[l]), cos, sin)
        k = apply_axial_rope(rms_norm(k.reshape(b, s, N_KV_HEADS, HEAD_DIM), k_norm_g[l]), cos, sin)
        v = v.reshape(b, s, N_KV_HEADS, HEAD_DIM)
        y_a = block_attention(q, k, v) @ w_branch_attn[l]
        mixed = jax.nn.sigmoid(g_f + b_gate[l, 0]) * y_f + jax.nn.sigmoid(g_a + b_gate[l, 1]) * y_a
        x = layer_norm(DEEPNORM_ALPHA * x + mixed @ w_out[l], ln1_g[l], ln1_b[l])
        y_p = peer_ffn(x, peer_w_query[l], peer_sub_keys[l], peer_u[l], peer_v[l])
        x = layer_norm(DEEPNORM_ALPHA * x + y_p, ln2_g[l], ln2_b[l])
    return x


_drawn_inputs = setup_inputs


def setup_inputs(seed=0):
    import zlib

    import numpy as np

    out = dict(_drawn_inputs(seed))
    spreads = {}
    factors = {'b_gate': 8.0, 'q_norm_g': 8.0, 'k_norm_g': 8.0}
    for name, (base, spread) in spreads.items():
        noise = np.random.default_rng([zlib.crc32(name.encode()), seed]).standard_normal(out[name].shape)
        drawn = base * np.exp(spread * noise) if base else spread * noise
        out[name] = __import__('jax').numpy.asarray(drawn.astype(out[name].dtype))
    for name, factor in factors.items():
        out[name] = (out[name] * factor).astype(out[name].dtype)
    return out
```

```python
from contextlib import ExitStack

import concourse.bass as bass
from concourse import mybir

F32 = mybir.dt.float32
F32R = mybir.dt.float32r
U32 = mybir.dt.uint32
ALU = mybir.AluOpType
ACT = mybir.ActivationFunctionType
AX_X = mybir.AxisListType.X

P = 128
S, D, DEPTH = 512, 1024, 2
TB, KD = S // P, D // P
GROUPS = 4
HEADS, KV_HEADS, HD = 8, 2, 64
PAIRS = HEADS // KV_HEADS
NORMED = HEADS + KV_HEADS
QKV = (HEADS + 2 * KV_HEADS) * HD
RH, KEYS, TOPK = 8, 128, 16
ALPHA = (2.0 * DEPTH) ** 0.25
LN_EPS, RMS_EPS = 1e-5, 1e-6
SCALE = float(HD) ** -0.5
LOWEST = -3.0e38

PIECE = 2048
LANDINGS, SPLITS = 4, 2
CG = 4
NG = KEYS // CG
P_XF, P_Q, P_KV, P_COS, P_SIN = 0, 2, 4, 5, 6
P_GF, P_WF, P_GA, P_WA, P_OUT = 7, 11, 13, 17, 19
P_QUERY, P_PAD, P_TAB = 23, 31, 32
NP = P_TAB + 4 * NG

C_IDENT, C_IOTA, C_DFT, C_COS, C_SIN = 0, 128, 256, 512, 768
N_CONST = 1024


class Tally:

    def __init__(self, sem, pre, per):
        self.sem, self.pre, self.per = sem, pre, per

    def at(self, layer, n):
        return self.pre + layer * self.per + n


class Chain:

    def __init__(self, eng, sem, base):
        self.eng, self.sem, self.base, self.n = eng, sem, base, 0

    def mark(self, ins):
        self.n += 1
        ins.then_inc(self.sem, 1)
        return self.n

    def wait(self, n=None):
        self.eng.wait_ge(self.sem, self.base + (self.n if n is None else n))

    def link(self, ins):
        self.mark(ins)
        self.wait()


def build(nc, x, stream, keys, ln0, ln1, ln2, qk_gain, gate_bias, consts, out):
    ctx = ExitStack()
    with ctx:
        def sb(name, shape, dt=F32):
            return ctx.enter_context(nc.sbuf_tensor(name, shape, dt))

        def sem(name):
            return ctx.enter_context(nc.semaphore(name))

        def tally(name, pre, per):
            return Tally(sem(name), pre, per)

        X = sb("X", [P, TB, D])
        XTh = sb("XTh", [P, KD, S], F32R)
        XTl = sb("XTl", [P, KD, S], F32R)
        landing = [sb(f"landing{i}", [P, PIECE]) for i in range(LANDINGS)]
        part_h = [sb(f"part_h{i}", [P, PIECE], F32R) for i in range(SPLITS)]
        part_l = [sb(f"part_l{i}", [P, PIECE], F32R) for i in range(SPLITS)]
        C = sb("C", [P, N_CONST])
        LNP = sb("LNP", [P, 2, D])
        QKG = sb("QKG", [P, 2, HD])
        GB = sb("GB", [P, 2, KD])
        stats = sb("stats", [P, TB, 2, 6])
        mv = sb("mv", [P, TB, 2])
        rs = sb("rs", [P, 4, TB * NORMED])
        att = sb("att", [P, 3, 32])
        attr = sb("attr", [P, 32])
        ident, iota = C[:, C_IDENT:C_IDENT + P], C[:, C_IOTA:C_IOTA + P]
        dft = C[:, C_DFT:C_DFT + 2 * P]
        cos = C[:, C_COS:C_COS + TB * HD].rearrange("p (t d) -> p t d", t=TB)
        sin = C[:, C_SIN:C_SIN + TB * HD].rearrange("p (t d) -> p t d", t=TB)

        base = nc.sbuf_base
        region = sb("region", [P, (nc.sbuf_usable_end - base) // 4 - 8])
        room = 4 * region.shape[1]

        def overlay(name, kib, shape, dt=F32):
            size = 4
            for n in shape[1:]:
                size *= n
            assert kib * 1024 + size <= room, (name, kib * 1024 + size, room)
            return nc.alloc_sbuf_tensor_at(name, shape, dt, offset=base + int(kib * 1024))

        yTh = overlay("yTh", 0, [P, GROUPS, S], F32R)
        yTl = overlay("yTl", 8, [P, GROUPS, S], F32R)
        Ga = overlay("Ga", 0, [P, KD, S])
        oTh = overlay("oTh", 16, [P, PAIRS, S], F32R)
        oTl = overlay("oTl", 24, [P, PAIRS, S], F32R)
        xfT = overlay("xfT", 16, [P, GROUPS, S])
        qkv = overlay("qkv", 32, [P, TB, QKV])
        Ch = overlay("Ch", 44, [P, GROUPS, TB, 2 * P], F32R)
        Cl = overlay("Cl", 60, [P, GROUPS, TB, 2 * P], F32R)
        turn = overlay("turn", 76, [P, 2, NORMED * HD])
        qT = overlay("qT", 44, [P, PAIRS, S])
        kT = overlay("kT", 52, [P, S])
        prob = overlay("prob", 54, [P, 2, S])
        PT = overlay("PT", 58, [P, 2, TB, S])
        Gf = overlay("Gf", 44, [P, KD, S])
        keyT = overlay("keyT", 0, [P, 2 * RH, KEYS])
        qrT = overlay("qrT", 8, [P, 2, 2, S])
        ks = overlay("ks", 16, [P, 2, 2, TB, KEYS])
        kv_ = overlay("kv_", 24, [P, TB, RH, 2, TOPK])
        ki = overlay("ki", 28, [P, TB, RH, 2, TOPK], U32)
        kf = overlay("kf", 32, [P, TB, RH, 2, TOPK])
        cand = overlay("cand", 36, [P, TB, TOPK * TOPK])
        sv = overlay("sv", 40, [P, TB, RH, TOPK])
        pos = overlay("pos", 42, [P, TB, RH, TOPK], U32)
        pab = overlay("pab", 44, [P, 2, TB, RH * TOPK], U32)
        paf = overlay("paf", 48, [P, 2, TB, RH * TOPK])
        pick = overlay("pick", 52, [P, RH, TOPK, TOPK])
        route = overlay("route", 60, [P, TB, 3, RH * TOPK])
        gsum = overlay("gsum", 66, [P, 3, TB * RH])
        routeT = overlay("routeT", 67, [P, TB, 3, P])
        hot1 = overlay("hot1", 0, [P, 2, 4, KEYS])
        hot2 = overlay("hot2", 4, [P, 2, 4, KEYS])
        spill = overlay("spill", 8, [P, 2, NG, 32, CG])
        Yacc = overlay("Yacc", 0, [P, KD, S])
        Wh = overlay("Wh", 16, [P, 2, CG, S], F32R)
        Wl = overlay("Wl", 32, [P, 2, CG, S], F32R)
        gate = [overlay(f"gate{i}", 48 + 8 * i, [P, S, CG]) for i in range(2)]
        acts = overlay("acts", 64, [P, 2, S])
        Wf = overlay("Wf", 68, [P, 2, S])

        bank = [ctx.enter_context(nc.psum_tensor(f"bank{i}", [P, S], F32)) for i in range(8)]
        dense = nc.dram_tensor("dense_gates", [NG, P, S, CG], F32, kind="Internal").ap()

        landed = [sem(f"landed{i}") for i in range(LANDINGS)]
        high_part = sem("high_part")
        split = tally("split", 0, NP)
        used = tally("used", 0, NP)
        x_in = sem("x_in")
        const_in = sem("const_in")
        ln_in = tally("ln_in", 16, 32)
        par_in = tally("par_in", 0, 32)
        key_in = tally("key_in", 0, 16)
        x_normed = tally("x_normed", TB, 2 * TB)
        xt_bank = tally("xt_bank", 2 * TB, 4 * TB)
        xt_high = tally("xt_high", 2 * TB, 4 * TB)
        xt_low = tally("xt_low", 2 * TB, 4 * TB)
        root_in = tally("root_in", 1, 3)
        root_out = tally("root_out", 1, 3)
        xf_copied = tally("xf_copied", 0, GROUPS)
        q_copied = tally("q_copied", 0, TB)
        kv_copied = tally("kv_copied", 0, 2)
        chan_done = tally("chan_done", 0, 8)
        chan_high = tally("chan_high", 0, 8)
        chan_low = tally("chan_low", 0, 8)
        y_high = tally("y_high", 0, GROUPS)
        y_low = tally("y_low", 0, GROUPS)
        roped = tally("roped", 0, TB)
        qk_turned = tally("qk_turned", 0, PAIRS + 1)
        qk_copied = tally("qk_copied", 0, PAIRS + 1)
        scored = tally("scored", 0, 32)
        max_ready = tally("max_ready", 0, 32)
        exped = tally("exped", 0, 32)
        prob_ready = tally("prob_ready", 0, 32)
        p_turned = tally("p_turned", 0, 32)
        p_copied = tally("p_copied", 0, 32)
        pv_done = tally("pv_done", 0, HEADS)
        o_high = tally("o_high", 0, HEADS)
        o_low = tally("o_low", 0, HEADS)
        gatef = tally("gatef", 0, KD)
        gatea = tally("gatea", 0, KD)
        yf_gated = tally("yf_gated", 0, KD)
        ya_gated = tally("ya_gated", 0, KD)
        mixed = tally("mixed", 0, KD)
        mixed_high = tally("mixed_high", 0, KD)
        mixed_low = tally("mixed_low", 0, KD)
        resid = tally("resid", 0, 8)
        qr_copied = tally("qr_copied", 0, RH)
        key_scored = tally("key_scored", 0, RH)
        ks_copied = tally("ks_copied", 0, RH)
        head_cut = tally("head_cut", 0, RH)
        sv_shifted = tally("sv_shifted", 0, 1)
        sv_exped = tally("sv_exped", 0, 1)
        routed = tally("routed", 0, TB)
        route_turned = tally("route_turned", 0, TB)
        route_copied = tally("route_copied", 0, TB)
        hots = tally("hots", 0, S // 4)
        gated = tally("gated", 0, S // 4)
        gate_copied = tally("gate_copied", 0, S // 4)
        spilled = [tally(f"spilled{i}", 0, 16 * S // 64) for i in range(2)]
        gate_in = [tally(f"gate_in{i}", 0, 16 * NG // 2) for i in range(2)]
        u_first = tally("u_first", 0, 2 * NG)
        act_out = tally("act_out", 0, CG * NG)
        w_full = tally("w_full", 0, CG * NG)
        w_high = tally("w_high", 0, CG * NG)
        w_low = tally("w_low", 0, CG * NG)
        v_first = tally("v_first", 0, 2 * NG)
        y_added = tally("y_added", 0, 4 * NG)
        y_turned = tally("y_turned", 0, 2 * TB)
        y_resid = tally("y_resid", 0, 2 * TB)
        out_done = sem("out_done")
        dve_step = sem("dve_step")
        went_on = sem("went_on")

        V_LAST = NP - 2
        block = ctx.enter_context(nc.Block())

        @block.sync
        def _(sp):
            flat = stream.rearrange("l n p w -> (l n) p w")
            sp.dma_start(X[:], x.rearrange("(t p) d -> p t d", p=P)).then_inc(x_in, 16)
            for s in range(LANDINGS):
                sp.dma_start(landing[s][:], flat[s]).then_inc(landed[s], 16)
            with sp.Fori(1, DEPTH * NP // LANDINGS) as r:
                for s in range(LANDINGS):
                    sp.wait_ge(split.sem, r * LANDINGS + (s - LANDINGS + 1))
                    sp.dma_start(landing[s][:], flat[r * LANDINGS + s]).then_inc(landed[s], 16)
            sp.wait_ge(x_normed.sem, x_normed.at(DEPTH, 0))
            sp.dma_start(out.rearrange("(t p) d -> p t d", p=P), X[:]).then_inc(out_done, 16)
            sp.wait_ge(out_done, 16)

        @block.gpsimd
        def _(pool):
            def split_round(r, first):
                for s in range(LANDINGS):
                    k = s % SPLITS
                    pool.wait_ge(landed[s], r * 16 + 16)
                    if not (first and s < SPLITS):
                        pool.wait_ge(used.sem, r * LANDINGS + (s - SPLITS + 1))
                    pool.sem_inc(went_on, 1)
                    nc.gpsimd.tensor_copy(part_h[k][:], landing[s][:]).then_inc(high_part, 1)
                    pool.wait_ge(high_part, r * LANDINGS + (s + 1))
                    nc.gpsimd.tensor_tensor(part_l[k][:], landing[s][:], part_h[k][:].bitcast(F32),
                                            ALU.subtract).then_inc(split.sem, 1)

            split_round(0, True)
            with pool.Fori(1, DEPTH * NP // LANDINGS) as r:
                split_round(r, False)

        @block.scalar
        def _(act):
            def root(l, n, width):
                act.wait_ge(root_in.sem, root_in.at(l, n) if l is not None else n)
                nc.scalar.activation(rs[:, 1, 0:width], rs[:, 0, 0:width], ACT.Sqrt).then_inc(root_out.sem, 1)

            def xt_parts(at):
                for tb in range(TB):
                    for h in range(2):
                        act.wait_ge(xt_bank.sem, at(2 * tb + h + 1))
                        nc.scalar.copy(XTh[:, 4 * h:4 * h + 4, tb * P:(tb + 1) * P],
                                       bank[4 + (2 * tb + h) % 4][:].rearrange("p (k t) -> p k t", k=4)
                                       ).then_inc(xt_high.sem, 1)

            act.dma_start(C[:], consts).then_inc(const_in, 16)
            act.dma_start(LNP[:], ln0.partition_broadcast(P)).then_inc(ln_in.sem, 16)
            root(None, 1, TB)
            xt_parts(lambda n: n)

            with act.Fori(0, DEPTH) as l:
                act.wait_ge(x_normed.sem, x_normed.at(l, 0))
                act.dma_start(LNP[:], ln1[l].partition_broadcast(P)).then_inc(ln_in.sem, 16)
                act.dma_start(QKG[:], qk_gain[l].partition_broadcast(P)).then_inc(par_in.sem, 16)
                act.dma_start(GB[:], gate_bias[l]).then_inc(par_in.sem, 16)
                for c in range(GROUPS):
                    act.wait_ge(used.sem, used.at(l, P_XF + c // 2 + 1))
                    nc.scalar.copy(xfT[:, c, :], bank[c][:]).then_inc(xf_copied.sem, 1)
                for tb in range(TB):
                    act.wait_ge(used.sem, used.at(l, P_Q + 2))
                    nc.scalar.copy(qkv[:, tb, 0:S], bank[4 + tb][:]).then_inc(q_copied.sem, 1)
                for h in range(2):
                    act.wait_ge(used.sem, used.at(l, P_KV + 1))
                    nc.scalar.copy(qkv[:, 2 * h:2 * h + 2, S:QKV],
                                   bank[h][:].rearrange("p (t c) -> p t c", t=2)).then_inc(kv_copied.sem, 1)
                for p in range(8):
                    act.wait_ge(chan_done.sem, chan_done.at(l, p + 1))
                    nc.scalar.copy(Ch[:, p // 2, 2 * (p % 2):2 * (p % 2) + 2, :],
                                   bank[(2 + p) if p < 6 else (p - 4)][:].rearrange("p (t c) -> p t c", t=2)
                                   ).then_inc(chan_high.sem, 1)
                root(l, 1, TB * NORMED)
                for g in range(GROUPS):
                    act.wait_ge(used.sem, used.at(l, P_SIN + 1))
                    nc.scalar.copy(yTh[:, g, :], bank[4 + g][:]).then_inc(y_high.sem, 1)
                for j in range(PAIRS + 1):
                    act.wait_ge(qk_turned.sem, qk_turned.at(l, j + 1))
                    dst = qT[:, j, :] if j < PAIRS else kT[:]
                    nc.scalar.copy(dst, bank[j][:]).then_inc(qk_copied.sem, 1)

                def p_copy(u):
                    h, tb = u // TB, u % TB
                    act.wait_ge(p_turned.sem, p_turned.at(l, u + 1))
                    if h >= 2:
                        act.wait_ge(pv_done.sem, pv_done.at(l, h - 1))
                    nc.scalar.copy(PT[:, h % 2, :, tb * P:(tb + 1) * P],
                                   bank[2 + u % 2][:].rearrange("p (s t) -> p s t", s=TB)).then_inc(p_copied.sem, 1)

                def o_copy(h):
                    g, j = h // PAIRS, h % PAIRS
                    act.wait_ge(pv_done.sem, pv_done.at(l, h + 1))
                    nc.scalar.copy(oTh[g * HD:(g + 1) * HD, j, :],
                                   bank[4 + h % 2][g * HD:(g + 1) * HD, :]).then_inc(o_high.sem, 1)

                for u in range(32):
                    act.wait_ge(max_ready.sem, max_ready.at(l, u + 1))
                    if u >= 2:
                        act.wait_ge(p_turned.sem, p_turned.at(l, u - 1))
                    nc.scalar.activation(prob[:, u % 2, :], bank[u % 2][:], ACT.Exp, bias=att[:, 1, u:u + 1],
                                         scale=SCALE, accum_out=att[:, 2, u:u + 1]).then_inc(exped.sem, 1)
                    if u >= 1:
                        p_copy(u - 1)
                    if u % TB == 2 and u > TB:
                        o_copy(u // TB - 1)
                p_copy(31)
                o_copy(HEADS - 1)
                act.wait_ge(par_in.sem, par_in.at(l, 32))
                for m in range(KD):
                    act.wait_ge(used.sem, used.at(l, P_GF + m // 2 + 1))
                    nc.scalar.activation(Gf[:, m, :], bank[m % 4][:], ACT.Sigmoid,
                                         bias=GB[:, 0, m:m + 1]).then_inc(gatef.sem, 1)
                for m in range(KD):
                    act.wait_ge(used.sem, used.at(l, P_GA + m // 2 + 1))
                    nc.scalar.activation(Ga[:, m, :], bank[m % 4][:], ACT.Sigmoid,
                                         bias=GB[:, 1, m:m + 1]).then_inc(gatea.sem, 1)
                for m in range(KD):
                    act.wait_ge(mixed.sem, mixed.at(l, m + 1))
                    nc.scalar.copy(XTh[:, m, :], Gf[:, m, :]).then_inc(mixed_high.sem, 1)
                root(l, 2, TB)
                xt_parts(lambda n: xt_bank.at(l, n))

                act.wait_ge(x_normed.sem, x_normed.at(l, TB))
                act.dma_start(LNP[:], ln2[l].partition_broadcast(P)).then_inc(ln_in.sem, 16)
                act.dma_start(keyT[:], keys[l]).then_inc(key_in.sem, 16)

                def ks_copy(h):
                    act.wait_ge(key_scored.sem, key_scored.at(l, h + 1))
                    if h >= 2:
                        act.wait_ge(head_cut.sem, head_cut.at(l, h - 1))
                    for f in range(2):
                        ins = nc.scalar.copy(ks[:, h % 2, f, :, :].rearrange("p t k -> p (t k)"),
                                             bank[4 + 2 * (h % 2) + f][:])
                    ins.then_inc(ks_copied.sem, 1)

                for h in range(RH):
                    act.wait_ge(used.sem, used.at(l, P_QUERY + h + 1))
                    if h >= 2:
                        act.wait_ge(key_scored.sem, key_scored.at(l, h - 1))
                    for f in range(2):
                        ins = nc.scalar.copy(qrT[:, h % 2, f, :], bank[2 * (h % 2) + f][:])
                    ins.then_inc(qr_copied.sem, 1)
                    if h >= 1:
                        ks_copy(h - 1)
                ks_copy(RH - 1)
                act.wait_ge(sv_shifted.sem, sv_shifted.at(l, 1))
                nc.scalar.activation(route[:, :, 2, :], sv[:].rearrange("p t h k -> p t (h k)"),
                                     ACT.Exp).then_inc(sv_exped.sem, 1)
                for tb in range(TB):
                    act.wait_ge(route_turned.sem, route_turned.at(l, tb + 1))
                    nc.scalar.copy(routeT[:, tb, :, :].rearrange("p a t -> p (a t)"),
                                   bank[tb][:, 0:3 * P]).then_inc(route_copied.sem, 1)

                def gate_block(b, first):
                    for k in range(2):
                        if not first:
                            act.wait_ge(spilled[k].sem, spilled[k].at(l, 16 * b))
                        for q in range(8):
                            act.wait_ge(gated.sem, gated.at(l, 16 * b + (8 * k + q + 1)))
                            dst = spill[:, k, :, 4 * q:4 * q + 4, :].rearrange("p g t j -> p t g j")
                            nc.scalar.copy(dst, bank[q % 4][:].rearrange("p (t g j) -> p t g j", t=4, j=CG)
                                           ).then_inc(gate_copied.sem, 1)
                        act.wait_ge(gate_copied.sem, gate_copied.at(l, 16 * b + 8 * (k + 1)))
                        dd = dense.rearrange("g p (b t) j -> b p g (t j)", t=32)
                        act.dma_start(dd[2 * b + k], spill[:, k, :, :, :].rearrange("p g t j -> p g (t j)")
                                      ).then_inc(spilled[k].sem, 16)

                gate_block(0, True)
                with act.Fori(1, S // 64) as b:
                    gate_block(b, False)
                for k in range(2):
                    act.wait_ge(spilled[k].sem, spilled[k].at(l, 16 * (S // 64)))
                for k in range(2):
                    act.dma_start(gate[k][:], dense[k]).then_inc(gate_in[k].sem, 16)

                def activate(g, s, par, half, early):
                    for c in (2 * half, 2 * half + 1):
                        if c % 2 == 0:
                            act.wait_ge(u_first.sem, u_first.at(l, 2 * g + (half + 1)))
                        else:
                            act.wait_ge(used.sem, used.at(l, early if early is not None
                                                          else 4 * g + (P_TAB - 1 + 2 * half)))
                        if not (early is not None and c < 2):
                            act.wait_ge(w_full.sem, w_full.at(l, CG * g + (c - 1)))
                        nc.scalar.activation(acts[:, c % 2, :], bank[c][:], ACT.Gelu).then_inc(act_out.sem, 1)
                    for c in (2 * half, 2 * half + 1):
                        act.wait_ge(w_full.sem, w_full.at(l, CG * g + (c + 1)))
                        nc.scalar.copy(Wh[:, par, c, :], Wf[:, c % 2, :]).then_inc(w_high.sem, 1)

                activate(0, 0, 0, 0, P_TAB + 1)
                activate(0, 0, 0, 1, P_TAB + 2)
                act.wait_ge(w_full.sem, w_full.at(l, CG))
                act.dma_start(gate[0][:], dense[2]).then_inc(gate_in[0].sem, 16)

                def act_group(g, par, fetch, wait_slot):
                    if wait_slot:
                        act.wait_ge(used.sem, used.at(l, 4 * g + (P_TAB - 2)))
                    activate(g, g, par, 0, None)
                    activate(g, g, par, 1, None)
                    if fetch:
                        act.dma_start(gate[par][:], dense[g + 2]).then_inc(gate_in[par].sem, 16)

                act_group(1, 1, True, False)
                with act.Fori(1, NG // 2 - 1) as m:
                    act_group(2 * m, 0, True, True)
                    act_group(2 * m + 1, 1, True, True)
                act_group(NG - 2, 0, False, True)
                act_group(NG - 1, 1, False, True)
                root(l, 3, TB)
                xt_parts(lambda n: xt_bank.at(l, 2 * TB + n))

        @block.vector
        def _(dve):
            def inv_root(ch, src_ready, n_out, width):
                v, r0 = rs[:, 2, 0:width], rs[:, 1, 0:width]
                a, r = rs[:, 0, 0:width], rs[:, 3, 0:width]
                nc.vector.reciprocal(a, v).then_inc(root_in.sem, 1)
                dve.wait_ge(root_out.sem, n_out)
                ch.link(nc.vector.tensor_tensor(a, r0, r0, ALU.mult))
                ch.link(nc.vector.tensor_tensor(a, a, v, ALU.mult))
                ch.link(nc.vector.tensor_scalar(a, a, -0.5, 1.5, ALU.mult, ALU.add))
                ch.link(nc.vector.tensor_tensor(r, r0, a, ALU.mult))

            def layer_norm(ch, n_root, n_par, xt):
                for tb in range(TB):
                    for h in range(2):
                        ch.mark(nc.vector.bn_stats(stats[:, tb, h, :], X[:, tb, h * S:(h + 1) * S]))
                n = ch.n
                for tb in range(TB):
                    ch.wait(n - 2 * (TB - 1 - tb))
                    ch.mark(nc.vector.bn_aggr(mv[:, tb, :], stats[:, tb, :, :].rearrange("p a b -> p (a b)")))
                ch.wait()
                ch.link(nc.vector.tensor_scalar(rs[:, 2, 0:TB], mv[:, :, 1], LN_EPS, None, ALU.add))
                inv_root(ch, None, n_root, TB)
                dve.wait_ge(ln_in.sem, n_par)
                for tb in range(TB):
                    xb = X[:, tb, :]
                    ch.link(nc.vector.tensor_scalar(xb, xb, mv[:, tb, 0:1], rs[:, 3, tb:tb + 1],
                                                    ALU.subtract, ALU.mult))
                    ch.link(nc.vector.tensor_tensor(xb, xb, LNP[:, 0, :], ALU.mult))
                    nc.vector.tensor_tensor(xb, xb, LNP[:, 1, :], ALU.add).then_inc(x_normed.sem, 1)
                    if tb >= 1:
                        low_parts(tb - 1, xt)
                low_parts(TB - 1, xt)

            def low_parts(tb, xt):
                for h in range(2):
                    dve.wait_ge(xt_high.sem, xt(2 * tb + h + 1))
                    part = XTh[:, 4 * h:4 * h + 4, tb * P:(tb + 1) * P].bitcast(F32)
                    nc.vector.tensor_tensor(XTl[:, 4 * h:4 * h + 4, tb * P:(tb + 1) * P],
                                            bank[4 + (2 * tb + h) % 4][:].rearrange("p (k t) -> p k t", k=4),
                                            part, ALU.subtract).then_inc(xt_low.sem, 1)

            pre = Chain(dve, dve_step, 0)
            dve.wait_ge(x_in, 16)
            layer_norm(pre, 1, 16, lambda n: n)

            with dve.Fori(0, DEPTH) as l:
                dve.sem_clear(dve_step)
                ch = Chain(dve, dve_step, 0)
                for tb in range(TB):
                    dve.wait_ge(q_copied.sem, q_copied.at(l, tb + 1))
                    dve.wait_ge(kv_copied.sem, kv_copied.at(l, tb // 2 + 1))
                    qk = qkv[:, tb, 0:NORMED * HD]
                    ch.link(nc.vector.tensor_tensor(turn[:, 0, :], qk, qk, ALU.mult))
                    ch.link(nc.vector.tensor_reduce(rs[:, 2, tb * NORMED:(tb + 1) * NORMED],
                                                    turn[:, 0, :].rearrange("p (h d) -> p h d", d=HD), AX_X, ALU.add))
                ch.link(nc.vector.tensor_scalar(rs[:, 2, :], rs[:, 2, :], 1.0 / HD, RMS_EPS, ALU.mult, ALU.add))
                for p in range(8):
                    dve.wait_ge(chan_high.sem, chan_high.at(l, p + 1))
                    sl = (slice(None), p // 2, slice(2 * (p % 2), 2 * (p % 2) + 2))
                    nc.vector.tensor_tensor(Cl[sl], bank[(2 + p) if p < 6 else (p - 4)][:].rearrange(
                        "p (t c) -> p t c", t=2), Ch[sl].bitcast(F32), ALU.subtract).then_inc(chan_low.sem, 1)
                inv_root(ch, None, root_out.at(l, 1), TB * NORMED)
                dve.wait_ge(par_in.sem, par_in.at(l, 32))
                for tb in range(TB):
                    qk = qkv[:, tb, 0:NORMED * HD].rearrange("p (h d) -> p h d", d=HD)
                    r = rs[:, 3, tb * NORMED:(tb + 1) * NORMED].unsqueeze(2).broadcast_to([P, NORMED, HD])
                    ch.link(nc.vector.tensor_tensor(qk, qk, r, ALU.mult))
                    for a, b, w in ((0, HEADS, 0), (HEADS, NORMED, 1)):
                        ch.mark(nc.vector.tensor_tensor(qk[:, a:b, :], qk[:, a:b, :],
                                                        QKG[:, w, :].unsqueeze(1).broadcast_to([P, b - a, HD]), ALU.mult))
                    ch.wait()
                    t0 = turn[:, 0, :].rearrange("p (h d) -> p h d", d=HD)
                    t1 = turn[:, 1, :].rearrange("p (h r c d) -> p h r c d", h=NORMED, r=2, c=2)
                    q5 = qkv[:, tb, 0:NORMED * HD].rearrange("p (h r c d) -> p h r c d", h=NORMED, r=2, c=2)
                    s5 = sin[:, tb, :].rearrange("p (r c d) -> p r c d", r=2, c=2)
                    ch.mark(nc.vector.tensor_tensor(t0, qk, cos[:, tb, :].unsqueeze(1).broadcast_to([P, NORMED, HD]),
                                                    ALU.mult))
                    for c in range(2):
                        ch.mark(nc.vector.tensor_tensor(
                            t1[:, :, :, c, :], q5[:, :, :, 1 - c, :],
                            s5[:, :, c, :].unsqueeze(1).broadcast_to([P, NORMED, 2, HD // 4]), ALU.mult))
                    ch.wait()
                    nc.vector.tensor_tensor(qkv[:, tb, 0:NORMED * HD], turn[:, 0, :], turn[:, 1, :],
                                            ALU.add).then_inc(roped.sem, 1)
                    dve.wait_ge(roped.sem, roped.at(l, tb + 1))
                for g in range(GROUPS):
                    dve.wait_ge(y_high.sem, y_high.at(l, g + 1))
                    nc.vector.tensor_tensor(yTl[:, g, :], bank[4 + g][:], yTh[:, g, :].bitcast(F32),
                                            ALU.subtract).then_inc(y_low.sem, 1)

                def row_max(u):
                    dve.wait_ge(scored.sem, scored.at(l, u + 1))
                    ch.link(nc.vector.tensor_reduce(att[:, 0, u:u + 1], bank[u % 2][:], AX_X, ALU.max))
                    nc.vector.tensor_scalar(att[:, 1, u:u + 1], att[:, 0, u:u + 1], -SCALE, None,
                                            ALU.mult).then_inc(max_ready.sem, 1)

                def o_rest(h):
                    g, j = h // PAIRS, h % PAIRS
                    rows = slice(g * HD, (g + 1) * HD)
                    dve.wait_ge(o_high.sem, o_high.at(l, h + 1))
                    nc.vector.tensor_tensor(oTl[rows, j, :], bank[4 + h % 2][rows, :], oTh[rows, j, :].bitcast(F32),
                                            ALU.subtract).then_inc(o_low.sem, 1)

                row_max(0)
                for u in range(32):
                    if u + 1 < 32:
                        row_max(u + 1)
                    dve.wait_ge(exped.sem, exped.at(l, u + 1))
                    ch.link(nc.vector.reciprocal(attr[:, u:u + 1], att[:, 2, u:u + 1]))
                    nc.vector.tensor_scalar(prob[:, u % 2, :], prob[:, u % 2, :], attr[:, u:u + 1], None,
                                            ALU.mult).then_inc(prob_ready.sem, 1)
                    if u % TB == 3 and u > TB:
                        o_rest(u // TB - 1)
                o_rest(HEADS - 1)

                for m in range(KD):
                    dve.wait_ge(gatef.sem, gatef.at(l, m + 1))
                    dve.wait_ge(used.sem, used.at(l, P_WF + m // 4 + 1))
                    nc.vector.tensor_tensor(Gf[:, m, :], Gf[:, m, :], bank[4 + m % 4][:],
                                            ALU.mult).then_inc(yf_gated.sem, 1)
                for m in range(KD):
                    dve.wait_ge(gatea.sem, gatea.at(l, m + 1))
                    dve.wait_ge(used.sem, used.at(l, P_WA + m // 4 + 1))
                    nc.vector.tensor_tensor(Ga[:, m, :], Ga[:, m, :], bank[4 + m % 4][:],
                                            ALU.mult).then_inc(ya_gated.sem, 1)
                    dve.wait_ge(ya_gated.sem, ya_gated.at(l, m + 1))
                    nc.vector.tensor_tensor(Gf[:, m, :], Gf[:, m, :], Ga[:, m, :], ALU.add).then_inc(mixed.sem, 1)
                    if m >= 1:
                        dve.wait_ge(mixed_high.sem, mixed_high.at(l, m))
                        nc.vector.tensor_tensor(XTl[:, m - 1, :], Gf[:, m - 1, :], XTh[:, m - 1, :].bitcast(F32),
                                                ALU.subtract).then_inc(mixed_low.sem, 1)
                dve.wait_ge(mixed_high.sem, mixed_high.at(l, KD))
                nc.vector.tensor_tensor(XTl[:, KD - 1, :], Gf[:, KD - 1, :], XTh[:, KD - 1, :].bitcast(F32),
                                        ALU.subtract).then_inc(mixed_low.sem, 1)
                for q in range(4):
                    dve.wait_ge(used.sem, used.at(l, P_OUT + q + 1))
                    for b in range(2):
                        xs = X[:, 2 * b:2 * b + 2, q * 256:(q + 1) * 256]
                        nc.vector.scalar_tensor_tensor(
                            out=xs, in0=xs, scalar=ALPHA,
                            in1=bank[2 * (q % 2) + b][:].rearrange("p (t c) -> p t c", t=2),
                            op0=ALU.mult, op1=ALU.add).then_inc(resid.sem, 1)
                dve.wait_ge(resid.sem, resid.at(l, 8))
                layer_norm(ch, root_out.at(l, 2), ln_in.at(l, 16), lambda n: xt_high.at(l, n))

                def best(width, scores, vals, idx):
                    n0 = ch.n
                    for half in (0, 8):
                        for tb in range(TB):
                            ch.wait(ch.n - (TB - 1) if ch.n - n0 >= TB else n0)
                            ch.mark(nc.vector.max(vals(tb)[:, half:half + 8], scores(tb)))
                        for tb in range(TB):
                            ch.wait(ch.n - (TB - 1))
                            ch.mark(nc.vector.max_index(idx(tb)[:, half:half + 8], vals(tb)[:, half:half + 8],
                                                        scores(tb)))
                        if half == 0:
                            for tb in range(TB):
                                ch.wait(ch.n - (TB - 1))
                                ch.mark(nc.vector.match_replace(scores(tb), vals(tb)[:, 0:8], scores(tb), LOWEST))

                for h in range(RH):
                    dve.wait_ge(ks_copied.sem, ks_copied.at(l, h + 1))
                    dve.sem_inc(went_on, 1)
                    for f in range(2):
                        best(KEYS, lambda tb: ks[:, h % 2, f, tb, :], lambda tb: kv_[:, tb, h, f, :],
                             lambda tb: ki[:, tb, h, f, :])
                    ch.wait()
                    a = kv_[:, :, h, 0, :].unsqueeze(3).broadcast_to([P, TB, TOPK, TOPK])
                    b = kv_[:, :, h, 1, :].unsqueeze(2).broadcast_to([P, TB, TOPK, TOPK])
                    nc.vector.tensor_tensor(cand[:].rearrange("p t (a b) -> p t a b", a=TOPK), a, b,
                                            ALU.add).then_inc(head_cut.sem, 1)
                    dve.wait_ge(head_cut.sem, head_cut.at(l, h + 1))
                    dve.sem_inc(went_on, 1)
                    best(TOPK * TOPK, lambda tb: cand[:, tb, :], lambda tb: sv[:, tb, h, :],
                         lambda tb: pos[:, tb, h, :])
                ch.wait()
                s3 = sv[:].rearrange("p t h k -> p (t h) k")
                ch.link(nc.vector.tensor_copy(gsum[:, 0, :].unsqueeze(2), s3[:, :, 0:1]))
                nc.vector.tensor_tensor(s3, s3, gsum[:, 0, :].unsqueeze(2).broadcast_to([P, TB * RH, TOPK]),
                                        ALU.subtract).then_inc(sv_shifted.sem, 1)
                p2 = pos[:].rearrange("p t h k -> p t (h k)")
                ch.mark(nc.vector.tensor_scalar(pab[:, 0, :, :], p2, 4, None, ALU.logical_shift_right))
                ch.mark(nc.vector.tensor_scalar(pab[:, 1, :, :], p2, TOPK - 1, None, ALU.bitwise_and))
                ch.mark(nc.vector.tensor_copy(kf[:].rearrange("p t h f k -> p (t h f k)"),
                                              ki[:].rearrange("p t h f k -> p (t h f k)")))
                ch.wait()
                ch.link(nc.vector.tensor_copy(paf[:].rearrange("p f t k -> p (f t k)"),
                                              pab[:].rearrange("p f t k -> p (f t k)")))
                dve.wait_ge(sv_exped.sem, sv_exped.at(l, 1))
                for tb in range(TB):
                    e = route[:, tb, 2, :].rearrange("p (h k) -> p h k", h=RH)
                    sm, rc = gsum[:, 1, tb * RH:(tb + 1) * RH], gsum[:, 2, tb * RH:(tb + 1) * RH]
                    ch.link(nc.vector.tensor_reduce(sm, e, AX_X, ALU.add))
                    ch.link(nc.vector.reciprocal(rc, sm))
                    ch.mark(nc.vector.tensor_tensor(e, e, rc.unsqueeze(2).broadcast_to([P, RH, TOPK]), ALU.mult))
                    for f in range(2):
                        eq = pick[:].rearrange("p h k a -> p (h k) a")
                        ch.link(nc.vector.tensor_tensor(
                            eq, paf[:, f, tb, :].unsqueeze(2).broadcast_to([P, RH * TOPK, TOPK]),
                            iota[:, 0:TOPK].unsqueeze(1).broadcast_to([P, RH * TOPK, TOPK]), ALU.is_equal))
                        ch.link(nc.vector.tensor_tensor(
                            pick[:], pick[:], kf[:, tb, :, f, :].unsqueeze(2).broadcast_to([P, RH, TOPK, TOPK]),
                            ALU.mult))
                        ins = nc.vector.tensor_reduce(route[:, tb, f, :], eq, AX_X, ALU.add)
                        if f == 0:
                            ch.link(ins)
                        else:
                            ins.then_inc(routed.sem, 1)
                            dve.wait_ge(routed.sem, routed.at(l, tb + 1))

                def hot_rows(b, first, tb):
                    for q in range(16):
                        slot = q % 2
                        if not (first and q < 2):
                            dve.wait_ge(gated.sem, gated.at(l, 16 * b + (q - 1)))
                        for t in range(4):
                            n = 4 * q + t
                            col = lambda a: routeT[:, tb, a, bass.ds(64 * (b - 2 * tb) + n, 1)]
                            nc.vector.tensor_scalar(hot1[:, slot, t, :], iota, col(0), None, ALU.is_equal)
                            ins = nc.vector.tensor_scalar(hot2[:, slot, t, :], iota, col(1), col(2),
                                                          ALU.is_equal, ALU.mult)
                        ins.then_inc(hots.sem, 1)

                for b in range(2):
                    dve.wait_ge(route_copied.sem, route_copied.at(l, 1))
                    hot_rows(b, b == 0, 0)
                for tb in range(1, TB):
                    dve.wait_ge(route_copied.sem, route_copied.at(l, tb + 1))
                    dve.sem_inc(went_on, 1)
                    with dve.Fori(2 * tb, 2 * tb + 2) as b:
                        hot_rows(b, False, tb)

                dve.wait_ge(spilled[0].sem, spilled[0].at(l, 16 * (S // 64)))
                dve.wait_ge(spilled[1].sem, spilled[1].at(l, 16 * (S // 64)))
                dve.wait_ge(gated.sem, gated.at(l, S // 4))
                ch.link(nc.vector.memset(Yacc[:].rearrange("p k t -> p (k t)"), 0.0))

                def weigh(g, par, half, early):
                    for c in (2 * half, 2 * half + 1):
                        dve.wait_ge(act_out.sem, act_out.at(l, CG * g + (c + 1)))
                        if not (early and c < 2):
                            dve.wait_ge(w_high.sem, w_high.at(l, CG * g + (c - 1)))
                            dve.wait_ge(w_low.sem, w_low.at(l, CG * g + (c - 1)))
                        nc.vector.tensor_tensor(Wf[:, c % 2, :], acts[:, c % 2, :], gate[par][:, :, c],
                                                ALU.mult).then_inc(w_full.sem, 1)
                    for c in (2 * half, 2 * half + 1):
                        dve.wait_ge(w_high.sem, w_high.at(l, CG * g + (c + 1)))
                        nc.vector.tensor_tensor(Wl[:, par, c, :], Wf[:, c % 2, :], Wh[:, par, c, :].bitcast(F32),
                                                ALU.subtract).then_inc(w_low.sem, 1)

                def add_up(g, half, last):
                    for s in range(2):
                        if s == 0:
                            dve.wait_ge(v_first.sem, v_first.at(l, 2 * g + (half + 1)))
                        else:
                            dve.wait_ge(used.sem, used.at(l, (V_LAST + half + 1) if last
                                                          else 4 * g + (P_TAB + 4 + 2 * half)))
                        for j in range(2):
                            k = 4 * half + 2 * s + j
                            ins = nc.vector.tensor_tensor(Yacc[:, k, :], Yacc[:, k, :], bank[4 + 2 * s + j][:],
                                                          ALU.add)
                        ins.then_inc(y_added.sem, 1)

                def dve_group(g, par, wait_prev):
                    dve.wait_ge(gate_in[par].sem, gate_in[par].at(l, 8 * g + 16 - 8 * par))
                    if wait_prev:
                        dve.wait_ge(used.sem, used.at(l, 4 * g + (P_TAB - 2)))
                    weigh(g, par, 0, False)
                    if wait_prev:
                        dve.wait_ge(y_added.sem, y_added.at(l, 4 * g - 4))
                    add_up(g - 1, 0, False)
                    weigh(g, par, 1, False)
                    add_up(g - 1, 1, False)

                dve.wait_ge(gate_in[0].sem, gate_in[0].at(l, 16))
                weigh(0, 0, 0, True)
                weigh(0, 0, 1, False)
                dve_group(1, 1, False)
                with dve.Fori(1, NG // 2) as m:
                    dve_group(2 * m, 0, True)
                    dve_group(2 * m + 1, 1, True)
                dve.wait_ge(y_added.sem, y_added.at(l, 4 * NG - 4))
                add_up(NG - 1, 0, True)
                add_up(NG - 1, 1, True)
                for tb in range(TB):
                    for h in range(2):
                        dve.wait_ge(y_turned.sem, y_turned.at(l, 2 * tb + h + 1))
                        xs = X[:, tb, h * S:(h + 1) * S]
                        nc.vector.scalar_tensor_tensor(out=xs, in0=xs, scalar=ALPHA, in1=bank[(2 * tb + h) % 4][:],
                                                       op0=ALU.mult, op1=ALU.add).then_inc(y_resid.sem, 1)
                dve.wait_ge(y_resid.sem, y_resid.at(l, 2 * TB))
                layer_norm(ch, root_out.at(l, 3), ln_in.at(l, 32), lambda n: xt_high.at(l, 2 * TB + n))

        @block.tensor
        def _(pe):
            def product(dst, sth, stl, mvh, mvl, first, last):
                nc.tensor.matmul(dst, sth, mvh, start=first, stop=False)
                nc.tensor.matmul(dst, sth, mvl, start=False, stop=False)
                return nc.tensor.matmul(dst, stl, mvh, start=False, stop=last)

            def turn_x(normed, at, low):
                for tb in range(TB):
                    pe.wait_ge(x_normed.sem, normed(tb + 1))
                    for h in range(2):
                        i = 2 * tb + h
                        if i >= 4:
                            pe.wait_ge(xt_low.sem, low(i - 3))
                        for k in range(4):
                            c = 4 * h + k
                            ins = nc.tensor.transpose(bank[4 + i % 4][:, k * P:(k + 1) * P],
                                                      X[:, tb, c * P:(c + 1) * P], ident)
                        ins.then_inc(xt_bank.sem, 1)

            pe.wait_ge(const_in, 16)
            turn_x(lambda n: n, lambda n: n, lambda n: n)

            with pe.Fori(0, DEPTH) as l:
                def piece(n, slot):
                    pe.wait_ge(split.sem, split.at(l, n + 1))
                    return part_h[slot], part_l[slot]

                def columns(n, banks, kc, movh, movl):
                    ph, pl = piece(n, n % 2)
                    for c, b in enumerate(banks):
                        for k in range(kc):
                            w = slice((c * kc + k) * P, (c * kc + k + 1) * P)
                            ins = product(b[:], ph[:, w], pl[:, w], movh[:, k, :], movl[:, k, :],
                                          k == 0, k == kc - 1)
                    ins.then_inc(used.sem, 1)

                pe.wait_ge(xt_low.sem, xt_low.at(l, 0))
                for n in range(2):
                    columns(P_XF + n, [bank[2 * n], bank[2 * n + 1]], KD, XTh, XTl)
                for n in range(2):
                    ph, pl = piece(P_Q + n, (P_Q + n) % 2)
                    for tb in range(TB):
                        for k in range(4):
                            kk, ts, w = 4 * n + k, slice(tb * P, (tb + 1) * P), slice(k * S, (k + 1) * S)
                            ins = product(bank[4 + tb][:], XTh[:, kk, ts], XTl[:, kk, ts], ph[:, w], pl[:, w],
                                          kk == 0, kk == KD - 1)
                    ins.then_inc(used.sem, 1)
                pe.wait_ge(xf_copied.sem, xf_copied.at(l, 2))
                ph, pl = piece(P_KV, P_KV % 2)
                for tb in range(TB):
                    for k in range(KD):
                        ts, w = slice(tb * P, (tb + 1) * P), slice(k * 256, (k + 1) * 256)
                        ins = product(bank[tb // 2][:, (tb % 2) * 256:(tb % 2 + 1) * 256], XTh[:, k, ts], XTl[:, k, ts],
                                      ph[:, w], pl[:, w], k == 0, k == KD - 1)
                ins.then_inc(used.sem, 1)
                for p in range(8):
                    if p == 0:
                        pe.wait_ge(xf_copied.sem, xf_copied.at(l, GROUPS))
                    elif 2 <= p < 6:
                        pe.wait_ge(q_copied.sem, q_copied.at(l, p - 1))
                    elif p >= 6:
                        pe.wait_ge(chan_low.sem, chan_low.at(l, p - 5))
                    for h in range(2):
                        g, tb = p // 2, 2 * (p % 2) + h
                        ins = nc.tensor.matmul(bank[(2 + p) if p < 6 else (p - 4)][:, h * 256:(h + 1) * 256],
                                               xfT[:, g, tb * P:(tb + 1) * P], dft, start=True, stop=True)
                    ins.then_inc(chan_done.sem, 1)
                for n in range(2):
                    ph, pl = piece(P_COS + n, (P_COS + n) % 2)
                    pe.wait_ge(chan_low.sem, chan_low.at(l, 8))
                    for g in range(GROUPS):
                        for s in range(TB):
                            w, cc = slice(s * S, (s + 1) * S), slice(n * P, (n + 1) * P)
                            ins = product(bank[4 + g][:], Ch[:, g, s, cc], Cl[:, g, s, cc], ph[:, w], pl[:, w],
                                          n == 0 and s == 0, n == 1 and s == TB - 1)
                    ins.then_inc(used.sem, 1)
                for tb in range(TB):
                    pe.wait_ge(roped.sem, roped.at(l, tb + 1))
                    if tb == 0:
                        pe.wait_ge(y_low.sem, y_low.at(l, 1))
                    for j in range(PAIRS + 1):
                        ins = nc.tensor.transpose(bank[j][:, tb * P:(tb + 1) * P], qkv[:, tb, j * P:(j + 1) * P], ident)
                        if tb == TB - 1:
                            ins.then_inc(qk_turned.sem, 1)

                def scores(u):
                    h, tb = u // TB, u % TB
                    g, j = h // PAIRS, h % PAIRS
                    if u >= 2:
                        pe.wait_ge(exped.sem, exped.at(l, u - 1))
                    rows = slice(g * HD, (g + 1) * HD)
                    nc.tensor.matmul(bank[u % 2][:], qT[rows, j, tb * P:(tb + 1) * P], kT[rows, :],
                                     start=True, stop=True).then_inc(scored.sem, 1)

                def turn_probs(u):
                    pe.wait_ge(prob_ready.sem, prob_ready.at(l, u + 1))
                    if u >= 2:
                        pe.wait_ge(p_copied.sem, p_copied.at(l, u - 1))
                    for s in range(TB):
                        ins = nc.tensor.transpose(bank[2 + u % 2][:, s * P:(s + 1) * P],
                                                  prob[:, u % 2, s * P:(s + 1) * P], ident)
                    ins.then_inc(p_turned.sem, 1)

                def values(h):
                    pe.wait_ge(p_copied.sem, p_copied.at(l, TB * (h + 1)))
                    if h >= 2:
                        pe.wait_ge(o_low.sem, o_low.at(l, h - 1))
                    for s in range(TB):
                        ins = nc.tensor.matmul(bank[4 + h % 2][:], qkv[:, s, NORMED * HD:QKV], PT[:, h % 2, s, :],
                                               start=(s == 0), stop=(s == TB - 1))
                    ins.then_inc(pv_done.sem, 1)

                pe.wait_ge(qk_copied.sem, qk_copied.at(l, PAIRS + 1))
                pe.wait_ge(y_low.sem, y_low.at(l, GROUPS))
                scores(0)
                for u in range(32):
                    if u + 1 < 32:
                        scores(u + 1)
                    turn_probs(u)
                    if u % TB == 1 and u > TB:
                        values(u // TB - 1)
                values(HEADS - 1)

                pe.wait_ge(p_copied.sem, p_copied.at(l, 32))
                for n in range(4):
                    if n >= 2:
                        pe.wait_ge(gatef.sem, gatef.at(l, 2 * n - 2))
                    columns(P_GF + n, [bank[2 * (n % 2)], bank[2 * (n % 2) + 1]], KD, XTh, XTl)
                pe.wait_ge(o_low.sem, o_low.at(l, HEADS))
                for n in range(2):
                    if n == 1:
                        pe.wait_ge(yf_gated.sem, yf_gated.at(l, 4))
                    columns(P_WF + n, bank[4:8], GROUPS, yTh, yTl)
                for n in range(4):
                    pe.wait_ge(gatef.sem, gatef.at(l, KD)) if n < 2 else pe.wait_ge(gatea.sem, gatea.at(l, 2 * n - 2))
                    columns(P_GA + n, [bank[2 * (n % 2)], bank[2 * (n % 2) + 1]], KD, XTh, XTl)
                for n in range(2):
                    pe.wait_ge(yf_gated.sem, yf_gated.at(l, KD)) if n == 0 else pe.wait_ge(ya_gated.sem, ya_gated.at(l, 4))
                    columns(P_WA + n, bank[4:8], PAIRS, oTh, oTl)
                pe.wait_ge(mixed_low.sem, mixed_low.at(l, KD))
                for n in range(4):
                    if n >= 2:
                        pe.wait_ge(resid.sem, resid.at(l, 2 * n - 2))
                    ph, pl = piece(P_OUT + n, (P_OUT + n) % 2)
                    for tb in range(TB):
                        for k in range(KD):
                            ts, w = slice(tb * P, (tb + 1) * P), slice(k * 256, (k + 1) * 256)
                            ins = product(bank[2 * (n % 2) + tb // 2][:, (tb % 2) * 256:(tb % 2 + 1) * 256],
                                          XTh[:, k, ts], XTl[:, k, ts], ph[:, w], pl[:, w], k == 0, k == KD - 1)
                    ins.then_inc(used.sem, 1)
                turn_x(lambda n: x_normed.at(l, n), None, lambda n: xt_low.at(l, n))

                pe.wait_ge(xt_low.sem, xt_low.at(l, 2 * TB))
                pe.wait_ge(key_in.sem, key_in.at(l, 16))

                def key_scores(h):
                    pe.wait_ge(qr_copied.sem, qr_copied.at(l, h + 1))
                    if h >= 2:
                        pe.wait_ge(ks_copied.sem, ks_copied.at(l, h - 1))
                    for f in range(2):
                        for tb in range(TB):
                            ins = nc.tensor.matmul(bank[4 + 2 * (h % 2) + f][:, tb * P:(tb + 1) * P],
                                                   qrT[:, h % 2, f, tb * P:(tb + 1) * P], keyT[:, 2 * h + f, :],
                                                   start=True, stop=True)
                    ins.then_inc(key_scored.sem, 1)

                for h in range(RH):
                    if h >= 2:
                        pe.wait_ge(qr_copied.sem, qr_copied.at(l, h - 1))
                    columns(P_QUERY + h, [bank[2 * (h % 2)], bank[2 * (h % 2) + 1]], KD, XTh, XTl)
                    if h >= 1:
                        key_scores(h - 1)
                key_scores(RH - 1)
                pe.wait_ge(split.sem, split.at(l, P_PAD + 1))
                pe.sem_inc(used.sem, 1)
                for tb in range(TB):
                    pe.wait_ge(routed.sem, routed.at(l, tb + 1))
                    for a in range(3):
                        ins = nc.tensor.transpose(bank[tb][:, a * P:(a + 1) * P], route[:, tb, a, :], ident)
                    ins.then_inc(route_turned.sem, 1)

                def dense_gates(b, first):
                    for q in range(16):
                        pe.wait_ge(hots.sem, hots.at(l, 16 * b + (q + 1)))
                        if not (first and q < 4):
                            pe.wait_ge(gate_copied.sem, gate_copied.at(l, 16 * b + (q - 3)))
                        for t in range(4):
                            ins = nc.tensor.matmul(bank[q % 4][:, t * P:(t + 1) * P], hot1[:, q % 2, t, :],
                                                   hot2[:, q % 2, t, :], start=True, stop=True)
                        ins.then_inc(gated.sem, 1)

                pe.wait_ge(route_copied.sem, route_copied.at(l, TB))
                dense_gates(0, True)
                with pe.Fori(1, S // 64) as b:
                    dense_gates(b, False)
                pe.wait_ge(gate_copied.sem, gate_copied.at(l, S // 4))

                def up(g, half, n, slot, first):
                    ph, pl = piece(n, slot)
                    for c in (2 * half, 2 * half + 1):
                        if not first:
                            pe.wait_ge(act_out.sem, act_out.at(l, CG * g + (c - 3)))
                        for k in range(KD):
                            w = slice(((c % 2) * KD + k) * P, ((c % 2) * KD + k + 1) * P)
                            ins = product(bank[c][:], ph[:, w], pl[:, w], XTh[:, k, :], XTl[:, k, :],
                                          k == 0, k == KD - 1)
                        ins.then_inc(u_first.sem if c % 2 == 0 else used.sem, 1)

                def down(g, par, half, n, slot, first):
                    ph, pl = piece(n, slot)
                    pe.wait_ge(w_low.sem, w_low.at(l, CG * g + CG))
                    for s in range(2):
                        if not first:
                            pe.wait_ge(y_added.sem, y_added.at(l, 4 * g + (2 * half + s - 1)))
                        for j in range(2):
                            for c in range(CG):
                                w = slice(c * S + (2 * s + j) * P, c * S + (2 * s + j + 1) * P)
                                ins = product(bank[4 + 2 * s + j][:], ph[:, w], pl[:, w], Wh[:, par, c, :],
                                              Wl[:, par, c, :], c == 0, c == CG - 1)
                        ins.then_inc(v_first.sem if s == 0 else used.sem, 1)

                def pe_group(g, par, first):
                    up(g + 1, 0, 4 * g + (P_TAB + 2), 0, False)
                    down(g, par, 0, 4 * g + (P_TAB + 3), 1, first)
                    up(g + 1, 1, 4 * g + (P_TAB + 4), 0, False)
                    down(g, par, 1, 4 * g + (P_TAB + 5), 1, False)

                up(0, 0, P_TAB, 0, True)
                up(0, 1, P_TAB + 1, 1, True)
                pe_group(0, 0, True)
                with pe.Fori(0, NG // 2 - 1) as m:
                    pe_group(2 * m + 1, 1, False)
                    pe_group(2 * m + 2, 0, False)
                down(NG - 1, 1, 0, V_LAST, 0, False)
                down(NG - 1, 1, 1, V_LAST + 1, 1, False)
                pe.wait_ge(y_added.sem, y_added.at(l, 4 * NG))
                for tb in range(TB):
                    for h in range(2):
                        i = 2 * tb + h
                        if i >= 4:
                            pe.wait_ge(y_resid.sem, y_resid.at(l, i - 3))
                        for k in range(4):
                            ins = nc.tensor.transpose(bank[i % 4][:, k * P:(k + 1) * P],
                                                      Yacc[:, 4 * h + k, tb * P:(tb + 1) * P], ident)
                        ins.then_inc(y_turned.sem, 1)
                turn_x(lambda n: x_normed.at(l, TB + n), None, lambda n: xt_low.at(l, 2 * TB + n))


def shape_tables():
    import numpy as np
    c = np.zeros((P, N_CONST), np.float64)
    c[:, C_IDENT:C_IDENT + P] = np.eye(P)
    c[:, C_IOTA:C_IOTA + P] = np.arange(P)
    a = 2 * np.pi * (np.outer(np.arange(P), np.arange(P)) % P) / P
    c[:, C_DFT:C_DFT + P], c[:, C_DFT + P:C_DFT + 2 * P] = np.cos(a), np.sin(a)
    pos = np.arange(S)
    inv = (1.0 / (np.float32(10000.0) ** (np.arange(0, HD // 2, 2, dtype=np.float32) / np.float32(HD // 2))))
    inv = inv.astype(np.float32)
    row = (pos // 64).astype(np.float32)[:, None] * inv
    col = (pos % 64).astype(np.float32)[:, None] * inv
    ang = np.concatenate([row, row, col, col], 1).astype(np.float64)
    sign = np.tile(np.repeat([-1.0, 1.0], HD // 4), 2)
    c[:, C_COS:C_COS + TB * HD] = np.cos(ang).reshape(TB, P, HD).transpose(1, 0, 2).reshape(P, -1)
    c[:, C_SIN:C_SIN + TB * HD] = (np.sin(ang) * sign).reshape(TB, P, HD).transpose(1, 0, 2).reshape(P, -1)
    b = 2 * np.pi * (np.outer(np.arange(S), np.arange(S)) % S) / S
    scale = 1.0 / np.sqrt(float(S * P))
    pos_dft = np.stack([np.cos(b) * scale, -np.sin(b) * scale])
    pos_dft = pos_dft.reshape(2, TB, P, S).transpose(0, 2, 1, 3).reshape(2, P, PIECE)
    return c.astype(np.float32), pos_dft.astype(np.float32)


def chunk_pieces(w, per):
    k, m = w.shape[0] // P, w.shape[1] // P
    return w.reshape(k, P, m // per, per, P).transpose(2, 1, 3, 0, 4).reshape(m // per, P, PIECE)


def kernel(x, ln0_g, ln0_b, w_in, b_gate, q_norm_g, k_norm_g, w_branch_fourier, w_branch_attn, w_out,
           ln1_g, ln1_b, peer_w_query, peer_sub_keys, peer_u, peer_v, ln2_g, ln2_b):
    import numpy as np
    import concourse.bacc as bacc
    from concourse.bass_utils import run_bass_kernel_spmd as run

    consts, pos_dft = shape_tables()
    order = [g * PAIRS + j for j in range(PAIRS) for g in range(KV_HEADS)]
    DF = GROUPS * P
    stream = np.zeros((DEPTH, NP, P, PIECE), np.float32)
    for l in range(DEPTH):
        w = np.asarray(w_in[l])
        st = stream[l]
        st[P_XF:P_XF + 2] = chunk_pieces(w[:, 0:DF], 2)
        wq = w[:, DF:DF + S].reshape(D, HEADS, HD)[:, order].reshape(2, 4, P, S)
        st[P_Q:P_Q + 2] = wq.transpose(0, 2, 1, 3).reshape(2, P, PIECE)
        st[P_KV] = w[:, DF + S:DF + S + 256].reshape(KD, P, 256).transpose(1, 0, 2).reshape(P, PIECE)
        st[P_COS], st[P_SIN] = pos_dft
        g0 = DF + S + 256
        st[P_GF:P_GF + 4] = chunk_pieces(w[:, g0:g0 + D], 2)
        st[P_GA:P_GA + 4] = chunk_pieces(w[:, g0 + D:g0 + 2 * D], 2)
        st[P_WF:P_WF + 2] = chunk_pieces(np.asarray(w_branch_fourier[l]), 4)
        wa = np.asarray(w_branch_attn[l]).reshape(HEADS, HD, D)[order].reshape(DF, D)
        st[P_WA:P_WA + 2] = chunk_pieces(wa, 4)
        wo = np.asarray(w_out[l]).reshape(KD, P, 4, 256)
        st[P_OUT:P_OUT + 4] = wo.transpose(2, 1, 0, 3).reshape(4, P, PIECE)
        st[P_QUERY:P_QUERY + RH] = chunk_pieces(np.asarray(peer_w_query[l]), 2)
        u = np.asarray(peer_u[l]).reshape(KEYS, 2 * NG, 2, KD, P).transpose(1, 4, 2, 3, 0).reshape(2 * NG, P, PIECE)
        v = np.asarray(peer_v[l]).reshape(KEYS, NG, CG, 2, S).transpose(1, 3, 0, 2, 4).reshape(2 * NG, P, PIECE)
        st[P_TAB:P_TAB + 2] = u[0:2]
        st[P_TAB + 2:NP - 2:2] = u[2:]
        st[P_TAB + 3:NP - 2:2] = v[:-2]
        st[NP - 2:] = v[-2:]
    keys = np.asarray(peer_sub_keys).reshape(DEPTH, 2 * RH, KEYS, P).transpose(0, 3, 1, 2)
    arrays = {
        "x": np.asarray(x).reshape(S, D),
        "stream": stream,
        "keys": np.ascontiguousarray(keys),
        "ln0": np.stack([np.asarray(ln0_g), np.asarray(ln0_b)]),
        "ln1": np.stack([np.asarray(ln1_g), np.asarray(ln1_b)], 1),
        "ln2": np.stack([np.asarray(ln2_g), np.asarray(ln2_b)], 1),
        "qk_gain": np.stack([np.asarray(q_norm_g), np.asarray(k_norm_g)], 1),
        "gate_bias": np.ascontiguousarray(np.asarray(b_gate).reshape(DEPTH, 2, KD, P).transpose(0, 3, 1, 2)),
        "consts": consts,
    }
    nc = bacc.Bacc("TRN2", target_bir_lowering=False, num_devices=1)
    args = [nc.dram_tensor(n, a.shape, F32, kind="ExternalInput").ap() for n, a in arrays.items()]
    out = nc.dram_tensor("out", (S, D), F32, kind="ExternalOutput").ap()
    build(nc, *args, out)
    r = run(nc, [arrays], core_ids=[0])
    return np.asarray(r.results[0]["out"]).reshape(1, S, D)
```

```python
from contextlib import ExitStack

import concourse.bass as bass
from concourse import mybir

F32 = mybir.dt.float32
F32R = mybir.dt.float32r
F16 = mybir.dt.float16
U32 = mybir.dt.uint32
ALU = mybir.AluOpType
ACT = mybir.ActivationFunctionType
AX_X = mybir.AxisListType.X

P = 128
S, D, DEPTH = 512, 1024, 2
TB, KD = S // P, D // P
GROUPS = 4
HEADS, KV_HEADS, HD = 8, 2, 64
PAIRS = HEADS // KV_HEADS
NORMED = HEADS + KV_HEADS
QKV = (HEADS + 2 * KV_HEADS) * HD
RH, KEYS, TOPK = 8, 128, 16
ALPHA = (2.0 * DEPTH) ** 0.25
LN_EPS, RMS_EPS = 1e-5, 1e-6
SCALE = float(HD) ** -0.5
LOWEST = -3.0e38
GATE_SCALE = 2.0 ** 15

PIECE = 2048
LANDINGS, SPLITS = 2, 2
CG = 4
NG = KEYS // CG
P_XF, P_Q, P_KV, P_COS, P_SIN = 0, 2, 4, 5, 6
P_GF, P_WF, P_GA, P_WA, P_OUT = 7, 11, 13, 17, 19
P_QUERY, P_PAD, P_TAB = 23, 31, 32
NP = P_TAB + 4 * NG
EG = 16
E_BEFORE, E_AFTER = 12, 4
E_WITHIN = 2 * EG - E_BEFORE - E_AFTER
assert E_WITHIN == 2 * (S // 64)
P_VA = P_TAB + 2 * EG
P_UV = P_VA + 2 * (EG - 1)
V_LAST = NP - 2
assert P_UV + 4 * (NG - EG) == V_LAST and EG % 2 == 0

C_IDENT, C_IOTA, C_DFT, C_COS, C_SIN = 0, 128, 256, 512, 768
N_CONST = 1024


class Tally:

    def __init__(self, sem, pre, per):
        self.sem, self.pre, self.per = sem, pre, per

    def at(self, layer, n):
        return self.pre + layer * self.per + n


class Chain:

    def __init__(self, eng, sem, base):
        self.eng, self.sem, self.base, self.n = eng, sem, base, 0

    def mark(self, ins):
        self.n += 1
        ins.then_inc(self.sem, 1)
        return self.n

    def wait(self, n=None):
        self.eng.wait_ge(self.sem, self.base + (self.n if n is None else n))

    def link(self, ins):
        self.mark(ins)
        self.wait()


def build(nc, x, stream, keys, ln0, ln1, ln2, qk_gain, gate_bias, consts, out):
    ctx = ExitStack()
    with ctx:
        def sb(name, shape, dt=F32):
            return ctx.enter_context(nc.sbuf_tensor(name, shape, dt))

        def sem(name):
            return ctx.enter_context(nc.semaphore(name))

        def tally(name, pre, per):
            return Tally(sem(name), pre, per)

        X = sb("X", [P, TB, D])
        XTh = sb("XTh", [P, KD, S], F32R)
        XTl = sb("XTl", [P, KD, S], F32R)
        landing = [sb(f"landing{i}", [P, PIECE]) for i in range(LANDINGS)]
        part_h = [sb(f"part_h{i}", [P, PIECE], F32R) for i in range(SPLITS)]
        part_l = [sb(f"part_l{i}", [P, PIECE], F32R) for i in range(SPLITS)]
        C = sb("C", [P, N_CONST])
        LNP = sb("LNP", [P, 2, D])
        QKG = sb("QKG", [P, 2, HD])
        GB = sb("GB", [P, 2, KD])
        stats = sb("stats", [P, TB, 4, 6])
        mv = sb("mv", [P, TB, 2])
        rs = sb("rs", [P, 4, TB * NORMED])
        att = sb("att", [P, 3, 32])
        attr = sb("attr", [P, 32])
        iota4 = sb("iota4", [P, KEYS, 4], F16)
        ident, iota = C[:, C_IDENT:C_IDENT + P], C[:, C_IOTA:C_IOTA + P]
        dft = C[:, C_DFT:C_DFT + 2 * P]
        cos = C[:, C_COS:C_COS + TB * HD].rearrange("p (t d) -> p t d", t=TB)
        sin = C[:, C_SIN:C_SIN + TB * HD].rearrange("p (t d) -> p t d", t=TB)

        base = nc.sbuf_base
        region = sb("region", [P, (nc.sbuf_usable_end - base) // 4 - 8])
        room = 4 * region.shape[1]

        def overlay(name, kib, shape, dt=F32):
            size = 4
            for n in shape[1:]:
                size *= n
            size = size // 2 if dt == F16 else size
            assert kib * 1024 + size <= room, (name, kib * 1024 + size, room)
            return nc.alloc_sbuf_tensor_at(name, shape, dt, offset=base + int(kib * 1024))

        yTh = overlay("yTh", 0, [P, GROUPS, S], F32R)
        yTl = overlay("yTl", 8, [P, GROUPS, S], F32R)
        Ga = overlay("Ga", 0, [P, KD, S])
        oTh = overlay("oTh", 16, [P, PAIRS, S], F32R)
        oTl = overlay("oTl", 24, [P, PAIRS, S], F32R)
        xfT = overlay("xfT", 16, [P, GROUPS, S])
        qkv = overlay("qkv", 32, [P, TB, QKV])
        Ch = overlay("Ch", 44, [P, GROUPS, TB, 2 * P], F32R)
        Cl = overlay("Cl", 60, [P, GROUPS, TB, 2 * P], F32R)
        turn = overlay("turn", 76, [P, 2, NORMED * HD])
        qT = overlay("qT", 44, [P, PAIRS, S])
        kT = overlay("kT", 52, [P, S])
        prob = overlay("prob", 54, [P, 2, S])
        PT = overlay("PT", 58, [P, 2, TB, S])
        Gf = overlay("Gf", 74, [P, KD, S])
        keyT = overlay("keyT", 0, [P, 2 * RH, KEYS])
        qrT = overlay("qrT", 8, [P, 2, 2, S])
        ks = overlay("ks", 16, [P, 2, 2, TB, KEYS])
        kv_ = overlay("kv_", 24, [P, TB, RH, 2, TOPK])
        ki = overlay("ki", 28, [P, TB, RH, 2, TOPK], U32)
        kf = overlay("kf", 32, [P, TB, RH, 2, TOPK])
        cand = overlay("cand", 36, [P, TB, TOPK * TOPK])
        sv = overlay("sv", 40, [P, TB, RH, TOPK])
        pos = overlay("pos", 42, [P, TB, RH, TOPK], U32)
        pab = overlay("pab", 44, [P, 2, TB, RH * TOPK], U32)
        paf = overlay("paf", 48, [P, 2, TB, RH * TOPK])
        pick = overlay("pick", 52, [P, RH, TOPK, TOPK])
        route = overlay("route", 60, [P, TB, 3, RH * TOPK])
        gsum = overlay("gsum", 66, [P, 3, TB * RH])
        routeT = overlay("routeT", 67, [P, 3, S])
        hot1 = overlay("hot1", 0, [P, 2, 2, KEYS, 4], F16)
        hot2 = overlay("hot2", 4, [P, 2, 2, KEYS, 4], F16)
        hot2h = overlay("hot2h", 8, [P, 2, 2, KEYS, 4], F16)
        hot2l = overlay("hot2l", 12, [P, 2, 2, KEYS, 4], F16)
        spill = overlay("spill", 16, [P, 2, NG, 32, CG])
        idx16 = overlay("idx16", 73, [P, 2, S], F16)
        wth = overlay("wth", 75, [P, S], F16)
        wtl = overlay("wtl", 76, [P, S], F16)
        early = overlay("early", 88, [P, 4, S])
        Yacc = overlay("Yacc", 0, [P, KD, S])
        Wh = overlay("Wh", 16, [P, 2, CG, S], F32R)
        Wl = overlay("Wl", 32, [P, 2, CG, S], F32R)
        gate = [overlay(f"gate{i}", 48 + 8 * i, [P, S, CG]) for i in range(2)]
        acts = overlay("acts", 64, [P, 2, S])
        Wf = overlay("Wf", 68, [P, 2, S])
        acts_in = [overlay(f"acts_in{i}", 72 + 8 * i, [P, CG, S]) for i in range(2)]

        bank = [ctx.enter_context(nc.psum_tensor(f"bank{i}", [P, S], F32)) for i in range(8)]
        early_acts = nc.dram_tensor("early_acts", [EG * CG, P, S], F32, kind="Internal").ap()
        dense = nc.dram_tensor("dense_gates", [NG, P, S, CG], F32, kind="Internal").ap()

        landed = [sem(f"landed{i}") for i in range(LANDINGS)]
        high_part = sem("high_part")
        split = tally("split", 0, NP)
        used = tally("used", 0, NP)
        x_in = [sem(f"x_in{tb}") for tb in range(TB)]
        const_in = sem("const_in")
        ln_in = tally("ln_in", 16, 32)
        par_in = tally("par_in", 0, 32)
        key_in = tally("key_in", 0, 16)
        x_normed = tally("x_normed", TB, 2 * TB)
        xt_bank = tally("xt_bank", 2 * TB, 4 * TB)
        xt_high = tally("xt_high", 2 * TB, 4 * TB)
        xt_low = tally("xt_low", 2 * TB, 4 * TB)
        root_in = tally("root_in", 1, 3)
        root_out = tally("root_out", 1, 3)
        xf_copied = tally("xf_copied", 0, GROUPS)
        q_copied = tally("q_copied", 0, TB)
        kv_copied = tally("kv_copied", 0, 2)
        chan_done = tally("chan_done", 0, 8)
        chan_high = tally("chan_high", 0, 8)
        chan_low = tally("chan_low", 0, 8)
        y_high = tally("y_high", 0, GROUPS)
        y_low = tally("y_low", 0, GROUPS)
        roped = tally("roped", 0, TB)
        qk_turned = tally("qk_turned", 0, PAIRS + 1)
        qk_copied = tally("qk_copied", 0, PAIRS + 1)
        scored = tally("scored", 0, 32)
        max_ready = tally("max_ready", 0, 32)
        exped = tally("exped", 0, 32)
        prob_ready = tally("prob_ready", 0, 32)
        p_turned = tally("p_turned", 0, 32)
        p_copied = tally("p_copied", 0, 32)
        pv_done = tally("pv_done", 0, HEADS)
        o_high = tally("o_high", 0, HEADS)
        o_low = tally("o_low", 0, HEADS)
        gatef = tally("gatef", 0, KD)
        gatea = tally("gatea", 0, KD)
        yf_gated = tally("yf_gated", 0, KD)
        ya_gated = tally("ya_gated", 0, KD)
        mixed = tally("mixed", 0, KD)
        mixed_high = tally("mixed_high", 0, KD)
        mixed_low = tally("mixed_low", 0, KD)
        resid = tally("resid", 0, 8)
        qr_copied = tally("qr_copied", 0, RH)
        key_scored = tally("key_scored", 0, RH)
        ks_copied = tally("ks_copied", 0, RH)
        head_cut = tally("head_cut", 0, RH)
        sv_shifted = tally("sv_shifted", 0, 1)
        sv_exped = tally("sv_exped", 0, 1)
        routed = tally("routed", 0, TB)
        route_turned = tally("route_turned", 0, TB)
        route_copied = tally("route_copied", 0, TB)
        hot2_done = tally("hot2_done", 0, S // 8)
        hots = tally("hots", 0, S // 8)
        gated = tally("gated", 0, S // 4)
        gate_copied = tally("gate_copied", 0, S // 4)
        spilled = [tally(f"spilled{i}", 0, 16 * S // 64) for i in range(2)]
        gate_in = [tally(f"gate_in{i}", 0, 16 * NG // 2) for i in range(2)]
        w_split = tally("w_split", 0, TB)
        w_rest = tally("w_rest", 0, TB)
        early_first = tally("early_first", 0, 2 * EG)
        early_out = tally("early_out", 0, CG * EG)
        early_saved = [tally(f"early_saved{i}", 0, 16 * EG) for i in range(4)]
        acts_back = [tally(f"acts_back{i}", 0, 16 * EG // 2) for i in range(2)]
        u_first = tally("u_first", 0, 2 * (NG - EG))
        act_out = tally("act_out", 0, CG * (NG - EG))
        w_full = tally("w_full", 0, CG * NG)
        w_high = tally("w_high", 0, CG * NG)
        w_low = tally("w_low", 0, CG * NG)
        v_first = tally("v_first", 0, 2 * NG)
        y_added = tally("y_added", 0, 4 * NG)
        y_turned = tally("y_turned", 0, 2 * TB)
        y_resid = tally("y_resid", 0, 2 * TB)
        out_done = sem("out_done")
        dve_step = sem("dve_step")
        went_on = sem("went_on")

        FILL = [("gf", m) for m in range(KD)] + [("wf", m) for m in range(KD)] + [("ga", m) for m in range(KD)]
        FILL_LEN = {"gf": KD, "wf": GROUPS, "ga": KD}
        FILL_STEP = -(-sum(FILL_LEN[k] for k, _ in FILL) // 32)
        FILL_END = [sum(FILL_LEN[k] for k, _ in FILL[:i + 1]) for i in range(len(FILL))]
        FILL_UNIT = [(e - 1) // FILL_STEP for e in FILL_END]
        FILL_PER = {"gf": 2, "wf": 4, "ga": 2}
        fill_done = tally("fill_done", 0, sum(m % FILL_PER[k] != FILL_PER[k] - 1 for k, m in FILL))

        def filled(layer, i):
            inner = [m % FILL_PER[k] != FILL_PER[k] - 1 for k, m in FILL[:i + 1]]
            if inner[i]:
                return fill_done.sem, fill_done.at(layer, sum(inner))
            return used.sem, used.at(layer, P_GF + len(inner) - sum(inner))

        block = ctx.enter_context(nc.Block())

        @block.sync
        def _(sp):
            flat = stream.rearrange("l n p w -> (l n) p w")
            for tb in range(TB):
                sp.dma_start(X[:, tb, :], x[tb * P:(tb + 1) * P]).then_inc(x_in[tb], 16)
            for s in range(LANDINGS):
                sp.dma_start(landing[s][:], flat[s]).then_inc(landed[s], 16)
            with sp.Fori(1, DEPTH * NP // LANDINGS) as r:
                for s in range(LANDINGS):
                    sp.wait_ge(split.sem, r * LANDINGS + (s - LANDINGS + 1))
                    sp.dma_start(landing[s][:], flat[r * LANDINGS + s]).then_inc(landed[s], 16)
            sp.wait_ge(x_normed.sem, x_normed.at(DEPTH, 0))
            sp.dma_start(out.rearrange("(t p) d -> p t d", p=P), X[:]).then_inc(out_done, 16)
            sp.wait_ge(out_done, 16)

        @block.gpsimd
        def _(pool):
            def split_round(r, first):
                for s in range(LANDINGS):
                    k = s % SPLITS
                    pool.wait_ge(landed[s], r * 16 + 16)
                    if not (first and s < SPLITS):
                        pool.wait_ge(used.sem, r * LANDINGS + (s - SPLITS + 1))
                    pool.sem_inc(went_on, 1)
                    nc.gpsimd.tensor_scalar(part_h[k][:], landing[s][:], 1.0, 0.0, ALU.mult, ALU.add).then_inc(high_part, 1)
                    pool.wait_ge(high_part, r * LANDINGS + (s + 1))
                    nc.gpsimd.tensor_tensor(part_l[k][:], landing[s][:], part_h[k][:].bitcast(F32),
                                            ALU.subtract).then_inc(split.sem, 1)

            split_round(0, True)
            with pool.Fori(1, DEPTH * NP // LANDINGS) as r:
                split_round(r, False)

        @block.scalar
        def _(act):
            def root(l, n, width):
                act.wait_ge(root_in.sem, root_in.at(l, n) if l is not None else n)
                nc.scalar.activation(rs[:, 1, 0:width], rs[:, 0, 0:width], ACT.Sqrt).then_inc(root_out.sem, 1)

            def xt_parts(at):
                for tb in range(TB):
                    for h in range(2):
                        act.wait_ge(xt_bank.sem, at(2 * tb + h + 1))
                        nc.scalar.copy(XTh[:, 4 * h:4 * h + 4, tb * P:(tb + 1) * P],
                                       bank[4 + (2 * tb + h) % 4][:].rearrange("p (k t) -> p k t", k=4)
                                       ).then_inc(xt_high.sem, 1)

            act.dma_start(C[:], consts).then_inc(const_in, 16)
            act.dma_start(LNP[:], ln0.partition_broadcast(P)).then_inc(ln_in.sem, 16)
            root(None, 1, TB)
            xt_parts(lambda n: n)

            with act.Fori(0, DEPTH) as l:
                act.wait_ge(x_normed.sem, x_normed.at(l, 0))
                act.dma_start(LNP[:], ln1[l].partition_broadcast(P)).then_inc(ln_in.sem, 16)
                act.dma_start(QKG[:], qk_gain[l].partition_broadcast(P)).then_inc(par_in.sem, 16)
                act.dma_start(GB[:], gate_bias[l]).then_inc(par_in.sem, 16)
                for c in range(GROUPS):
                    act.wait_ge(used.sem, used.at(l, P_XF + c // 2 + 1))
                    nc.scalar.copy(xfT[:, c, :], bank[c][:]).then_inc(xf_copied.sem, 1)
                for tb in range(TB):
                    act.wait_ge(used.sem, used.at(l, P_Q + 2))
                    nc.scalar.copy(qkv[:, tb, 0:S], bank[4 + tb][:]).then_inc(q_copied.sem, 1)
                for h in range(2):
                    act.wait_ge(used.sem, used.at(l, P_KV + 1))
                    nc.scalar.copy(qkv[:, 2 * h:2 * h + 2, S:QKV],
                                   bank[h][:].rearrange("p (t c) -> p t c", t=2)).then_inc(kv_copied.sem, 1)
                for p in range(8):
                    act.wait_ge(chan_done.sem, chan_done.at(l, p + 1))
                    nc.scalar.copy(Ch[:, p // 2, 2 * (p % 2):2 * (p % 2) + 2, :],
                                   bank[(2 + p) if p < 6 else (p - 4)][:].rearrange("p (t c) -> p t c", t=2)
                                   ).then_inc(chan_high.sem, 1)
                root(l, 1, TB * NORMED)
                for g in range(GROUPS):
                    act.wait_ge(used.sem, used.at(l, P_SIN + 1))
                    nc.scalar.copy(yTh[:, g, :], bank[4 + g][:]).then_inc(y_high.sem, 1)
                for j in range(PAIRS + 1):
                    act.wait_ge(qk_turned.sem, qk_turned.at(l, j + 1))
                    dst = qT[:, j, :] if j < PAIRS else kT[:]
                    nc.scalar.copy(dst, bank[j][:]).then_inc(qk_copied.sem, 1)

                def p_copy(u):
                    h, tb = u // TB, u % TB
                    act.wait_ge(p_turned.sem, p_turned.at(l, u + 1))
                    if h >= 2:
                        act.wait_ge(pv_done.sem, pv_done.at(l, h - 1))
                    nc.scalar.copy(PT[:, h % 2, :, tb * P:(tb + 1) * P],
                                   bank[2 + u % 2][:].rearrange("p (s t) -> p s t", s=TB)).then_inc(p_copied.sem, 1)

                def fill_gates(u):
                    for i, (kind, m) in enumerate(FILL):
                        if FILL_UNIT[i] != u or kind == "wf":
                            continue
                        act.wait_ge(*filled(l, i))
                        dst, w, done = (Gf, 0, gatef) if kind == "gf" else (Ga, 1, gatea)
                        nc.scalar.activation(dst[:, m, :], bank[6 + i % 2][:], ACT.Sigmoid,
                                             bias=GB[:, w, m:m + 1]).then_inc(done.sem, 1)

                def o_copy(h):
                    g, j = h // PAIRS, h % PAIRS
                    act.wait_ge(pv_done.sem, pv_done.at(l, h + 1))
                    nc.scalar.copy(oTh[g * HD:(g + 1) * HD, j, :],
                                   bank[4 + h % 2][g * HD:(g + 1) * HD, :]).then_inc(o_high.sem, 1)

                act.wait_ge(par_in.sem, par_in.at(l, 32))
                for u in range(32):
                    act.wait_ge(max_ready.sem, max_ready.at(l, u + 1))
                    if u >= 2:
                        act.wait_ge(p_turned.sem, p_turned.at(l, u - 1))
                    nc.scalar.activation(prob[:, u % 2, :], bank[u % 2][:], ACT.Exp, bias=att[:, 1, u:u + 1],
                                         scale=SCALE, accum_out=att[:, 2, u:u + 1]).then_inc(exped.sem, 1)
                    if u >= 1:
                        p_copy(u - 1)
                    if u % TB == 2 and u > TB:
                        o_copy(u // TB - 1)
                    if u >= 1:
                        fill_gates(u - 1)
                p_copy(31)
                o_copy(HEADS - 1)
                fill_gates(31)
                for m in range(KD):
                    act.wait_ge(mixed.sem, mixed.at(l, m + 1))
                    nc.scalar.copy(XTh[:, m, :], Gf[:, m, :]).then_inc(mixed_high.sem, 1)
                act.dma_start(keyT[:], keys[l]).then_inc(key_in.sem, 16)
                root(l, 2, TB)
                xt_parts(lambda n: xt_bank.at(l, n))

                act.wait_ge(x_normed.sem, x_normed.at(l, TB))
                act.dma_start(LNP[:], ln2[l].partition_broadcast(P)).then_inc(ln_in.sem, 16)

                def ks_copy(h):
                    act.wait_ge(key_scored.sem, key_scored.at(l, h + 1))
                    if h >= 2:
                        act.wait_ge(head_cut.sem, head_cut.at(l, h - 1))
                    for f in range(2):
                        ins = nc.scalar.copy(ks[:, h % 2, f, :, :].rearrange("p t k -> p (t k)"),
                                             bank[4 + 2 * (h % 2) + f][:])
                    ins.then_inc(ks_copied.sem, 1)

                for h in range(RH):
                    act.wait_ge(used.sem, used.at(l, P_QUERY + h + 1))
                    if h >= 2:
                        act.wait_ge(key_scored.sem, key_scored.at(l, h - 1))
                    for f in range(2):
                        ins = nc.scalar.copy(qrT[:, h % 2, f, :], bank[2 * (h % 2) + f][:])
                    ins.then_inc(qr_copied.sem, 1)
                    if h >= 1:
                        ks_copy(h - 1)
                ks_copy(RH - 1)

                def early_gelu(n, ready, reuse):
                    slot = reuse[1]
                    act.wait_ge(*ready)
                    if reuse[0] is not None:
                        act.wait_ge(early_saved[slot].sem, reuse[0])
                    nc.scalar.activation(early[:, slot, :], bank[slot][:], ACT.Gelu).then_inc(early_out.sem, 1)
                    act.wait_ge(early_out.sem, early_out.at(l, n + 1))
                    act.dma_start(early_acts[n], early[:, slot, :]).then_inc(early_saved[slot].sem, 16)

                def early_piece(i, base, first):
                    for c in range(2):
                        slot = (2 * i + c) % 4
                        n = 2 * base + (2 * i + c)
                        ready = ((early_first.sem, early_first.at(l, base + (i + 1))) if c == 0
                                 else (used.sem, used.at(l, base + (P_TAB + i + 1))))
                        left = None if first and 2 * i + c < 4 else early_saved[slot].at(
                            l, 8 * base + 16 * ((2 * i + c) // 4))
                        early_gelu(n, ready, (left, slot))

                for i in range(E_BEFORE):
                    early_piece(i, 0, True)
                act.wait_ge(sv_shifted.sem, sv_shifted.at(l, 1))
                nc.scalar.activation(route[:, :, 2, :], sv[:].rearrange("p t h k -> p t (h k)"),
                                     ACT.Exp).then_inc(sv_exped.sem, 1)
                for tb in range(TB):
                    act.wait_ge(route_turned.sem, route_turned.at(l, tb + 1))
                    ts = slice(tb * P, (tb + 1) * P)
                    nc.scalar.copy(routeT[:, :, ts], bank[4 + tb][:, 0:3 * P].rearrange("p (a t) -> p a t", a=3)
                                   ).then_inc(route_copied.sem, 1)
                    nc.scalar.copy(idx16[:, :, ts], bank[4 + tb][:, 0:2 * P].rearrange("p (a t) -> p a t", a=2))
                    nc.scalar.activation(wth[:, ts], bank[4 + tb][:, 2 * P:3 * P], ACT.Copy,
                                         scale=GATE_SCALE).then_inc(w_split.sem, 1)

                def gate_block(b, first):
                    for k in range(2):
                        if not first:
                            act.wait_ge(spilled[k].sem, spilled[k].at(l, 16 * b))
                        for q in range(8):
                            act.wait_ge(gated.sem, gated.at(l, 16 * b + (8 * k + q + 1)))
                            dst = spill[:, k, :, 4 * q:4 * q + 4, :].rearrange("p g t j -> p t g j")
                            nc.scalar.activation(dst, bank[4 + q % 4][:].rearrange("p (t g j) -> p t g j", t=4, j=CG),
                                                 ACT.Copy, scale=1.0 / GATE_SCALE).then_inc(gate_copied.sem, 1)
                            if q % 4 == 3:
                                early_half(b, 2 * k + q // 4)
                        act.wait_ge(gate_copied.sem, gate_copied.at(l, 16 * b + 8 * (k + 1)))
                        dd = dense.rearrange("g p (b t) j -> b p g (t j)", t=32)
                        act.dma_start(dd[2 * b + k], spill[:, k, :, :, :].rearrange("p g t j -> p g (t j)")
                                      ).then_inc(spilled[k].sem, 16)

                def early_half(b, c):
                    slot = (2 * E_BEFORE + c) % 4
                    piece = E_BEFORE + c // 2
                    ready = ((early_first.sem, early_first.at(l, 2 * b + (piece + 1))) if c % 2 == 0
                             else (used.sem, used.at(l, 2 * b + (P_TAB + piece + 1))))
                    left = early_saved[slot].at(l, 16 * b + 16 * ((2 * E_BEFORE + c) // 4))
                    early_gelu(4 * b + (2 * E_BEFORE + c), ready, (left, slot))

                gate_block(0, True)
                with act.Fori(1, S // 64) as b:
                    gate_block(b, False)
                for k in range(2):
                    act.wait_ge(spilled[k].sem, spilled[k].at(l, 16 * (S // 64)))
                for k in range(2):
                    act.dma_start(gate[k][:], dense[k]).then_inc(gate_in[k].sem, 16)
                    act.dma_start(acts_in[k][:], early_acts[CG * k:CG * (k + 1)].rearrange("c p t -> p c t")
                                  ).then_inc(acts_back[k].sem, 16)
                for i in range(E_AFTER):
                    early_piece(E_BEFORE + E_WITHIN + i, 0, True)
                for slot in range(4):
                    act.wait_ge(early_saved[slot].sem, early_saved[slot].at(l, 16 * EG))

                def w_highs(g, par, half):
                    for c in (2 * half, 2 * half + 1):
                        act.wait_ge(w_full.sem, w_full.at(l, CG * g + (c + 1)))
                        nc.scalar.copy(Wh[:, par, c, :], Wf[:, c % 2, :]).then_inc(w_high.sem, 1)

                def activate(g, half):
                    for c in (2 * half, 2 * half + 1):
                        if c % 2 == 0:
                            act.wait_ge(u_first.sem, u_first.at(l, 2 * g + (half + 1 - 2 * EG)))
                        else:
                            act.wait_ge(used.sem, used.at(l, 4 * g + (P_TAB - 1 + 2 * half)))
                        act.wait_ge(w_full.sem, w_full.at(l, CG * g + (c - 1)))
                        nc.scalar.activation(acts[:, c % 2, :], bank[c][:], ACT.Gelu).then_inc(act_out.sem, 1)

                def fetch(g, par, acts_too):
                    act.dma_start(gate[par][:], dense[g]).then_inc(gate_in[par].sem, 16)
                    if acts_too:
                        act.dma_start(acts_in[par][:], early_acts[bass.ds(g * CG, CG)].rearrange("c p t -> p c t")
                                      ).then_inc(acts_back[par].sem, 16)

                def act_group(g, par, early_group, fetch_next, slot_used):
                    if slot_used is not None:
                        act.wait_ge(used.sem, used.at(l, slot_used))
                    for half in range(2):
                        if not early_group:
                            activate(g, half)
                        w_highs(g, par, half)
                    if fetch_next:
                        fetch(g + 2, par, fetch_next == "acts too")

                act_group(0, 0, True, "acts too", None)
                act_group(1, 1, True, "acts too", None)
                with act.Fori(1, EG // 2 - 1) as m:
                    for par in range(2):
                        act_group(2 * m + par, par, True, "acts too", 4 * m + (2 * par + P_VA - 2))
                for par in range(2):
                    act_group(EG - 2 + par, par, True, "gates", 2 * (EG - 2 + par) + P_VA - 2)
                with act.Fori(EG // 2, NG // 2 - 1) as m:
                    for par in range(2):
                        act_group(2 * m + par, par, False, "gates", 8 * m + (4 * par + P_TAB - 2))
                for par in range(2):
                    act_group(NG - 2 + par, par, False, None, 4 * (NG - 2 + par) + P_TAB - 2)
                root(l, 3, TB)
                xt_parts(lambda n: xt_bank.at(l, 2 * TB + n))

        @block.vector
        def _(dve):
            def inv_root(ch, src_ready, n_out, width):
                v, r0 = rs[:, 2, 0:width], rs[:, 1, 0:width]
                a, r = rs[:, 0, 0:width], rs[:, 3, 0:width]
                nc.vector.reciprocal(a, v).then_inc(root_in.sem, 1)
                dve.wait_ge(root_out.sem, n_out)
                ch.link(nc.vector.tensor_tensor(a, r0, r0, ALU.mult))
                ch.link(nc.vector.tensor_tensor(a, a, v, ALU.mult))
                ch.link(nc.vector.tensor_scalar(a, a, -0.5, 1.5, ALU.mult, ALU.add))
                ch.link(nc.vector.tensor_tensor(r, r0, a, ALU.mult))

            def block_stats(ch, tb, q):
                ch.mark(nc.vector.bn_stats(stats[:, tb, q, :], X[:, tb, q * 256:(q + 1) * 256]))

            def layer_norm(ch, n_root, n_par, xt):
                ch.wait()
                for tb in range(TB):
                    ch.mark(nc.vector.bn_aggr(mv[:, tb, :], stats[:, tb, :, :].rearrange("p a b -> p (a b)")))
                ch.wait()
                ch.link(nc.vector.tensor_scalar(rs[:, 2, 0:TB], mv[:, :, 1], LN_EPS, None, ALU.add))
                inv_root(ch, None, n_root, TB)
                dve.wait_ge(ln_in.sem, n_par)
                for tb in range(TB):
                    xb = X[:, tb, :]
                    ch.link(nc.vector.scalar_tensor_tensor(out=xb, in0=xb, scalar=mv[:, tb, 0:1], in1=LNP[:, 0, :],
                                                           op0=ALU.subtract, op1=ALU.mult))
                    nc.vector.scalar_tensor_tensor(out=xb, in0=xb, scalar=rs[:, 3, tb:tb + 1], in1=LNP[:, 1, :],
                                                   op0=ALU.mult, op1=ALU.add).then_inc(x_normed.sem, 1)
                    if tb >= 1:
                        low_parts(tb - 1, xt)
                low_parts(TB - 1, xt)

            def low_parts(tb, xt):
                for h in range(2):
                    dve.wait_ge(xt_high.sem, xt(2 * tb + h + 1))
                    part = XTh[:, 4 * h:4 * h + 4, tb * P:(tb + 1) * P].bitcast(F32)
                    nc.vector.tensor_tensor(XTl[:, 4 * h:4 * h + 4, tb * P:(tb + 1) * P],
                                            bank[4 + (2 * tb + h) % 4][:].rearrange("p (k t) -> p k t", k=4),
                                            part, ALU.subtract).then_inc(xt_low.sem, 1)

            pre = Chain(dve, dve_step, 0)
            for tb in range(TB):
                dve.wait_ge(x_in[tb], 16)
                for q in range(4):
                    block_stats(pre, tb, q)
            dve.wait_ge(const_in, 16)
            pre.mark(nc.vector.tensor_copy(iota4[:], iota.unsqueeze(2).broadcast_to([P, KEYS, 4])))
            layer_norm(pre, 1, 16, lambda n: n)

            with dve.Fori(0, DEPTH) as l:
                dve.sem_clear(dve_step)
                ch = Chain(dve, dve_step, 0)
                for tb in range(TB):
                    dve.wait_ge(q_copied.sem, q_copied.at(l, tb + 1))
                    dve.wait_ge(kv_copied.sem, kv_copied.at(l, tb // 2 + 1))
                    qk = qkv[:, tb, 0:NORMED * HD]
                    ch.link(nc.vector.tensor_tensor(turn[:, 0, :], qk, qk, ALU.mult))
                    ch.link(nc.vector.tensor_reduce(rs[:, 2, tb * NORMED:(tb + 1) * NORMED],
                                                    turn[:, 0, :].rearrange("p (h d) -> p h d", d=HD), AX_X, ALU.add))
                ch.link(nc.vector.tensor_scalar(rs[:, 2, :], rs[:, 2, :], 1.0 / HD, RMS_EPS, ALU.mult, ALU.add))
                for p in range(8):
                    dve.wait_ge(chan_high.sem, chan_high.at(l, p + 1))
                    sl = (slice(None), p // 2, slice(2 * (p % 2), 2 * (p % 2) + 2))
                    nc.vector.tensor_tensor(Cl[sl], bank[(2 + p) if p < 6 else (p - 4)][:].rearrange(
                        "p (t c) -> p t c", t=2), Ch[sl].bitcast(F32), ALU.subtract).then_inc(chan_low.sem, 1)
                inv_root(ch, None, root_out.at(l, 1), TB * NORMED)
                dve.wait_ge(par_in.sem, par_in.at(l, 32))
                for tb in range(TB):
                    qk = qkv[:, tb, 0:NORMED * HD].rearrange("p (h d) -> p h d", d=HD)
                    r = rs[:, 3, tb * NORMED:(tb + 1) * NORMED].unsqueeze(2).broadcast_to([P, NORMED, HD])
                    ch.link(nc.vector.tensor_tensor(qk, qk, r, ALU.mult))
                    for a, b, w in ((0, HEADS, 0), (HEADS, NORMED, 1)):
                        ch.mark(nc.vector.tensor_tensor(qk[:, a:b, :], qk[:, a:b, :],
                                                        QKG[:, w, :].unsqueeze(1).broadcast_to([P, b - a, HD]), ALU.mult))
                    ch.wait()
                    t0 = turn[:, 0, :].rearrange("p (h d) -> p h d", d=HD)
                    t1 = turn[:, 1, :].rearrange("p (h r c d) -> p h r c d", h=NORMED, r=2, c=2)
                    q5 = qkv[:, tb, 0:NORMED * HD].rearrange("p (h r c d) -> p h r c d", h=NORMED, r=2, c=2)
                    s5 = sin[:, tb, :].rearrange("p (r c d) -> p r c d", r=2, c=2)
                    ch.mark(nc.vector.tensor_tensor(t0, qk, cos[:, tb, :].unsqueeze(1).broadcast_to([P, NORMED, HD]),
                                                    ALU.mult))
                    for c in range(2):
                        ch.mark(nc.vector.tensor_tensor(
                            t1[:, :, :, c, :], q5[:, :, :, 1 - c, :],
                            s5[:, :, c, :].unsqueeze(1).broadcast_to([P, NORMED, 2, HD // 4]), ALU.mult))
                    ch.wait()
                    nc.vector.tensor_tensor(qkv[:, tb, 0:NORMED * HD], turn[:, 0, :], turn[:, 1, :],
                                            ALU.add).then_inc(roped.sem, 1)
                    dve.wait_ge(roped.sem, roped.at(l, tb + 1))
                for g in range(GROUPS):
                    dve.wait_ge(y_high.sem, y_high.at(l, g + 1))
                    nc.vector.tensor_tensor(yTl[:, g, :], bank[4 + g][:], yTh[:, g, :].bitcast(F32),
                                            ALU.subtract).then_inc(y_low.sem, 1)

                def row_max(u):
                    dve.wait_ge(scored.sem, scored.at(l, u + 1))
                    ch.link(nc.vector.tensor_reduce(att[:, 0, u:u + 1], bank[u % 2][:], AX_X, ALU.max))
                    nc.vector.tensor_scalar(att[:, 1, u:u + 1], att[:, 0, u:u + 1], -SCALE, None,
                                            ALU.mult).then_inc(max_ready.sem, 1)

                def o_rest(h):
                    g, j = h // PAIRS, h % PAIRS
                    rows = slice(g * HD, (g + 1) * HD)
                    dve.wait_ge(o_high.sem, o_high.at(l, h + 1))
                    nc.vector.tensor_tensor(oTl[rows, j, :], bank[4 + h % 2][rows, :], oTh[rows, j, :].bitcast(F32),
                                            ALU.subtract).then_inc(o_low.sem, 1)

                def fill_products(u):
                    for i, (kind, m) in enumerate(FILL):
                        if kind != "wf" or FILL_UNIT[i] != u:
                            continue
                        dve.wait_ge(gatef.sem, gatef.at(l, m + 1))
                        dve.wait_ge(*filled(l, i))
                        nc.vector.tensor_tensor(Gf[:, m, :], Gf[:, m, :], bank[6 + i % 2][:],
                                                ALU.mult).then_inc(yf_gated.sem, 1)

                row_max(0)
                for u in range(32):
                    if u + 1 < 32:
                        row_max(u + 1)
                    dve.wait_ge(exped.sem, exped.at(l, u + 1))
                    ch.link(nc.vector.reciprocal(attr[:, u:u + 1], att[:, 2, u:u + 1]))
                    nc.vector.tensor_scalar(prob[:, u % 2, :], prob[:, u % 2, :], attr[:, u:u + 1], None,
                                            ALU.mult).then_inc(prob_ready.sem, 1)
                    if u % TB == 3 and u > TB:
                        o_rest(u // TB - 1)
                    if u >= 1:
                        fill_products(u - 1)
                o_rest(HEADS - 1)
                fill_products(31)

                dve.wait_ge(yf_gated.sem, yf_gated.at(l, KD))
                for m in range(KD):
                    dve.wait_ge(gatea.sem, gatea.at(l, m + 1))
                    dve.wait_ge(used.sem, used.at(l, P_WA + m // 4 + 1))
                    nc.vector.tensor_tensor(Ga[:, m, :], Ga[:, m, :], bank[m % 4][:],
                                            ALU.mult).then_inc(ya_gated.sem, 1)
                    dve.wait_ge(ya_gated.sem, ya_gated.at(l, m + 1))
                    nc.vector.tensor_tensor(Gf[:, m, :], Gf[:, m, :], Ga[:, m, :], ALU.add).then_inc(mixed.sem, 1)
                    if m >= 1:
                        dve.wait_ge(mixed_high.sem, mixed_high.at(l, m))
                        nc.vector.tensor_tensor(XTl[:, m - 1, :], Gf[:, m - 1, :], XTh[:, m - 1, :].bitcast(F32),
                                                ALU.subtract).then_inc(mixed_low.sem, 1)
                dve.wait_ge(mixed_high.sem, mixed_high.at(l, KD))
                nc.vector.tensor_tensor(XTl[:, KD - 1, :], Gf[:, KD - 1, :], XTh[:, KD - 1, :].bitcast(F32),
                                        ALU.subtract).then_inc(mixed_low.sem, 1)
                for q in range(4):
                    dve.wait_ge(used.sem, used.at(l, P_OUT + q + 1))
                    for b in range(2):
                        xs = X[:, 2 * b:2 * b + 2, q * 256:(q + 1) * 256]
                        nc.vector.scalar_tensor_tensor(
                            out=xs, in0=xs, scalar=ALPHA,
                            in1=bank[4 + 2 * (q % 2) + b][:].rearrange("p (t c) -> p t c", t=2),
                            op0=ALU.mult, op1=ALU.add).then_inc(resid.sem, 1)
                    dve.wait_ge(resid.sem, resid.at(l, 2 * q + 2))
                    for tb in range(TB):
                        block_stats(ch, tb, q)
                layer_norm(ch, root_out.at(l, 2), ln_in.at(l, 16), lambda n: xt_high.at(l, n))

                def best(width, scores, vals, idx):
                    n0 = ch.n
                    for half in (0, 8):
                        for tb in range(TB):
                            ch.wait(ch.n - (TB - 1) if ch.n - n0 >= TB else n0)
                            ch.mark(nc.vector.max(vals(tb)[:, half:half + 8], scores(tb)))
                        for tb in range(TB):
                            ch.wait(ch.n - (TB - 1))
                            ch.mark(nc.vector.max_index(idx(tb)[:, half:half + 8], vals(tb)[:, half:half + 8],
                                                        scores(tb)))
                        if half == 0:
                            for tb in range(TB):
                                ch.wait(ch.n - (TB - 1))
                                ch.mark(nc.vector.match_replace(scores(tb), vals(tb)[:, 0:8], scores(tb), LOWEST))

                for h in range(RH):
                    dve.wait_ge(ks_copied.sem, ks_copied.at(l, h + 1))
                    dve.sem_inc(went_on, 1)
                    for f in range(2):
                        best(KEYS, lambda tb: ks[:, h % 2, f, tb, :], lambda tb: kv_[:, tb, h, f, :],
                             lambda tb: ki[:, tb, h, f, :])
                    ch.wait()
                    a = kv_[:, :, h, 0, :].unsqueeze(3).broadcast_to([P, TB, TOPK, TOPK])
                    b = kv_[:, :, h, 1, :].unsqueeze(2).broadcast_to([P, TB, TOPK, TOPK])
                    nc.vector.tensor_tensor(cand[:].rearrange("p t (a b) -> p t a b", a=TOPK), a, b,
                                            ALU.add).then_inc(head_cut.sem, 1)
                    dve.wait_ge(head_cut.sem, head_cut.at(l, h + 1))
                    dve.sem_inc(went_on, 1)
                    best(TOPK * TOPK, lambda tb: cand[:, tb, :], lambda tb: sv[:, tb, h, :],
                         lambda tb: pos[:, tb, h, :])
                ch.wait()
                s3 = sv[:].rearrange("p t h k -> p (t h) k")
                ch.link(nc.vector.tensor_copy(gsum[:, 0, :].unsqueeze(2), s3[:, :, 0:1]))
                nc.vector.tensor_tensor(s3, s3, gsum[:, 0, :].unsqueeze(2).broadcast_to([P, TB * RH, TOPK]),
                                        ALU.subtract).then_inc(sv_shifted.sem, 1)
                p2 = pos[:].rearrange("p t h k -> p t (h k)")
                ch.mark(nc.vector.tensor_scalar(pab[:, 0, :, :], p2, 4, None, ALU.logical_shift_right))
                ch.mark(nc.vector.tensor_scalar(pab[:, 1, :, :], p2, TOPK - 1, None, ALU.bitwise_and))
                ch.mark(nc.vector.tensor_copy(kf[:].rearrange("p t h f k -> p (t h f k)"),
                                              ki[:].rearrange("p t h f k -> p (t h f k)")))
                ch.wait()
                ch.link(nc.vector.tensor_copy(paf[:].rearrange("p f t k -> p (f t k)"),
                                              pab[:].rearrange("p f t k -> p (f t k)")))
                for tb in range(TB):
                    for f in range(2):
                        eq = pick[:].rearrange("p h k a -> p (h k) a")
                        ch.link(nc.vector.tensor_tensor(
                            eq, paf[:, f, tb, :].unsqueeze(2).broadcast_to([P, RH * TOPK, TOPK]),
                            iota[:, 0:TOPK].unsqueeze(1).broadcast_to([P, RH * TOPK, TOPK]), ALU.is_equal))
                        ch.link(nc.vector.tensor_tensor(
                            pick[:], pick[:], kf[:, tb, :, f, :].unsqueeze(2).broadcast_to([P, RH, TOPK, TOPK]),
                            ALU.mult))
                        ch.link(nc.vector.tensor_reduce(route[:, tb, f, :], eq, AX_X, ALU.add))
                dve.wait_ge(sv_exped.sem, sv_exped.at(l, 1))
                for tb in range(TB):
                    hs = slice(tb * RH, (tb + 1) * RH)
                    ch.mark(nc.vector.tensor_reduce(gsum[:, 1, hs], route[:, tb, 2, :].rearrange(
                        "p (h k) -> p h k", h=RH), AX_X, ALU.add))
                ch.wait()
                ch.link(nc.vector.reciprocal(gsum[:, 2, :], gsum[:, 1, :]))
                for tb in range(TB):
                    e = route[:, tb, 2, :].rearrange("p (h k) -> p h k", h=RH)
                    rc = gsum[:, 2, tb * RH:(tb + 1) * RH].unsqueeze(2).broadcast_to([P, RH, TOPK])
                    nc.vector.tensor_tensor(e, e, rc, ALU.mult).then_inc(routed.sem, 1)

                for tb in range(TB):
                    dve.wait_ge(route_copied.sem, route_copied.at(l, tb + 1))
                    dve.wait_ge(w_split.sem, w_split.at(l, tb + 1))
                    ts = slice(tb * P, (tb + 1) * P)
                    nc.vector.scalar_tensor_tensor(out=wtl[:, ts], in0=routeT[:, 2, ts], scalar=GATE_SCALE,
                                                   in1=wth[:, ts], op0=ALU.mult, op1=ALU.subtract
                                                   ).then_inc(w_rest.sem, 1)

                def hot_rows(b, first):
                    for q in range(8):
                        slot = q % 2
                        if not (first and q < 2):
                            dve.wait_ge(gated.sem, gated.at(l, 16 * b + (2 * q - 2)))

                        def spread(x):
                            return x[:, bass.ds(64 * b + 8 * q, 8)].rearrange("p (n t) -> p n t", t=4).unsqueeze(
                                2).broadcast_to([P, 2, KEYS, 4])
                        keys4 = iota4[:].unsqueeze(1).broadcast_to([P, 2, KEYS, 4])
                        nc.vector.tensor_tensor(hot1[:, slot], keys4, spread(idx16[:, 0, :]), ALU.is_equal)
                        nc.vector.tensor_tensor(hot2[:, slot], keys4, spread(idx16[:, 1, :]),
                                                ALU.is_equal).then_inc(hot2_done.sem, 1)
                        dve.wait_ge(hot2_done.sem, hot2_done.at(l, 8 * b + (q + 1)))
                        nc.vector.tensor_tensor(hot2h[:, slot], hot2[:, slot], spread(wth), ALU.mult)
                        nc.vector.tensor_tensor(hot2l[:, slot], hot2[:, slot], spread(wtl), ALU.mult).then_inc(hots.sem, 1)

                dve.wait_ge(w_rest.sem, w_rest.at(l, TB))
                dve.sem_inc(went_on, 1)
                hot_rows(0, True)
                with dve.Fori(1, S // 64) as b:
                    hot_rows(b, False)

                dve.wait_ge(spilled[0].sem, spilled[0].at(l, 16 * (S // 64)))
                dve.wait_ge(spilled[1].sem, spilled[1].at(l, 16 * (S // 64)))
                dve.wait_ge(gated.sem, gated.at(l, S // 4))
                ch.link(nc.vector.memset(Yacc[:].rearrange("p k t -> p (k t)"), 0.0))

                def weigh(g, par, half, early_group, first):
                    for c in (2 * half, 2 * half + 1):
                        if not early_group:
                            dve.wait_ge(act_out.sem, act_out.at(l, CG * g + (c + 1 - CG * EG)))
                        if not (first and c < 2):
                            dve.wait_ge(w_high.sem, w_high.at(l, CG * g + (c - 1)))
                            dve.wait_ge(w_low.sem, w_low.at(l, CG * g + (c - 1)))
                        a = acts_in[par][:, c, :] if early_group else acts[:, c % 2, :]
                        nc.vector.tensor_tensor(Wf[:, c % 2, :], a, gate[par][:, :, c],
                                                ALU.mult).then_inc(w_full.sem, 1)
                    for c in (2 * half, 2 * half + 1):
                        dve.wait_ge(w_high.sem, w_high.at(l, CG * g + (c + 1)))
                        nc.vector.tensor_tensor(Wl[:, par, c, :], Wf[:, c % 2, :], Wh[:, par, c, :].bitcast(F32),
                                                ALU.subtract).then_inc(w_low.sem, 1)

                def add_up(g, half, piece_done):
                    for s in range(2):
                        if s == 0:
                            dve.wait_ge(v_first.sem, v_first.at(l, 2 * g + (half + 1)))
                        else:
                            dve.wait_ge(used.sem, used.at(l, piece_done))
                        for j in range(2):
                            k = 4 * half + 2 * s + j
                            ins = nc.vector.tensor_tensor(Yacc[:, k, :], Yacc[:, k, :], bank[4 + 2 * s + j][:],
                                                          ALU.add)
                        ins.then_inc(y_added.sem, 1)

                def dve_group(g, par, early_group, slot_used, v_done):
                    dve.wait_ge(gate_in[par].sem, gate_in[par].at(l, 8 * g + 16 - 8 * par))
                    if early_group:
                        dve.wait_ge(acts_back[par].sem, acts_back[par].at(l, 8 * g + 16 - 8 * par))
                    if slot_used is not None:
                        dve.wait_ge(used.sem, used.at(l, slot_used))
                    weigh(g, par, 0, early_group, False)
                    if slot_used is not None:
                        dve.wait_ge(y_added.sem, y_added.at(l, 4 * g - 4))
                    add_up(g - 1, 0, v_done(0))
                    weigh(g, par, 1, early_group, False)
                    add_up(g - 1, 1, v_done(1))

                dve.wait_ge(gate_in[0].sem, gate_in[0].at(l, 16))
                dve.wait_ge(acts_back[0].sem, acts_back[0].at(l, 16))
                weigh(0, 0, 0, True, True)
                weigh(0, 0, 1, True, False)
                dve_group(1, 1, True, None, lambda half: P_VA + half + 1)
                with dve.Fori(1, EG // 2) as m:
                    for par in range(2):
                        dve_group(2 * m + par, par, True, 4 * m + (2 * par + P_VA - 2),
                                  lambda half: 4 * m + (2 * par + P_VA - 1 + half))
                with dve.Fori(EG // 2, NG // 2) as m:
                    for par in range(2):
                        dve_group(2 * m + par, par, False, 8 * m + (4 * par + P_TAB - 2),
                                  lambda half: 8 * m + (4 * par + P_TAB + 2 * half))
                dve.wait_ge(y_added.sem, y_added.at(l, 4 * NG - 4))
                add_up(NG - 1, 0, V_LAST + 1)
                add_up(NG - 1, 1, V_LAST + 2)
                for h in range(2):
                    for tb in range(TB):
                        i = TB * h + tb
                        dve.wait_ge(y_turned.sem, y_turned.at(l, i + 1))
                        xs = X[:, tb, h * S:(h + 1) * S]
                        nc.vector.scalar_tensor_tensor(out=xs, in0=xs, scalar=ALPHA, in1=bank[i % 4][:],
                                                       op0=ALU.mult, op1=ALU.add).then_inc(y_resid.sem, 1)
                        dve.wait_ge(y_resid.sem, y_resid.at(l, i + 1))
                        block_stats(ch, tb, 2 * h)
                        block_stats(ch, tb, 2 * h + 1)
                layer_norm(ch, root_out.at(l, 3), ln_in.at(l, 32), lambda n: xt_high.at(l, 2 * TB + n))

        @block.tensor
        def _(pe):
            def product(dst, sth, stl, mvh, mvl, first, last):
                nc.tensor.matmul(dst, sth, mvh, start=first, stop=False)
                nc.tensor.matmul(dst, sth, mvl, start=False, stop=False)
                return nc.tensor.matmul(dst, stl, mvh, start=False, stop=last)

            def turn_x(normed, at, low):
                for tb in range(TB):
                    pe.wait_ge(x_normed.sem, normed(tb + 1))
                    for h in range(2):
                        i = 2 * tb + h
                        if i >= 4:
                            pe.wait_ge(xt_low.sem, low(i - 3))
                        for k in range(4):
                            c = 4 * h + k
                            ins = nc.tensor.transpose(bank[4 + i % 4][:, k * P:(k + 1) * P],
                                                      X[:, tb, c * P:(c + 1) * P], ident)
                        ins.then_inc(xt_bank.sem, 1)

            pe.wait_ge(const_in, 16)
            turn_x(lambda n: n, lambda n: n, lambda n: n)

            with pe.Fori(0, DEPTH) as l:
                def piece(n, slot):
                    pe.wait_ge(split.sem, split.at(l, n + 1))
                    return part_h[slot], part_l[slot]

                def columns(n, banks, kc, movh, movl):
                    ph, pl = piece(n, n % 2)
                    for c, b in enumerate(banks):
                        for k in range(kc):
                            w = slice((c * kc + k) * P, (c * kc + k + 1) * P)
                            ins = product(b[:], ph[:, w], pl[:, w], movh[:, k, :], movl[:, k, :],
                                          k == 0, k == kc - 1)
                    ins.then_inc(used.sem, 1)

                pe.wait_ge(xt_low.sem, xt_low.at(l, 0))
                for n in range(2):
                    columns(P_XF + n, [bank[2 * n], bank[2 * n + 1]], KD, XTh, XTl)
                for n in range(2):
                    ph, pl = piece(P_Q + n, (P_Q + n) % 2)
                    for tb in range(TB):
                        for k in range(4):
                            kk, ts, w = 4 * n + k, slice(tb * P, (tb + 1) * P), slice(k * S, (k + 1) * S)
                            ins = product(bank[4 + tb][:], XTh[:, kk, ts], XTl[:, kk, ts], ph[:, w], pl[:, w],
                                          kk == 0, kk == KD - 1)
                    ins.then_inc(used.sem, 1)
                pe.wait_ge(xf_copied.sem, xf_copied.at(l, 2))
                ph, pl = piece(P_KV, P_KV % 2)
                for tb in range(TB):
                    for k in range(KD):
                        ts, w = slice(tb * P, (tb + 1) * P), slice(k * 256, (k + 1) * 256)
                        ins = product(bank[tb // 2][:, (tb % 2) * 256:(tb % 2 + 1) * 256], XTh[:, k, ts], XTl[:, k, ts],
                                      ph[:, w], pl[:, w], k == 0, k == KD - 1)
                ins.then_inc(used.sem, 1)
                for p in range(8):
                    if p == 0:
                        pe.wait_ge(xf_copied.sem, xf_copied.at(l, GROUPS))
                    elif 2 <= p < 6:
                        pe.wait_ge(q_copied.sem, q_copied.at(l, p - 1))
                    elif p >= 6:
                        pe.wait_ge(chan_low.sem, chan_low.at(l, p - 5))
                    for h in range(2):
                        g, tb = p // 2, 2 * (p % 2) + h
                        ins = nc.tensor.matmul(bank[(2 + p) if p < 6 else (p - 4)][:, h * 256:(h + 1) * 256],
                                               xfT[:, g, tb * P:(tb + 1) * P], dft, start=True, stop=True)
                    ins.then_inc(chan_done.sem, 1)
                for n in range(2):
                    ph, pl = piece(P_COS + n, (P_COS + n) % 2)
                    pe.wait_ge(chan_low.sem, chan_low.at(l, 8))
                    for g in range(GROUPS):
                        for s in range(TB):
                            w, cc = slice(s * S, (s + 1) * S), slice(n * P, (n + 1) * P)
                            ins = product(bank[4 + g][:], Ch[:, g, s, cc], Cl[:, g, s, cc], ph[:, w], pl[:, w],
                                          n == 0 and s == 0, n == 1 and s == TB - 1)
                    ins.then_inc(used.sem, 1)
                for tb in range(TB):
                    pe.wait_ge(roped.sem, roped.at(l, tb + 1))
                    if tb == 0:
                        pe.wait_ge(y_low.sem, y_low.at(l, 1))
                    for j in range(PAIRS + 1):
                        ins = nc.tensor.transpose(bank[j][:, tb * P:(tb + 1) * P], qkv[:, tb, j * P:(j + 1) * P], ident)
                        if tb == TB - 1:
                            ins.then_inc(qk_turned.sem, 1)

                def scores(u):
                    h, tb = u // TB, u % TB
                    g, j = h // PAIRS, h % PAIRS
                    if u >= 2:
                        pe.wait_ge(exped.sem, exped.at(l, u - 1))
                    rows = slice(g * HD, (g + 1) * HD)
                    nc.tensor.matmul(bank[u % 2][:], qT[rows, j, tb * P:(tb + 1) * P], kT[rows, :],
                                     start=True, stop=True).then_inc(scored.sem, 1)

                def turn_probs(u):
                    pe.wait_ge(prob_ready.sem, prob_ready.at(l, u + 1))
                    if u >= 2:
                        pe.wait_ge(p_copied.sem, p_copied.at(l, u - 1))
                    for s in range(TB):
                        ins = nc.tensor.transpose(bank[2 + u % 2][:, s * P:(s + 1) * P],
                                                  prob[:, u % 2, s * P:(s + 1) * P], ident)
                    ins.then_inc(p_turned.sem, 1)

                def values(h):
                    pe.wait_ge(p_copied.sem, p_copied.at(l, TB * (h + 1)))
                    if h >= 2:
                        pe.wait_ge(o_low.sem, o_low.at(l, h - 1))
                    for s in range(TB):
                        ins = nc.tensor.matmul(bank[4 + h % 2][:], qkv[:, s, NORMED * HD:QKV], PT[:, h % 2, s, :],
                                               start=(s == 0), stop=(s == TB - 1))
                    ins.then_inc(pv_done.sem, 1)

                def filler():
                    n = P_GF
                    for i, (kind, m) in enumerate(FILL):
                        per = FILL_PER[kind]
                        kc = FILL_LEN[kind]
                        mvh, mvl = (yTh, yTl) if kind == "wf" else (XTh, XTl)
                        if m % per == 0:
                            ph, pl = piece(n, n % 2)
                        if i >= 2:
                            k2, m2 = FILL[i - 2]
                            done = {"gf": gatef, "wf": yf_gated, "ga": gatea}[k2]
                            pe.wait_ge(done.sem, done.at(l, m2 + 1))
                        for k in range(kc):
                            w = slice((m % per * kc + k) * P, (m % per * kc + k + 1) * P)
                            ins = product(bank[6 + i % 2][:], ph[:, w], pl[:, w], mvh[:, k, :], mvl[:, k, :],
                                          k == 0, k == kc - 1)
                            if k == kc - 1:
                                ins.then_inc(used.sem if m % per == per - 1 else fill_done.sem, 1)
                            yield
                        n += m % per == per - 1

                fill = filler()
                pe.wait_ge(qk_copied.sem, qk_copied.at(l, PAIRS + 1))
                pe.wait_ge(y_low.sem, y_low.at(l, GROUPS))
                scores(0)
                for u in range(32):
                    if u + 1 < 32:
                        scores(u + 1)
                    for _ in range(FILL_STEP if u < 31 else 0):
                        next(fill, None)
                    turn_probs(u)
                    if u % TB == 1 and u > TB:
                        values(u // TB - 1)
                values(HEADS - 1)
                for _ in range(FILL_STEP):
                    next(fill, None)
                assert next(fill, "all") == "all"

                pe.wait_ge(p_copied.sem, p_copied.at(l, 32))
                pe.wait_ge(o_low.sem, o_low.at(l, HEADS))
                for n in range(2):
                    if n == 1:
                        pe.wait_ge(ya_gated.sem, ya_gated.at(l, 4))
                    columns(P_WA + n, bank[0:4], PAIRS, oTh, oTl)
                pe.wait_ge(mixed_low.sem, mixed_low.at(l, KD))
                for n in range(4):
                    if n >= 2:
                        pe.wait_ge(resid.sem, resid.at(l, 2 * n - 2))
                    ph, pl = piece(P_OUT + n, (P_OUT + n) % 2)
                    for tb in range(TB):
                        for k in range(KD):
                            ts, w = slice(tb * P, (tb + 1) * P), slice(k * 256, (k + 1) * 256)
                            ins = product(bank[4 + 2 * (n % 2) + tb // 2][:, (tb % 2) * 256:(tb % 2 + 1) * 256],
                                          XTh[:, k, ts], XTl[:, k, ts], ph[:, w], pl[:, w], k == 0, k == KD - 1)
                    ins.then_inc(used.sem, 1)
                turn_x(lambda n: x_normed.at(l, n), None, lambda n: xt_low.at(l, n))

                pe.wait_ge(xt_low.sem, xt_low.at(l, 2 * TB))
                def early_product(i, base, j, first):
                    c, k = divmod(j, KD)
                    slot = (2 * i + c) % 4
                    if j == 0:
                        piece(base + (P_TAB + i), i % 2)
                    if k == 0 and not (first and 2 * i + c < 4):
                        pe.wait_ge(early_out.sem, early_out.at(l, 2 * base + (2 * i + c - 3)))
                    w = slice(j * P, (j + 1) * P)
                    ins = product(bank[slot][:], part_h[i % 2][:, w], part_l[i % 2][:, w], XTh[:, k, :],
                                  XTl[:, k, :], k == 0, k == KD - 1)
                    if k == KD - 1:
                        ins.then_inc(early_first.sem if c == 0 else used.sem, 1)

                def key_scores(h):
                    if h == 0:
                        pe.wait_ge(key_in.sem, key_in.at(l, 16))
                    pe.wait_ge(qr_copied.sem, qr_copied.at(l, h + 1))
                    if h >= 2:
                        pe.wait_ge(ks_copied.sem, ks_copied.at(l, h - 1))
                    for f in range(2):
                        for tb in range(TB):
                            ins = nc.tensor.matmul(bank[4 + 2 * (h % 2) + f][:, tb * P:(tb + 1) * P],
                                                   qrT[:, h % 2, f, tb * P:(tb + 1) * P], keyT[:, 2 * h + f, :],
                                                   start=True, stop=True)
                    ins.then_inc(key_scored.sem, 1)

                for h in range(RH):
                    if h >= 2:
                        pe.wait_ge(qr_copied.sem, qr_copied.at(l, h - 1))
                    columns(P_QUERY + h, [bank[2 * (h % 2)], bank[2 * (h % 2) + 1]], KD, XTh, XTl)
                    if h >= 1:
                        key_scores(h - 1)
                key_scores(RH - 1)
                pe.wait_ge(split.sem, split.at(l, P_PAD + 1))
                pe.sem_inc(used.sem, 1)
                for i in range(E_BEFORE):
                    for j in range(2 * KD):
                        early_product(i, 0, j, True)
                pe.wait_ge(ks_copied.sem, ks_copied.at(l, RH))
                for tb in range(TB):
                    pe.wait_ge(routed.sem, routed.at(l, tb + 1))
                    for a in range(3):
                        ins = nc.tensor.transpose(bank[4 + tb][:, a * P:(a + 1) * P], route[:, tb, a, :], ident)
                    ins.then_inc(route_turned.sem, 1)

                def dense_gates(b, first):
                    for q in range(16):
                        if q % 2 == 0:
                            pe.wait_ge(hots.sem, hots.at(l, 8 * b + (q // 2 + 1)))
                        if not (first and q < 4):
                            pe.wait_ge(gate_copied.sem, gate_copied.at(l, 16 * b + (q - 3)))
                        for t in range(4):
                            dst = bank[4 + q % 4][:, t * P:(t + 1) * P]
                            at = (slice(None), q // 2 % 2, q % 2, slice(None), t)
                            nc.tensor.matmul(dst, hot1[at], hot2h[at], start=True, stop=False)
                            ins = nc.tensor.matmul(dst, hot1[at], hot2l[at], start=False, stop=True)
                        ins.then_inc(gated.sem, 1)
                        for j in range(2):
                            early_product(E_BEFORE + q // 8, 2 * b, 2 * (q % 8) + j, False)

                pe.wait_ge(route_copied.sem, route_copied.at(l, TB))
                pe.wait_ge(w_split.sem, w_split.at(l, TB))
                dense_gates(0, True)
                with pe.Fori(1, S // 64) as b:
                    dense_gates(b, False)
                for i in range(E_AFTER):
                    for j in range(2 * KD):
                        early_product(E_BEFORE + E_WITHIN + i, 0, j, False)
                pe.wait_ge(gate_copied.sem, gate_copied.at(l, S // 4))
                pe.wait_ge(early_out.sem, early_out.at(l, CG * EG))

                def up(g, half, n, slot, first):
                    ph, pl = piece(n, slot)
                    for c in (2 * half, 2 * half + 1):
                        if not first:
                            pe.wait_ge(act_out.sem, act_out.at(l, CG * g + (c - 3 - CG * EG)))
                        for k in range(KD):
                            w = slice(((c % 2) * KD + k) * P, ((c % 2) * KD + k + 1) * P)
                            ins = product(bank[c][:], ph[:, w], pl[:, w], XTh[:, k, :], XTl[:, k, :],
                                          k == 0, k == KD - 1)
                        ins.then_inc(u_first.sem if c % 2 == 0 else used.sem, 1)

                def down(g, par, half, n, slot, first):
                    ph, pl = piece(n, slot)
                    pe.wait_ge(w_low.sem, w_low.at(l, CG * g + CG))
                    for s in range(2):
                        if not first:
                            pe.wait_ge(y_added.sem, y_added.at(l, 4 * g + (2 * half + s - 1)))
                        for j in range(2):
                            for c in range(CG):
                                w = slice(c * S + (2 * s + j) * P, c * S + (2 * s + j + 1) * P)
                                ins = product(bank[4 + 2 * s + j][:], ph[:, w], pl[:, w], Wh[:, par, c, :],
                                              Wl[:, par, c, :], c == 0, c == CG - 1)
                        ins.then_inc(v_first.sem if s == 0 else used.sem, 1)

                def down_group(g, par, n, first):
                    down(g, par, 0, n, 0, first)
                    down(g, par, 1, n + 1, 1, False)

                def both_group(g, par, n, first):
                    up(g + 1, 0, n, 0, first)
                    down(g, par, 0, n + 1, 1, False)
                    up(g + 1, 1, n + 2, 0, first)
                    down(g, par, 1, n + 3, 1, False)

                down_group(0, 0, P_VA, True)
                with pe.Fori(0, EG // 2 - 1) as m:
                    down_group(2 * m + 1, 1, 4 * m + (P_VA + 2), False)
                    down_group(2 * m + 2, 0, 4 * m + (P_VA + 4), False)
                both_group(EG - 1, 1, P_UV, True)
                both_group(EG, 0, P_UV + 4, False)
                with pe.Fori(EG // 2, NG // 2 - 1) as m:
                    both_group(2 * m + 1, 1, 8 * m + (P_UV - 4 * (EG - 2)), False)
                    both_group(2 * m + 2, 0, 8 * m + (P_UV - 4 * (EG - 3)), False)
                down(NG - 1, 1, 0, V_LAST, 0, False)
                down(NG - 1, 1, 1, V_LAST + 1, 1, False)
                for h in range(2):
                    pe.wait_ge(y_added.sem, y_added.at(l, 4 * NG - 2 + 2 * h))
                    for tb in range(TB):
                        i = TB * h + tb
                        if i >= 4:
                            pe.wait_ge(y_resid.sem, y_resid.at(l, i - 3))
                        for k in range(4):
                            ins = nc.tensor.transpose(bank[i % 4][:, k * P:(k + 1) * P],
                                                      Yacc[:, 4 * h + k, tb * P:(tb + 1) * P], ident)
                        ins.then_inc(y_turned.sem, 1)
                turn_x(lambda n: x_normed.at(l, TB + n), None, lambda n: xt_low.at(l, 2 * TB + n))


def shape_tables():
    import numpy as np
    c = np.zeros((P, N_CONST), np.float64)
    c[:, C_IDENT:C_IDENT + P] = np.eye(P)
    c[:, C_IOTA:C_IOTA + P] = np.arange(P)
    a = 2 * np.pi * (np.outer(np.arange(P), np.arange(P)) % P) / P
    c[:, C_DFT:C_DFT + P], c[:, C_DFT + P:C_DFT + 2 * P] = np.cos(a), np.sin(a)
    pos = np.arange(S)
    inv = (1.0 / (np.float32(10000.0) ** (np.arange(0, HD // 2, 2, dtype=np.float32) / np.float32(HD // 2))))
    inv = inv.astype(np.float32)
    row = (pos // 64).astype(np.float32)[:, None] * inv
    col = (pos % 64).astype(np.float32)[:, None] * inv
    ang = np.concatenate([row, row, col, col], 1).astype(np.float64)
    sign = np.tile(np.repeat([-1.0, 1.0], HD // 4), 2)
    c[:, C_COS:C_COS + TB * HD] = np.cos(ang).reshape(TB, P, HD).transpose(1, 0, 2).reshape(P, -1)
    c[:, C_SIN:C_SIN + TB * HD] = (np.sin(ang) * sign).reshape(TB, P, HD).transpose(1, 0, 2).reshape(P, -1)
    b = 2 * np.pi * (np.outer(np.arange(S), np.arange(S)) % S) / S
    scale = 1.0 / np.sqrt(float(S * P))
    pos_dft = np.stack([np.cos(b) * scale, -np.sin(b) * scale])
    pos_dft = pos_dft.reshape(2, TB, P, S).transpose(0, 2, 1, 3).reshape(2, P, PIECE)
    return c.astype(np.float32), pos_dft.astype(np.float32)


def chunk_pieces(w, per):
    k, m = w.shape[0] // P, w.shape[1] // P
    return w.reshape(k, P, m // per, per, P).transpose(2, 1, 3, 0, 4).reshape(m // per, P, PIECE)


def kernel(x, ln0_g, ln0_b, w_in, b_gate, q_norm_g, k_norm_g, w_branch_fourier, w_branch_attn, w_out,
           ln1_g, ln1_b, peer_w_query, peer_sub_keys, peer_u, peer_v, ln2_g, ln2_b):
    import numpy as np
    import concourse.bacc as bacc
    from concourse.bass_utils import run_bass_kernel_spmd as run

    consts, pos_dft = shape_tables()
    order = [g * PAIRS + j for j in range(PAIRS) for g in range(KV_HEADS)]
    DF = GROUPS * P
    stream = np.zeros((DEPTH, NP, P, PIECE), np.float32)
    for l in range(DEPTH):
        w = np.asarray(w_in[l])
        st = stream[l]
        st[P_XF:P_XF + 2] = chunk_pieces(w[:, 0:DF], 2)
        wq = w[:, DF:DF + S].reshape(D, HEADS, HD)[:, order].reshape(2, 4, P, S)
        st[P_Q:P_Q + 2] = wq.transpose(0, 2, 1, 3).reshape(2, P, PIECE)
        st[P_KV] = w[:, DF + S:DF + S + 256].reshape(KD, P, 256).transpose(1, 0, 2).reshape(P, PIECE)
        st[P_COS], st[P_SIN] = pos_dft
        g0 = DF + S + 256
        st[P_GF:P_GF + 4] = chunk_pieces(w[:, g0:g0 + D], 2)
        st[P_GA:P_GA + 4] = chunk_pieces(w[:, g0 + D:g0 + 2 * D], 2)
        st[P_WF:P_WF + 2] = chunk_pieces(np.asarray(w_branch_fourier[l]), 4)
        wa = np.asarray(w_branch_attn[l]).reshape(HEADS, HD, D)[order].reshape(DF, D)
        st[P_WA:P_WA + 2] = chunk_pieces(wa, 4)
        wo = np.asarray(w_out[l]).reshape(KD, P, 4, 256)
        st[P_OUT:P_OUT + 4] = wo.transpose(2, 1, 0, 3).reshape(4, P, PIECE)
        st[P_QUERY:P_QUERY + RH] = chunk_pieces(np.asarray(peer_w_query[l]), 2)
        u = np.asarray(peer_u[l]).reshape(KEYS, 2 * NG, 2, KD, P).transpose(1, 4, 2, 3, 0).reshape(2 * NG, P, PIECE)
        v = np.asarray(peer_v[l]).reshape(KEYS, NG, CG, 2, S).transpose(1, 3, 0, 2, 4).reshape(2 * NG, P, PIECE)
        st[P_TAB:P_VA] = u[0:2 * EG]
        st[P_VA:P_UV] = v[0:2 * (EG - 1)]
        st[P_UV:V_LAST:2] = u[2 * EG:]
        st[P_UV + 1:V_LAST:2] = v[2 * (EG - 1):-2]
        st[V_LAST:] = v[-2:]
    keys = np.asarray(peer_sub_keys).reshape(DEPTH, 2 * RH, KEYS, P).transpose(0, 3, 1, 2)
    arrays = {
        "x": np.asarray(x).reshape(S, D),
        "stream": stream,
        "keys": np.ascontiguousarray(keys),
        "ln0": np.stack([np.asarray(ln0_g), np.asarray(ln0_b)]),
        "ln1": np.stack([np.asarray(ln1_g), np.asarray(ln1_b)], 1),
        "ln2": np.stack([np.asarray(ln2_g), np.asarray(ln2_b)], 1),
        "qk_gain": np.stack([np.asarray(q_norm_g), np.asarray(k_norm_g)], 1),
        "gate_bias": np.ascontiguousarray(np.asarray(b_gate).reshape(DEPTH, 2, KD, P).transpose(0, 3, 1, 2)),
        "consts": consts,
    }
    nc = bacc.Bacc("TRN2", target_bir_lowering=False, num_devices=1)
    args = [nc.dram_tensor(n, a.shape, F32, kind="ExternalInput").ap() for n, a in arrays.items()]
    out = nc.dram_tensor("out", (S, D), F32, kind="ExternalOutput").ap()
    build(nc, *args, out)
    r = run(nc, [arrays], core_ids=[0])
    return np.asarray(r.results[0]["out"]).reshape(1, S, D)
```

```python
from contextlib import ExitStack

import concourse.bass as bass
from concourse import mybir

F32 = mybir.dt.float32
F32R = mybir.dt.float32r
F16 = mybir.dt.float16
U32 = mybir.dt.uint32
ALU = mybir.AluOpType
ACT = mybir.ActivationFunctionType
AX_X = mybir.AxisListType.X

P = 128
S, D, DEPTH = 512, 1024, 2
TB, KD = S // P, D // P
GROUPS = 4
HEADS, KV_HEADS, HD = 8, 2, 64
PAIRS = HEADS // KV_HEADS
NORMED = HEADS + KV_HEADS
QKV = (HEADS + 2 * KV_HEADS) * HD
RH, KEYS, TOPK = 8, 128, 16
ALPHA = (2.0 * DEPTH) ** 0.25
LN_EPS, RMS_EPS = 1e-5, 1e-6
SCALE = float(HD) ** -0.5
LOWEST = -3.0e38
GATE_SCALE = 2.0 ** 15

PIECE = 2048
LANDINGS, SPLITS = 2, 2
CG = 4
NG = KEYS // CG
P_Q, P_XF, P_KV, P_DFT = 0, 2, 4, 5
P_GF, P_WF, P_GA, P_WA, P_OUT = 6, 10, 12, 16, 18
P_QUERY, P_TAB = 22, 30
NP = P_TAB + 4 * NG
EG = 16
E_BEFORE, E_AFTER = 12, 4
E_WITHIN = 2 * EG - E_BEFORE - E_AFTER
KEYS_BESIDE = [0, 2]
E_EXP = 6
assert E_WITHIN == 2 * (S // 64)
BLOCK_ORDER = [(0, 0), (1, 0), (0, 1), (1, 1), (2, 0), (3, 0), (2, 1), (3, 1)]
P_VA = P_TAB + 2 * EG
P_UV = P_VA + 2 * (EG - 1)
V_LAST = NP - 2
assert P_UV + 4 * (NG - EG) == V_LAST and EG % 2 == 0 and NP % 2 == 0

HALF = S // 2
NCOS = HALF + 2
T_MID, T_SIN = 2 * NCOS, 3 * NCOS

C_IDENT, C_IOTA, C_DFT, C_COS, C_SIN = 0, 128, 256, 512, 768
N_CONST = 1024


class Tally:

    def __init__(self, sem, pre, per):
        self.sem, self.pre, self.per = sem, pre, per

    def at(self, layer, n):
        return self.pre + layer * self.per + n


class Chain:

    def __init__(self, eng, sem, base):
        self.eng, self.sem, self.base, self.n = eng, sem, base, 0

    def mark(self, ins):
        self.n += 1
        ins.then_inc(self.sem, 1)
        return self.n

    def wait(self, n=None):
        self.eng.wait_ge(self.sem, self.base + (self.n if n is None else n))

    def link(self, ins):
        self.mark(ins)
        self.wait()


def build(nc, x, stream, keys, ln0, ln1, ln2, qk_gain, gate_bias, consts, out):
    ctx = ExitStack()
    with ctx:
        def sb(name, shape, dt=F32):
            return ctx.enter_context(nc.sbuf_tensor(name, shape, dt))

        def sem(name):
            return ctx.enter_context(nc.semaphore(name))

        def tally(name, pre, per):
            return Tally(sem(name), pre, per)

        X = sb("X", [P, TB, D])
        XTh = sb("XTh", [P, KD, S], F32R)
        XTl = sb("XTl", [P, KD, S], F32R)
        landing = [sb(f"landing{i}", [P, PIECE]) for i in range(LANDINGS)]
        part_h = [sb(f"part_h{i}", [P, PIECE], F32R) for i in range(SPLITS)]
        part_l = [sb(f"part_l{i}", [P, PIECE], F32R) for i in range(SPLITS)]
        C = sb("C", [P, N_CONST])
        LNP = sb("LNP", [P, 2, D])
        QKG = sb("QKG", [P, 2, HD])
        GB = sb("GB", [P, 2, KD])
        stats = sb("stats", [P, TB, 2, 6])
        mv = sb("mv", [P, TB, 2])
        rs = sb("rs", [P, 4, TB * NORMED])
        att = sb("att", [P, 3, 32])
        attr = sb("attr", [P, 32])
        iota4 = sb("iota4", [P, KEYS, 4], F16)
        ident, iota = C[:, C_IDENT:C_IDENT + P], C[:, C_IOTA:C_IOTA + P]
        dft = C[:, C_DFT:C_DFT + 2 * P]
        cos = C[:, C_COS:C_COS + TB * HD].rearrange("p (t d) -> p t d", t=TB)
        sin = C[:, C_SIN:C_SIN + TB * HD].rearrange("p (t d) -> p t d", t=TB)

        base = nc.sbuf_base
        region = sb("region", [P, (nc.sbuf_usable_end - base) // 4 - 8])
        room = 4 * region.shape[1]

        def overlay(name, kib, shape, dt=F32):
            size = 4
            for n in shape[1:]:
                size *= n
            size = size // 2 if dt == F16 else size
            assert kib * 1024 + size <= room, (name, kib * 1024 + size, room)
            return nc.alloc_sbuf_tensor_at(name, shape, dt, offset=base + int(kib * 1024))

        yTh = overlay("yTh", 0, [P, GROUPS, S], F32R)
        yTl = overlay("yTl", 8, [P, GROUPS, S], F32R)
        Ga = overlay("Ga", 0, [P, KD, S])
        oTh = overlay("oTh", 44, [P, PAIRS, S], F32R)
        oTl = overlay("oTl", 24, [P, PAIRS, S], F32R)
        xfT = overlay("xfT", 16, [P, GROUPS, S])
        yf = overlay("yf", 24, [P, GROUPS, S])
        sines = overlay("sines", 72, [P, GROUPS, HALF])
        qkv = overlay("qkv", 32, [P, TB, QKV])
        Zh = overlay("Zh", 44, [P, GROUPS, 4, P], F32R)
        Zl = overlay("Zl", 52, [P, GROUPS, 4, P], F32R)
        even_odd = overlay("even_odd", 60, [P, GROUPS, 2, HALF])
        mid_h = overlay("mid_h", 68, [P, GROUPS, P], F32R)
        mid_l = overlay("mid_l", 70, [P, GROUPS, P], F32R)
        turn = overlay("turn", 76, [P, 2, NORMED * HD])
        q_split = overlay("q_split", 52, [P, TB, HEADS, 2, HD], F32R)
        k_split = overlay("k_split", 68, [P, TB, KV_HEADS, 3, HD], F32R)
        q_stack = [overlay(f"q_stack{i}", kib, [P, PAIRS, S], F32R) for i, kib in enumerate((44, 16))]
        k_stack = [overlay(f"k_stack{g}", 90 + 2 * g, [P, S], F32R) for g in range(KV_HEADS)]
        k_low = [overlay(f"k_low{g}", kib, [P, S], F32R) for g, kib in enumerate((52, 94))]
        prob = overlay("prob", 54, [P, 2, S])
        PT = overlay("PT", 58, [P, 2, TB, S])
        Gf = overlay("Gf", 74, [P, KD, S])
        keyT = overlay("keyT", 0, [P, 2 * RH, KEYS])
        qrT = overlay("qrT", 8, [P, 2, 2, S])
        ks = overlay("ks", 16, [P, 2, 2, TB, KEYS])
        kv_ = overlay("kv_", 24, [P, TB, RH, 2, TOPK])
        ki = overlay("ki", 28, [P, TB, RH, 2, TOPK], U32)
        kf = overlay("kf", 32, [P, TB, RH, 2, TOPK])
        cand = overlay("cand", 36, [P, TB, TOPK * TOPK])
        sv = overlay("sv", 40, [P, TB, RH, TOPK])
        pos = overlay("pos", 42, [P, TB, RH, TOPK], U32)
        pab = overlay("pab", 44, [P, 2, TB, RH * TOPK], U32)
        paf = overlay("paf", 48, [P, 2, TB, RH * TOPK])
        pick = overlay("pick", 52, [P, RH, TOPK, TOPK])
        route = overlay("route", 60, [P, TB, 3, RH * TOPK])
        gsum = overlay("gsum", 66, [P, 3, TB * RH])
        routeT = overlay("routeT", 67, [P, 3, S])
        hot1 = overlay("hot1", 0, [P, 2, 2, KEYS, 4], F16)
        hot2 = overlay("hot2", 4, [P, 2, 2, KEYS, 4], F16)
        hot2h = overlay("hot2h", 8, [P, 2, 2, KEYS, 4], F16)
        hot2l = overlay("hot2l", 12, [P, 2, 2, KEYS, 4], F16)
        spill = overlay("spill", 16, [P, 2, NG, 32, CG])
        idx16 = overlay("idx16", 73, [P, 2, S], F16)
        wth = overlay("wth", 75, [P, S], F16)
        wtl = overlay("wtl", 76, [P, S], F16)
        early = overlay("early", 88, [P, 4, S])
        Wh = overlay("Wh", 16, [P, 2, CG, S], F32R)
        Wl = overlay("Wl", 32, [P, 2, CG, S], F32R)
        gate = [overlay(f"gate{i}", 48 + 8 * i, [P, S, CG]) for i in range(2)]
        acts = overlay("acts", 64, [P, 2, S])
        Wf = overlay("Wf", 68, [P, 2, S])
        acts_in = [overlay(f"acts_in{i}", 72 + 8 * i, [P, CG, S]) for i in range(2)]

        bank = [ctx.enter_context(nc.psum_tensor(f"bank{i}", [P, S], F32)) for i in range(8)]
        early_acts = nc.dram_tensor("early_acts", [EG * CG, P, S], F32, kind="Internal").ap()
        dense = nc.dram_tensor("dense_gates", [NG, P, S, CG], F32, kind="Internal").ap()

        landed = [sem(f"landed{i}") for i in range(LANDINGS)]
        high_part = sem("high_part")
        split = tally("split", 0, 2 * NP)
        used = tally("used", 0, NP)
        x_in = [sem(f"x_in{tb}") for tb in range(TB)]
        const_in = sem("const_in")
        ln_in = tally("ln_in", 16, 32)
        par_in = tally("par_in", 0, 32)
        key_in = tally("key_in", 0, 16)
        x_normed = tally("x_normed", TB, 2 * TB)
        xt_bank = tally("xt_bank", TB, 4 * TB)
        xt_high = tally("xt_high", TB, 4 * TB)
        xt_low = tally("xt_low", TB, 4 * TB)
        root_in = tally("root_in", 2, 6)
        root_out = tally("root_out", 2, 6)
        xf_copied = tally("xf_copied", 0, GROUPS)
        q_copied = tally("q_copied", 0, TB)
        kv_copied = tally("kv_copied", 0, 2)
        folded = tally("folded", 0, GROUPS)
        chan_done = tally("chan_done", 0, GROUPS + 1)
        chan_high = tally("chan_high", 0, GROUPS + 1)
        chan_low = tally("chan_low", 0, GROUPS + 1)
        y_done = tally("y_done", 0, GROUPS - 1)
        sines_copied = tally("sines_copied", 0, GROUPS)
        y_summed = tally("y_summed", 0, GROUPS)
        y_high = tally("y_high", 0, GROUPS)
        y_low = tally("y_low", 0, GROUPS)
        q_roped = tally("q_roped", 0, TB)
        k_roped = tally("k_roped", 0, TB)
        qk_high = tally("qk_high", 0, TB + 1)
        qk_low = tally("qk_low", 0, TB + 1)
        qk_turned = tally("qk_turned", 0, HEADS + 4)
        qk_copied = tally("qk_copied", 0, HEADS + 4)
        scored = tally("scored", 0, 32)
        max_ready = tally("max_ready", 0, 32)
        exped = tally("exped", 0, 32)
        prob_ready = tally("prob_ready", 0, 32)
        p_turned = tally("p_turned", 0, 32)
        p_copied = tally("p_copied", 0, 32)
        pv_done = tally("pv_done", 0, HEADS)
        o_high = tally("o_high", 0, HEADS)
        o_low = tally("o_low", 0, HEADS)
        gatef = tally("gatef", 0, KD)
        gatea = tally("gatea", 0, KD)
        yf_gated = tally("yf_gated", 0, KD)
        wa_done = tally("wa_done", 0, KD - 2)
        ya_gated = tally("ya_gated", 0, KD)
        mixed = tally("mixed", 0, KD)
        mixed_high = tally("mixed_high", 0, KD)
        mixed_low = tally("mixed_low", 0, KD)
        rows_done = tally("rows_done", 0, 2 * (TB - 1))
        resid = tally("resid", 0, 4 + TB)
        qr_copied = tally("qr_copied", 0, RH)
        key_scored = tally("key_scored", 0, RH)
        ks_copied = tally("ks_copied", 0, RH)
        head_cut = tally("head_cut", 0, RH)
        sv_shifted = tally("sv_shifted", 0, 1)
        sv_exped = tally("sv_exped", 0, 1)
        routed = tally("routed", 0, TB)
        route_turned = tally("route_turned", 0, TB)
        route_copied = tally("route_copied", 0, TB)
        hot2_done = tally("hot2_done", 0, S // 8)
        hots = tally("hots", 0, S // 8)
        gated = tally("gated", 0, S // 4)
        gate_copied = tally("gate_copied", 0, S // 4)
        spilled = [tally(f"spilled{i}", 0, 16 * S // 64) for i in range(2)]
        gate_in = [tally(f"gate_in{i}", 0, 16 * NG // 2) for i in range(2)]
        w_split = tally("w_split", 0, TB)
        w_rest = tally("w_rest", 0, TB)
        early_first = tally("early_first", 0, 2 * EG)
        early_out = tally("early_out", 0, CG * EG)
        early_saved = [tally(f"early_saved{i}", 0, 16 * EG) for i in range(4)]
        acts_back = [tally(f"acts_back{i}", 0, 16 * EG // 2) for i in range(2)]
        u_first = tally("u_first", 0, 2 * (NG - EG))
        act_out = tally("act_out", 0, CG * (NG - EG))
        w_full = tally("w_full", 0, CG * NG)
        w_high = tally("w_high", 0, CG * NG)
        w_low = tally("w_low", 0, CG * NG)
        v_first = tally("v_first", 0, 2 * (NG - 1))
        y_added = tally("y_added", 0, 4 * (NG - 1))
        y_resid = tally("y_resid", 0, TB)
        out_done = sem("out_done")
        dve_step = sem("dve_step")
        went_on = sem("went_on")

        FILL = [("gf", m) for m in range(KD)] + [("wf", m) for m in range(KD)] + [("ga", m) for m in range(KD)]
        FILL_LEN = {"gf": KD, "wf": GROUPS, "ga": KD}
        FILL_DFT, FILL_Q, FILL_QK, FILL_FIRST, FILL_LAST, FILL_TURNED, FILL_VALUES = 10, 12, 4, 4, 4, 3, 4
        FILL_END = [sum(FILL_LEN[k] for k, _ in FILL[:i + 1]) for i in range(len(FILL))]
        beside = FILL_END[-1] - FILL_DFT - FILL_Q - FILL_QK - FILL_FIRST - FILL_LAST - FILL_TURNED - FILL_VALUES
        FILL_STEP = [FILL_FIRST] + [beside * (u + 1) // 30 - beside * u // 30 for u in range(30)] + [FILL_LAST]
        FILL_UNIT = [-2 if e <= FILL_DFT else -1 if e <= FILL_DFT + FILL_Q + FILL_QK else
                     min(sum(FILL_DFT + FILL_Q + FILL_QK + sum(FILL_STEP[:u + 1]) < e for u in range(32)), 31) for e in FILL_END]
        FILL_PER = {"gf": 2, "wf": 4, "ga": 2}
        fill_done = tally("fill_done", 0, sum(m % FILL_PER[k] != FILL_PER[k] - 1 for k, m in FILL))

        def filled(layer, i):
            inner = [m % FILL_PER[k] != FILL_PER[k] - 1 for k, m in FILL[:i + 1]]
            if inner[i]:
                return fill_done.sem, fill_done.at(layer, sum(inner))
            return used.sem, used.at(layer, P_GF + len(inner) - sum(inner))

        Y_UNITS = [0, 1, 2, 3]

        def stacked(i):
            if i < HEADS:
                return q_stack[i // PAIRS][:, i % PAIRS, :]
            g, low = (i - HEADS) // 2, (i - HEADS) % 2
            return k_low[g][0:HD, :] if low else k_stack[g][:]

        def y_ready(layer, g):
            return (y_done.sem, y_done.at(layer, g + 1)) if g < GROUPS - 1 else (used.sem, used.at(layer, P_DFT + 1))

        def wa_ready(layer, m):
            if m % 4 < 3:
                return wa_done.sem, wa_done.at(layer, 3 * (m // 4) + m % 4 + 1)
            return used.sem, used.at(layer, P_WA + m // 4 + 1)

        def rows_ready(layer, n, tb, piece_done):
            if tb < TB - 1:
                return rows_done.sem, rows_done.at(layer, n * (TB - 1) + tb + 1)
            return used.sem, used.at(layer, piece_done)

        block = ctx.enter_context(nc.Block())

        TURN_LOW, TURN_HIGH = [0, 1, 2, 3], [4, 5, 6, 7]
        XF_BANK = [4, 5, 6, 7]
        CHAN_BANK = [6, 2, 3, 4, 5]
        COS_BANK, SIN_BANK = [7, 6, 2, 4], [0, 1, 3, 5]

        @block.sync
        def _(sp):
            flat = stream.rearrange("l n p w -> (l n) p w")
            for s in range(LANDINGS):
                for tb in (2 * s, 2 * s + 1):
                    sp.dma_start(X[:, tb, :], x[tb * P:(tb + 1) * P]).then_inc(x_in[tb], 16)
                sp.dma_start(landing[s][:], flat[s]).then_inc(landed[s], 16)
            with sp.Fori(1, DEPTH * NP // LANDINGS) as r:
                for s in range(LANDINGS):
                    sp.wait_ge(split.sem, r * (2 * LANDINGS) + 2 * (s - LANDINGS + 1))
                    sp.dma_start(landing[s][:], flat[r * LANDINGS + s]).then_inc(landed[s], 16)
            for tb in range(TB):
                sp.wait_ge(x_normed.sem, x_normed.at(DEPTH, tb + 1 - TB))
                sp.dma_start(out[tb * P:(tb + 1) * P], X[:, tb, :]).then_inc(out_done, 16)
            sp.wait_ge(out_done, 16 * TB)

        @block.gpsimd
        def _(pool):
            def split_round(r, first):
                for s in range(LANDINGS):
                    k = s % SPLITS
                    pool.wait_ge(landed[s], r * 16 + 16)
                    if not (first and s < SPLITS):
                        pool.wait_ge(used.sem, r * LANDINGS + (s - SPLITS + 1))
                    pool.sem_inc(went_on, 1)
                    for h in range(2):
                        w = slice(h * PIECE // 2, (h + 1) * PIECE // 2)
                        nc.gpsimd.tensor_scalar(part_h[k][:, w], landing[s][:, w], 1.0, 0.0, ALU.mult,
                                                ALU.add).then_inc(high_part, 1)
                        pool.wait_ge(high_part, r * (2 * LANDINGS) + (2 * s + h + 1))
                        nc.gpsimd.tensor_tensor(part_l[k][:, w], landing[s][:, w], part_h[k][:, w].bitcast(F32),
                                                ALU.subtract).then_inc(split.sem, 1)

            split_round(0, True)
            with pool.Fori(1, DEPTH * NP // LANDINGS) as r:
                split_round(r, False)

        @block.scalar
        def _(act):
            def root(count, cols):
                act.wait_ge(root_in.sem, count)
                nc.scalar.activation(rs[:, 1, cols], rs[:, 0, cols], ACT.Sqrt).then_inc(root_out.sem, 1)

            def xt_parts(tbs, banks, at):
                for i in range(2 * len(tbs)):
                    tb, h = tbs[i // 2], i % 2
                    act.wait_ge(xt_bank.sem, at(i + 1))
                    nc.scalar.copy(XTh[:, 4 * h:4 * h + 4, tb * P:(tb + 1) * P],
                                   bank[banks[i]][:].rearrange("p (k t) -> p k t", k=4)).then_inc(xt_high.sem, 1)

            act.dma_start(C[:], consts).then_inc(const_in, 16)
            act.dma_start(LNP[:], ln0.partition_broadcast(P)).then_inc(ln_in.sem, 16)
            root(1, slice(0, 2))
            xt_parts([0, 1], TURN_LOW, lambda n: n)
            root(2, slice(2, 4))

            with act.Fori(0, DEPTH) as l:
                xt_parts([2, 3], TURN_HIGH, lambda n: xt_bank.at(l, n))
                act.wait_ge(x_normed.sem, x_normed.at(l, 0))
                act.dma_start(LNP[:], ln1[l].partition_broadcast(P)).then_inc(ln_in.sem, 16)
                act.dma_start(QKG[:], qk_gain[l].partition_broadcast(P)).then_inc(par_in.sem, 16)
                act.dma_start(GB[:], gate_bias[l]).then_inc(par_in.sem, 16)
                for tb in range(TB):
                    act.wait_ge(used.sem, used.at(l, P_Q + 2))
                    nc.scalar.copy(qkv[:, tb, 0:S], bank[tb][:]).then_inc(q_copied.sem, 1)
                root(root_in.at(l, 1), slice(0, TB * HEADS))
                for c in range(GROUPS):
                    act.wait_ge(used.sem, used.at(l, P_XF + c // 2 + 1))
                    nc.scalar.copy(xfT[:, c, :], bank[XF_BANK[c]][:]).then_inc(xf_copied.sem, 1)
                for h in range(2):
                    act.wait_ge(used.sem, used.at(l, P_KV + 1))
                    nc.scalar.copy(qkv[:, 2 * h:2 * h + 2, S:QKV],
                                   bank[h][:].rearrange("p (t c) -> p t c", t=2)).then_inc(kv_copied.sem, 1)
                act.wait_ge(chan_done.sem, chan_done.at(l, 1))
                nc.scalar.copy(mid_h[0:1].rearrange("p g c -> p (g c)"), bank[CHAN_BANK[0]][0:1, :]
                               ).then_inc(chan_high.sem, 1)
                for g in range(GROUPS):
                    act.wait_ge(chan_done.sem, chan_done.at(l, g + 2))
                    nc.scalar.copy(Zh[:, g, :, :].rearrange("p a c -> p (a c)"), bank[CHAN_BANK[g + 1]][:]
                                   ).then_inc(chan_high.sem, 1)
                root(root_in.at(l, 2), slice(TB * HEADS, TB * NORMED))
                for g in range(GROUPS):
                    act.wait_ge(*y_ready(l, g))
                    nc.scalar.copy(sines[:, g, :], bank[SIN_BANK[g]][:, 0:HALF]).then_inc(sines_copied.sem, 1)
                for tb in range(TB):
                    act.wait_ge(q_roped.sem, q_roped.at(l, tb + 1))
                    nc.scalar.copy(q_split[:, tb, :, 0, :], qkv[:, tb, 0:S].rearrange("p (h d) -> p h d", d=HD)
                                   ).then_inc(qk_high.sem, 1)

                def fill_gates(u):
                    for i, (kind, m) in enumerate(FILL):
                        if FILL_UNIT[i] != u or kind == "wf":
                            continue
                        act.wait_ge(*filled(l, i))
                        dst, w, done = (Gf, 0, gatef) if kind == "gf" else (Ga, 1, gatea)
                        nc.scalar.activation(dst[:, m, :], bank[6 + i % 2][:], ACT.Sigmoid,
                                             bias=GB[:, w, m:m + 1]).then_inc(done.sem, 1)

                def stack_copy(i):
                    act.wait_ge(qk_turned.sem, qk_turned.at(l, i + 1))
                    dst = stacked(i)
                    nc.scalar.copy(dst, bank[i % 6][0:dst.shape[0], :]).then_inc(qk_copied.sem, 1)

                for i in range(HEADS):
                    stack_copy(i)
                act.wait_ge(par_in.sem, par_in.at(l, 32))
                fill_gates(-2)
                act.wait_ge(k_roped.sem, k_roped.at(l, TB))
                for copy in range(2):
                    ins = nc.scalar.copy(k_split[:, :, :, 1 + copy, :],
                                         qkv[:, :, HEADS * HD:NORMED * HD].rearrange("p t (g d) -> p t g d", d=HD))
                ins.then_inc(qk_high.sem, 1)
                for i in range(HEADS, HEADS + 4):
                    stack_copy(i)

                def p_copy(u):
                    h, tb = u // TB, u % TB
                    act.wait_ge(p_turned.sem, p_turned.at(l, u + 1))
                    if h >= 2:
                        act.wait_ge(pv_done.sem, pv_done.at(l, h - 1))
                    nc.scalar.copy(PT[:, h % 2, :, tb * P:(tb + 1) * P],
                                   bank[2 + u % 2][:].rearrange("p (s t) -> p s t", s=TB)).then_inc(p_copied.sem, 1)

                def o_copy(h):
                    g, j = h // PAIRS, h % PAIRS
                    act.wait_ge(pv_done.sem, pv_done.at(l, h + 1))
                    nc.scalar.copy(oTh[g * HD:(g + 1) * HD, j, :],
                                   bank[4 + h % 2][g * HD:(g + 1) * HD, :]).then_inc(o_high.sem, 1)

                fill_gates(-1)
                for u in range(32):
                    act.wait_ge(max_ready.sem, max_ready.at(l, u + 1))
                    if u >= 2:
                        act.wait_ge(p_turned.sem, p_turned.at(l, u - 1))
                    nc.scalar.activation(prob[:, u % 2, :], bank[u % 2][:], ACT.Exp, bias=att[:, 1, u:u + 1],
                                         scale=SCALE, accum_out=att[:, 2, u:u + 1]).then_inc(exped.sem, 1)
                    if u >= 1:
                        fill_gates(u - 1)
                        p_copy(u - 1)
                    if u in Y_UNITS:
                        g = Y_UNITS.index(u)
                        act.wait_ge(y_summed.sem, y_summed.at(l, g + 1))
                        nc.scalar.copy(yTh[:, g, :], yf[:, g, :]).then_inc(y_high.sem, 1)
                    if u % TB == 2 and u > TB:
                        o_copy(u // TB - 1)
                p_copy(31)
                o_copy(HEADS - 1)
                fill_gates(31)
                for m in range(KD):
                    act.wait_ge(mixed.sem, mixed.at(l, m + 1))
                    nc.scalar.copy(XTh[:, m, :], Gf[:, m, :]).then_inc(mixed_high.sem, 1)
                act.dma_start(keyT[:], keys[l]).then_inc(key_in.sem, 16)
                root(root_in.at(l, 3), slice(0, 2))
                xt_parts([0, 1], [4, 5, 6, 7], lambda n: xt_bank.at(l, TB + n))
                root(root_in.at(l, 4), slice(2, 4))
                xt_parts([2, 3], [4, 5, 6, 7], lambda n: xt_bank.at(l, 2 * TB + n))

                act.wait_ge(x_normed.sem, x_normed.at(l, TB))
                act.dma_start(LNP[:], ln2[l].partition_broadcast(P)).then_inc(ln_in.sem, 16)

                def ks_copy(h):
                    act.wait_ge(key_scored.sem, key_scored.at(l, h + 1))
                    if h >= 2:
                        act.wait_ge(head_cut.sem, head_cut.at(l, h - 1))
                    for f in range(2):
                        ins = nc.scalar.copy(ks[:, h % 2, f, :, :].rearrange("p t k -> p (t k)"),
                                             bank[4 + 2 * (h % 2) + f][:])
                    ins.then_inc(ks_copied.sem, 1)

                for h in range(RH):
                    act.wait_ge(used.sem, used.at(l, P_QUERY + h + 1))
                    if h >= 2:
                        act.wait_ge(key_scored.sem, key_scored.at(l, h - 1))
                    for f in range(2):
                        ins = nc.scalar.copy(qrT[:, h % 2, f, :], bank[2 * (h % 2) + f][:])
                    ins.then_inc(qr_copied.sem, 1)
                    if h >= 1:
                        ks_copy(h - 1)

                def early_gelu(n, ready, reuse):
                    slot = reuse[1]
                    act.wait_ge(*ready)
                    if reuse[0] is not None:
                        act.wait_ge(early_saved[slot].sem, reuse[0])
                    nc.scalar.activation(early[:, slot, :], bank[slot][:], ACT.Gelu).then_inc(early_out.sem, 1)
                    act.wait_ge(early_out.sem, early_out.at(l, n + 1))
                    act.dma_start(early_acts[n], early[:, slot, :]).then_inc(early_saved[slot].sem, 16)

                def early_piece(i, base, first, chunks=range(2)):
                    for c in chunks:
                        slot = (2 * i + c) % 4
                        n = 2 * base + (2 * i + c)
                        ready = ((early_first.sem, early_first.at(l, base + (i + 1))) if c == 0
                                 else (used.sem, used.at(l, base + (P_TAB + i + 1))))
                        left = None if first and 2 * i + c < 4 else early_saved[slot].at(
                            l, 8 * base + 16 * ((2 * i + c) // 4))
                        early_gelu(n, ready, (left, slot))

                for i in range(E_BEFORE - 1):
                    if i == E_EXP:
                        act.wait_ge(sv_shifted.sem, sv_shifted.at(l, 1))
                        nc.scalar.activation(route[:, :, 2, :], sv[:].rearrange("p t h k -> p t (h k)"),
                                             ACT.Exp).then_inc(sv_exped.sem, 1)
                    early_piece(i, 0, True)
                    if i == 0:
                        ks_copy(RH - 1)
                early_piece(E_BEFORE - 1, 0, True, [0])
                for tb in range(TB):
                    act.wait_ge(route_turned.sem, route_turned.at(l, tb + 1))
                    ts = slice(tb * P, (tb + 1) * P)
                    nc.scalar.copy(routeT[:, :, ts], bank[4 + tb][:, 0:3 * P].rearrange("p (a t) -> p a t", a=3)
                                   ).then_inc(route_copied.sem, 1)
                    nc.scalar.copy(idx16[:, :, ts], bank[4 + tb][:, 0:2 * P].rearrange("p (a t) -> p a t", a=2))
                    nc.scalar.activation(wth[:, ts], bank[4 + tb][:, 2 * P:3 * P], ACT.Copy,
                                         scale=GATE_SCALE).then_inc(w_split.sem, 1)
                early_piece(E_BEFORE - 1, 0, True, [1])

                def gate_block(b, first):
                    for k in range(2):
                        if not first:
                            act.wait_ge(spilled[k].sem, spilled[k].at(l, 16 * b))
                        for q in range(8):
                            act.wait_ge(gated.sem, gated.at(l, 16 * b + (8 * k + q + 1)))
                            dst = spill[:, k, :, 4 * q:4 * q + 4, :].rearrange("p g t j -> p t g j")
                            nc.scalar.activation(dst, bank[4 + q % 4][:].rearrange("p (t g j) -> p t g j", t=4, j=CG),
                                                 ACT.Copy, scale=1.0 / GATE_SCALE).then_inc(gate_copied.sem, 1)
                            if q % 4 == 3:
                                early_half(b, 2 * k + q // 4)
                        act.wait_ge(gate_copied.sem, gate_copied.at(l, 16 * b + 8 * (k + 1)))
                        dd = dense.rearrange("g p (b t) j -> b p g (t j)", t=32)
                        act.dma_start(dd[2 * b + k], spill[:, k, :, :, :].rearrange("p g t j -> p g (t j)")
                                      ).then_inc(spilled[k].sem, 16)

                def early_half(b, c):
                    slot = (2 * E_BEFORE + c) % 4
                    piece = E_BEFORE + c // 2
                    ready = ((early_first.sem, early_first.at(l, 2 * b + (piece + 1))) if c % 2 == 0
                             else (used.sem, used.at(l, 2 * b + (P_TAB + piece + 1))))
                    left = early_saved[slot].at(l, 16 * b + 16 * ((2 * E_BEFORE + c) // 4))
                    early_gelu(4 * b + (2 * E_BEFORE + c), ready, (left, slot))

                gate_block(0, True)
                with act.Fori(1, S // 64) as b:
                    gate_block(b, False)
                for k in range(2):
                    act.wait_ge(spilled[k].sem, spilled[k].at(l, 16 * (S // 64)))
                for k in range(2):
                    act.dma_start(gate[k][:], dense[k]).then_inc(gate_in[k].sem, 16)
                    act.dma_start(acts_in[k][:], early_acts[CG * k:CG * (k + 1)].rearrange("c p t -> p c t")
                                  ).then_inc(acts_back[k].sem, 16)
                for i in range(E_AFTER - 1):
                    early_piece(E_BEFORE + E_WITHIN + i, 0, True)

                def w_highs(g, par, half):
                    for c in (2 * half, 2 * half + 1):
                        act.wait_ge(w_full.sem, w_full.at(l, CG * g + (c + 1)))
                        nc.scalar.copy(Wh[:, par, c, :], Wf[:, c % 2, :]).then_inc(w_high.sem, 1)

                def activate(g, half):
                    for c in (2 * half, 2 * half + 1):
                        if c % 2 == 0:
                            act.wait_ge(u_first.sem, u_first.at(l, 2 * g + (half + 1 - 2 * EG)))
                        else:
                            act.wait_ge(used.sem, used.at(l, 4 * g + (P_TAB - 1 + 2 * half)))
                        act.wait_ge(w_full.sem, w_full.at(l, CG * g + (c - 1)))
                        nc.scalar.activation(acts[:, c % 2, :], bank[c][:], ACT.Gelu).then_inc(act_out.sem, 1)

                def fetch(g, par, acts_too):
                    act.dma_start(gate[par][:], dense[g]).then_inc(gate_in[par].sem, 16)
                    if acts_too:
                        act.dma_start(acts_in[par][:], early_acts[bass.ds(g * CG, CG)].rearrange("c p t -> p c t")
                                      ).then_inc(acts_back[par].sem, 16)

                def act_group(g, par, early_group, fetch_next, slot_used):
                    if slot_used is not None:
                        act.wait_ge(used.sem, used.at(l, slot_used))
                    for half in range(2):
                        if not early_group:
                            activate(g, half)
                        w_highs(g, par, half)
                    if fetch_next:
                        fetch(g + 2, par, fetch_next == "acts too")

                act_group(0, 0, True, None, None)
                early_piece(2 * EG - 1, 0, True)
                for slot in range(4):
                    act.wait_ge(early_saved[slot].sem, early_saved[slot].at(l, 16 * EG))
                fetch(2, 0, True)
                act_group(1, 1, True, "acts too", None)
                with act.Fori(1, EG // 2 - 1) as m:
                    for par in range(2):
                        act_group(2 * m + par, par, True, "acts too", 4 * m + (2 * par + P_VA - 2))
                for par in range(2):
                    act_group(EG - 2 + par, par, True, "gates", 2 * (EG - 2 + par) + P_VA - 2)
                with act.Fori(EG // 2, NG // 2 - 1) as m:
                    for par in range(2):
                        act_group(2 * m + par, par, False, "gates", 8 * m + (4 * par + P_TAB - 2))
                for par in range(2):
                    act_group(NG - 2 + par, par, False, None, 4 * (NG - 2 + par) + P_TAB - 2)
                root(root_in.at(l, 5), slice(0, 2))
                xt_parts([0, 1], TURN_LOW, lambda n: xt_bank.at(l, 3 * TB + n))
                root(root_in.at(l, 6), slice(2, 4))

        @block.vector
        def _(dve):
            def inv_root(ch, n_out, cols):
                v, r0 = rs[:, 2, cols], rs[:, 1, cols]
                a, r = rs[:, 0, cols], rs[:, 3, cols]
                nc.vector.reciprocal(a, v).then_inc(root_in.sem, 1)
                dve.wait_ge(root_out.sem, n_out)
                ch.link(nc.vector.tensor_tensor(a, r0, r0, ALU.mult))
                ch.link(nc.vector.tensor_tensor(a, a, v, ALU.mult))
                ch.link(nc.vector.tensor_scalar(a, a, -0.5, 1.5, ALU.mult, ALU.add))
                ch.link(nc.vector.tensor_tensor(r, r0, a, ALU.mult))

            def half_stats(ch, tb, h):
                ch.mark(nc.vector.bn_stats(stats[:, tb, h, :], X[:, tb, h * S:(h + 1) * S]))

            def layer_norm(ch, pair, n_root, n_par):
                ch.wait()
                cols = slice(2 * pair, 2 * pair + 2)
                for tb in (2 * pair, 2 * pair + 1):
                    ch.mark(nc.vector.bn_aggr(mv[:, tb, :], stats[:, tb, :, :].rearrange("p a b -> p (a b)")))
                ch.wait()
                ch.link(nc.vector.tensor_scalar(rs[:, 2, cols], mv[:, cols, 1], LN_EPS, None, ALU.add))
                inv_root(ch, n_root, cols)
                dve.wait_ge(ln_in.sem, n_par)
                for tb in (2 * pair, 2 * pair + 1):
                    xb = X[:, tb, :]
                    ch.link(nc.vector.scalar_tensor_tensor(out=xb, in0=xb, scalar=mv[:, tb, 0:1], in1=LNP[:, 0, :],
                                                           op0=ALU.subtract, op1=ALU.mult))
                    nc.vector.scalar_tensor_tensor(out=xb, in0=xb, scalar=rs[:, 3, tb:tb + 1], in1=LNP[:, 1, :],
                                                   op0=ALU.mult, op1=ALU.add).then_inc(x_normed.sem, 1)

            def low_parts(tbs, banks, at):
                for i in range(2 * len(tbs)):
                    tb, h = tbs[i // 2], i % 2
                    dve.wait_ge(xt_high.sem, at(i + 1))
                    part = XTh[:, 4 * h:4 * h + 4, tb * P:(tb + 1) * P].bitcast(F32)
                    nc.vector.tensor_tensor(XTl[:, 4 * h:4 * h + 4, tb * P:(tb + 1) * P],
                                            bank[banks[i]][:].rearrange("p (k t) -> p k t", k=4),
                                            part, ALU.subtract).then_inc(xt_low.sem, 1)

            pre = Chain(dve, dve_step, 0)
            for pair in range(2):
                for tb in (2 * pair, 2 * pair + 1):
                    dve.wait_ge(x_in[tb], 16)
                    half_stats(pre, tb, 0)
                    half_stats(pre, tb, 1)
                layer_norm(pre, pair, pair + 1, 16)
                if pair == 0:
                    low_parts([0, 1], TURN_LOW, lambda n: n)
            dve.wait_ge(const_in, 16)
            pre.link(nc.vector.tensor_copy(iota4[:], iota.unsqueeze(2).broadcast_to([P, KEYS, 4])))

            with dve.Fori(0, DEPTH) as l:
                dve.sem_clear(dve_step)
                ch = Chain(dve, dve_step, 0)
                low_parts([2, 3], TURN_HIGH, lambda n: xt_high.at(l, n))
                def norm_heads(a, b, first, copied, n_root):
                    n = b - a
                    for tb in range(TB):
                        dve.wait_ge(*copied(tb))
                        part, sq = qkv[:, tb, a * HD:b * HD], turn[:, 0, a * HD:b * HD]
                        ch.link(nc.vector.tensor_tensor(sq, part, part, ALU.mult))
                        ch.link(nc.vector.tensor_reduce(rs[:, 2, first + tb * n:first + (tb + 1) * n],
                                                        sq.rearrange("p (h d) -> p h d", d=HD), AX_X, ALU.add))
                    cols = slice(first, first + TB * n)
                    ch.link(nc.vector.tensor_scalar(rs[:, 2, cols], rs[:, 2, cols], 1.0 / HD, RMS_EPS, ALU.mult,
                                                    ALU.add))
                    inv_root(ch, n_root, cols)

                def rope(tb, a, b, first, w, done):
                    n = b - a
                    flat = qkv[:, tb, a * HD:b * HD]
                    part = flat.rearrange("p (h d) -> p h d", d=HD)
                    halves = flat.rearrange("p (h r c d) -> p h r c d", h=n, r=2, c=2)
                    straight, crossed = turn[:, 0, a * HD:b * HD], turn[:, 1, a * HD:b * HD]
                    crossed5 = crossed.rearrange("p (h r c d) -> p h r c d", h=n, r=2, c=2)
                    s5 = sin[:, tb, :].rearrange("p (r c d) -> p r c d", r=2, c=2)
                    r = rs[:, 3, first + tb * n:first + (tb + 1) * n].unsqueeze(2).broadcast_to([P, n, HD])
                    ch.link(nc.vector.tensor_tensor(part, part, r, ALU.mult))
                    ch.link(nc.vector.tensor_tensor(part, part, QKG[:, w, :].unsqueeze(1).broadcast_to([P, n, HD]),
                                                    ALU.mult))
                    ch.mark(nc.vector.tensor_tensor(straight.rearrange("p (h d) -> p h d", d=HD), part,
                                                    cos[:, tb, :].unsqueeze(1).broadcast_to([P, n, HD]), ALU.mult))
                    for c in range(2):
                        ch.mark(nc.vector.tensor_tensor(
                            crossed5[:, :, :, c, :], halves[:, :, :, 1 - c, :],
                            s5[:, :, c, :].unsqueeze(1).broadcast_to([P, n, 2, HD // 4]), ALU.mult))
                    ch.wait()
                    nc.vector.tensor_tensor(flat, straight, crossed, ALU.add).then_inc(done.sem, 1)
                    dve.wait_ge(done.sem, done.at(l, tb + 1))

                norm_heads(0, HEADS, 0, lambda tb: (q_copied.sem, q_copied.at(l, tb + 1)), root_out.at(l, 1))
                dve.wait_ge(par_in.sem, par_in.at(l, 32))
                for tb in range(TB):
                    rope(tb, 0, HEADS, 0, 0, q_roped)
                for g in range(GROUPS):
                    dve.wait_ge(xf_copied.sem, xf_copied.at(l, g + 1))
                    nc.vector.tensor_tensor(even_odd[:, g, 1, :], xfT[:, g, 0:HALF], xfT[:, g, HALF:S], ALU.subtract)
                    nc.vector.tensor_tensor(even_odd[:, g, 0, 1:HALF], xfT[:, g, 1:HALF], xfT[:, g, HALF + 1:S], ALU.add)
                    nc.vector.tensor_copy(even_odd[:, g, 0, 0:1], xfT[:, g, 0:1]).then_inc(folded.sem, 1)
                dve.wait_ge(chan_high.sem, chan_high.at(l, 1))
                nc.vector.tensor_tensor(mid_l[0:1].rearrange("p g c -> p (g c)"), bank[CHAN_BANK[0]][0:1, :],
                                        mid_h[0:1].rearrange("p g c -> p (g c)").bitcast(F32),
                                        ALU.subtract).then_inc(chan_low.sem, 1)
                for g in range(GROUPS):
                    dve.wait_ge(chan_high.sem, chan_high.at(l, g + 2))
                    nc.vector.tensor_tensor(Zl[:, g, :, :].rearrange("p a c -> p (a c)"), bank[CHAN_BANK[g + 1]][:],
                                            Zh[:, g, :, :].rearrange("p a c -> p (a c)").bitcast(F32),
                                            ALU.subtract).then_inc(chan_low.sem, 1)
                norm_heads(HEADS, NORMED, TB * HEADS, lambda tb: (kv_copied.sem, kv_copied.at(l, tb // 2 + 1)),
                           root_out.at(l, 2))
                for g in range(GROUPS):
                    if g == GROUPS - 1:
                        rope(0, HEADS, NORMED, TB * HEADS, 1, k_roped)
                    dve.wait_ge(*y_ready(l, g))
                    dve.wait_ge(sines_copied.sem, sines_copied.at(l, g + 1))
                    yc, ys = bank[COS_BANK[g]], sines[:, g, :]
                    nc.vector.tensor_tensor(yf[:, g, 0:HALF], yc[:, 0:HALF], ys[:, 0:HALF], ALU.subtract)
                    nc.vector.tensor_tensor(yf[:, g, HALF + 1:S], yc[:, 1:HALF], ys[:, 1:HALF], ALU.add)
                    nc.vector.tensor_copy(yf[:, g, HALF:HALF + 1], yc[:, HALF:HALF + 1]).then_inc(y_summed.sem, 1)
                for tb in range(TB):
                    dve.wait_ge(qk_high.sem, qk_high.at(l, tb + 1))
                    nc.vector.tensor_tensor(q_split[:, tb, :, 1, :],
                                            qkv[:, tb, 0:S].rearrange("p (h d) -> p h d", d=HD),
                                            q_split[:, tb, :, 0, :].bitcast(F32), ALU.subtract).then_inc(qk_low.sem, 1)
                for tb in range(1, TB):
                    rope(tb, HEADS, NORMED, TB * HEADS, 1, k_roped)
                dve.wait_ge(qk_high.sem, qk_high.at(l, TB + 1))
                nc.vector.tensor_tensor(k_split[:, :, :, 0, :],
                                        qkv[:, :, HEADS * HD:NORMED * HD].rearrange("p t (g d) -> p t g d", d=HD),
                                        k_split[:, :, :, 1, :].bitcast(F32), ALU.subtract).then_inc(qk_low.sem, 1)

                def row_max(u):
                    dve.wait_ge(scored.sem, scored.at(l, u + 1))
                    ch.link(nc.vector.tensor_reduce(att[:, 0, u:u + 1], bank[u % 2][:], AX_X, ALU.max))
                    nc.vector.tensor_scalar(att[:, 1, u:u + 1], att[:, 0, u:u + 1], -SCALE, None,
                                            ALU.mult).then_inc(max_ready.sem, 1)

                def o_rest(h):
                    g, j = h // PAIRS, h % PAIRS
                    rows = slice(g * HD, (g + 1) * HD)
                    dve.wait_ge(o_high.sem, o_high.at(l, h + 1))
                    nc.vector.tensor_tensor(oTl[rows, j, :], bank[4 + h % 2][rows, :], oTh[rows, j, :].bitcast(F32),
                                            ALU.subtract).then_inc(o_low.sem, 1)

                def fill_products(u):
                    for i, (kind, m) in enumerate(FILL):
                        if kind != "wf" or FILL_UNIT[i] != u:
                            continue
                        dve.wait_ge(gatef.sem, gatef.at(l, m + 1))
                        dve.wait_ge(*filled(l, i))
                        nc.vector.tensor_tensor(Gf[:, m, :], Gf[:, m, :], bank[6 + i % 2][:],
                                                ALU.mult).then_inc(yf_gated.sem, 1)

                row_max(0)
                for u in range(32):
                    if u >= 1:
                        fill_products(u - 1)
                    if u + 1 < 32:
                        row_max(u + 1)
                    dve.wait_ge(exped.sem, exped.at(l, u + 1))
                    ch.link(nc.vector.reciprocal(attr[:, u:u + 1], att[:, 2, u:u + 1]))
                    nc.vector.tensor_scalar(prob[:, u % 2, :], prob[:, u % 2, :], attr[:, u:u + 1], None,
                                            ALU.mult).then_inc(prob_ready.sem, 1)
                    if u in Y_UNITS:
                        g = Y_UNITS.index(u)
                        dve.wait_ge(y_high.sem, y_high.at(l, g + 1))
                        nc.vector.tensor_tensor(yTl[:, g, :], yf[:, g, :], yTh[:, g, :].bitcast(F32),
                                                ALU.subtract).then_inc(y_low.sem, 1)
                    if u % TB == 3 and u > TB:
                        o_rest(u // TB - 1)
                o_rest(HEADS - 1)
                fill_products(31)

                dve.wait_ge(yf_gated.sem, yf_gated.at(l, KD))
                for m in range(KD):
                    dve.wait_ge(gatea.sem, gatea.at(l, m + 1))
                    dve.wait_ge(*wa_ready(l, m))
                    nc.vector.tensor_tensor(Ga[:, m, :], Ga[:, m, :], bank[m % 4][:],
                                            ALU.mult).then_inc(ya_gated.sem, 1)
                    dve.wait_ge(ya_gated.sem, ya_gated.at(l, m + 1))
                    nc.vector.tensor_tensor(Gf[:, m, :], Gf[:, m, :], Ga[:, m, :], ALU.add).then_inc(mixed.sem, 1)
                    if m >= 1:
                        dve.wait_ge(mixed_high.sem, mixed_high.at(l, m))
                        nc.vector.tensor_tensor(XTl[:, m - 1, :], Gf[:, m - 1, :], XTh[:, m - 1, :].bitcast(F32),
                                                ALU.subtract).then_inc(mixed_low.sem, 1)
                dve.wait_ge(mixed_high.sem, mixed_high.at(l, KD))
                nc.vector.tensor_tensor(XTl[:, KD - 1, :], Gf[:, KD - 1, :], XTh[:, KD - 1, :].bitcast(F32),
                                        ALU.subtract).then_inc(mixed_low.sem, 1)
                for q in range(2):
                    dve.wait_ge(used.sem, used.at(l, P_OUT + q + 1))
                    for b in range(2):
                        xs = X[:, 2 * b:2 * b + 2, q * 256:(q + 1) * 256]
                        nc.vector.scalar_tensor_tensor(
                            out=xs, in0=xs, scalar=ALPHA,
                            in1=bank[4 + 2 * q + b][:].rearrange("p (t c) -> p t c", t=2),
                            op0=ALU.mult, op1=ALU.add).then_inc(resid.sem, 1)
                dve.wait_ge(resid.sem, resid.at(l, 4))
                for tb in range(TB):
                    half_stats(ch, tb, 0)
                for pair in range(2):
                    for tb in (2 * pair, 2 * pair + 1):
                        dve.wait_ge(*rows_ready(l, 0, tb, P_OUT + 4))
                        xs = X[:, tb, S:D]
                        nc.vector.scalar_tensor_tensor(out=xs, in0=xs, scalar=ALPHA, in1=bank[tb][:],
                                                       op0=ALU.mult, op1=ALU.add).then_inc(resid.sem, 1)
                        dve.wait_ge(resid.sem, resid.at(l, 4 + tb + 1))
                        half_stats(ch, tb, 1)
                    layer_norm(ch, pair, root_out.at(l, 3 + pair), ln_in.at(l, 16))
                    low_parts([2 * pair, 2 * pair + 1], [4, 5, 6, 7], lambda n: xt_high.at(l, TB + TB * pair + n))

                def best(width, scores, vals, idx):
                    n0 = ch.n
                    for half in (0, 8):
                        for tb in range(TB):
                            ch.wait(ch.n - (TB - 1) if ch.n - n0 >= TB else n0)
                            ch.mark(nc.vector.max(vals(tb)[:, half:half + 8], scores(tb)))
                        for tb in range(TB):
                            ch.wait(ch.n - (TB - 1))
                            ch.mark(nc.vector.max_index(idx(tb)[:, half:half + 8], vals(tb)[:, half:half + 8],
                                                        scores(tb)))
                        if half == 0:
                            for tb in range(TB):
                                ch.wait(ch.n - (TB - 1))
                                ch.mark(nc.vector.match_replace(scores(tb), vals(tb)[:, 0:8], scores(tb), LOWEST))

                for h in range(RH):
                    dve.wait_ge(ks_copied.sem, ks_copied.at(l, h + 1))
                    dve.sem_inc(went_on, 1)
                    for f in range(2):
                        best(KEYS, lambda tb: ks[:, h % 2, f, tb, :], lambda tb: kv_[:, tb, h, f, :],
                             lambda tb: ki[:, tb, h, f, :])
                    ch.wait()
                    a = kv_[:, :, h, 0, :].unsqueeze(3).broadcast_to([P, TB, TOPK, TOPK])
                    b = kv_[:, :, h, 1, :].unsqueeze(2).broadcast_to([P, TB, TOPK, TOPK])
                    nc.vector.tensor_tensor(cand[:].rearrange("p t (a b) -> p t a b", a=TOPK), a, b,
                                            ALU.add).then_inc(head_cut.sem, 1)
                    dve.wait_ge(head_cut.sem, head_cut.at(l, h + 1))
                    dve.sem_inc(went_on, 1)
                    best(TOPK * TOPK, lambda tb: cand[:, tb, :], lambda tb: sv[:, tb, h, :],
                         lambda tb: pos[:, tb, h, :])
                ch.wait()
                s3 = sv[:].rearrange("p t h k -> p (t h) k")
                ch.link(nc.vector.tensor_copy(gsum[:, 0, :].unsqueeze(2), s3[:, :, 0:1]))
                nc.vector.tensor_tensor(s3, s3, gsum[:, 0, :].unsqueeze(2).broadcast_to([P, TB * RH, TOPK]),
                                        ALU.subtract).then_inc(sv_shifted.sem, 1)
                p2 = pos[:].rearrange("p t h k -> p t (h k)")
                ch.mark(nc.vector.tensor_scalar(pab[:, 0, :, :], p2, 4, None, ALU.logical_shift_right))
                ch.mark(nc.vector.tensor_scalar(pab[:, 1, :, :], p2, TOPK - 1, None, ALU.bitwise_and))
                ch.mark(nc.vector.tensor_copy(kf[:].rearrange("p t h f k -> p (t h f k)"),
                                              ki[:].rearrange("p t h f k -> p (t h f k)")))
                ch.wait()
                ch.link(nc.vector.tensor_copy(paf[:].rearrange("p f t k -> p (f t k)"),
                                              pab[:].rearrange("p f t k -> p (f t k)")))
                for tb in range(TB):
                    for f in range(2):
                        eq = pick[:].rearrange("p h k a -> p (h k) a")
                        ch.link(nc.vector.tensor_tensor(
                            eq, paf[:, f, tb, :].unsqueeze(2).broadcast_to([P, RH * TOPK, TOPK]),
                            iota[:, 0:TOPK].unsqueeze(1).broadcast_to([P, RH * TOPK, TOPK]), ALU.is_equal))
                        ch.link(nc.vector.tensor_tensor(
                            pick[:], pick[:], kf[:, tb, :, f, :].unsqueeze(2).broadcast_to([P, RH, TOPK, TOPK]),
                            ALU.mult))
                        ch.link(nc.vector.tensor_reduce(route[:, tb, f, :], eq, AX_X, ALU.add))
                dve.wait_ge(sv_exped.sem, sv_exped.at(l, 1))
                for tb in range(TB):
                    hs = slice(tb * RH, (tb + 1) * RH)
                    ch.mark(nc.vector.tensor_reduce(gsum[:, 1, hs], route[:, tb, 2, :].rearrange(
                        "p (h k) -> p h k", h=RH), AX_X, ALU.add))
                ch.wait()
                ch.link(nc.vector.reciprocal(gsum[:, 2, :], gsum[:, 1, :]))
                for tb in range(TB):
                    e = route[:, tb, 2, :].rearrange("p (h k) -> p h k", h=RH)
                    rc = gsum[:, 2, tb * RH:(tb + 1) * RH].unsqueeze(2).broadcast_to([P, RH, TOPK])
                    nc.vector.tensor_tensor(e, e, rc, ALU.mult).then_inc(routed.sem, 1)

                for tb in range(TB):
                    dve.wait_ge(route_copied.sem, route_copied.at(l, tb + 1))
                    dve.wait_ge(w_split.sem, w_split.at(l, tb + 1))
                    ts = slice(tb * P, (tb + 1) * P)
                    nc.vector.scalar_tensor_tensor(out=wtl[:, ts], in0=routeT[:, 2, ts], scalar=GATE_SCALE,
                                                   in1=wth[:, ts], op0=ALU.mult, op1=ALU.subtract
                                                   ).then_inc(w_rest.sem, 1)

                def hot_rows(b, first):
                    for q in range(8):
                        slot = q % 2
                        if not (first and q < 2):
                            dve.wait_ge(gated.sem, gated.at(l, 16 * b + (2 * q - 2)))

                        def spread(x):
                            return x[:, bass.ds(64 * b + 8 * q, 8)].rearrange("p (n t) -> p n t", t=4).unsqueeze(
                                2).broadcast_to([P, 2, KEYS, 4])
                        keys4 = iota4[:].unsqueeze(1).broadcast_to([P, 2, KEYS, 4])
                        nc.vector.tensor_tensor(hot1[:, slot], keys4, spread(idx16[:, 0, :]), ALU.is_equal)
                        nc.vector.tensor_tensor(hot2[:, slot], keys4, spread(idx16[:, 1, :]),
                                                ALU.is_equal).then_inc(hot2_done.sem, 1)
                        dve.wait_ge(hot2_done.sem, hot2_done.at(l, 8 * b + (q + 1)))
                        nc.vector.tensor_tensor(hot2h[:, slot], hot2[:, slot], spread(wth), ALU.mult)
                        nc.vector.tensor_tensor(hot2l[:, slot], hot2[:, slot], spread(wtl), ALU.mult).then_inc(hots.sem, 1)

                dve.wait_ge(w_rest.sem, w_rest.at(l, TB))
                dve.sem_inc(went_on, 1)
                hot_rows(0, True)
                with dve.Fori(1, S // 64) as b:
                    hot_rows(b, False)

                dve.wait_ge(spilled[0].sem, spilled[0].at(l, 16 * (S // 64)))
                dve.wait_ge(spilled[1].sem, spilled[1].at(l, 16 * (S // 64)))
                dve.wait_ge(gated.sem, gated.at(l, S // 4))

                def weigh(g, par, half, early_group, first):
                    for c in (2 * half, 2 * half + 1):
                        if not early_group:
                            dve.wait_ge(act_out.sem, act_out.at(l, CG * g + (c + 1 - CG * EG)))
                        if not (first and c < 2):
                            dve.wait_ge(w_high.sem, w_high.at(l, CG * g + (c - 1)))
                            dve.wait_ge(w_low.sem, w_low.at(l, CG * g + (c - 1)))
                        a = acts_in[par][:, c, :] if early_group else acts[:, c % 2, :]
                        nc.vector.tensor_tensor(Wf[:, c % 2, :], a, gate[par][:, :, c],
                                                ALU.mult).then_inc(w_full.sem, 1)
                    for c in (2 * half, 2 * half + 1):
                        dve.wait_ge(w_high.sem, w_high.at(l, CG * g + (c + 1)))
                        nc.vector.tensor_tensor(Wl[:, par, c, :], Wf[:, c % 2, :], Wh[:, par, c, :].bitcast(F32),
                                                ALU.subtract).then_inc(w_low.sem, 1)

                def add_up(g, half, piece_done, first):
                    for s in range(2):
                        if s == 0:
                            dve.wait_ge(v_first.sem, v_first.at(l, 2 * g + (half + 1)))
                        else:
                            dve.wait_ge(used.sem, used.at(l, piece_done))
                        for j in range(2):
                            xs = X[:, 2 * s + j, half * S:(half + 1) * S]
                            new = bank[4 + 2 * s + j][:]
                            if first:
                                ins = nc.vector.scalar_tensor_tensor(out=xs, in0=xs, scalar=ALPHA, in1=new,
                                                                     op0=ALU.mult, op1=ALU.add)
                            else:
                                ins = nc.vector.tensor_tensor(xs, xs, new, ALU.add)
                        ins.then_inc(y_added.sem, 1)

                def dve_group(g, par, early_group, slot_used, v_done):
                    dve.wait_ge(gate_in[par].sem, gate_in[par].at(l, 8 * g + 16 - 8 * par))
                    if early_group:
                        dve.wait_ge(acts_back[par].sem, acts_back[par].at(l, 8 * g + 16 - 8 * par))
                    if slot_used is not None:
                        dve.wait_ge(used.sem, used.at(l, slot_used))
                    weigh(g, par, 0, early_group, False)
                    if slot_used is not None:
                        dve.wait_ge(y_added.sem, y_added.at(l, 4 * g - 4))
                    add_up(g - 1, 0, v_done(0), slot_used is None)
                    weigh(g, par, 1, early_group, False)
                    add_up(g - 1, 1, v_done(1), slot_used is None)

                dve.wait_ge(gate_in[0].sem, gate_in[0].at(l, 16))
                dve.wait_ge(acts_back[0].sem, acts_back[0].at(l, 16))
                weigh(0, 0, 0, True, True)
                weigh(0, 0, 1, True, False)
                dve_group(1, 1, True, None, lambda half: P_VA + half + 1)
                with dve.Fori(1, EG // 2) as m:
                    for par in range(2):
                        dve_group(2 * m + par, par, True, 4 * m + (2 * par + P_VA - 2),
                                  lambda half: 4 * m + (2 * par + P_VA - 1 + half))
                with dve.Fori(EG // 2, NG // 2) as m:
                    for par in range(2):
                        dve_group(2 * m + par, par, False, 8 * m + (4 * par + P_TAB - 2),
                                  lambda half: 8 * m + (4 * par + P_TAB + 2 * half))
                dve.wait_ge(y_added.sem, y_added.at(l, 4 * NG - 4))
                for pair in range(2):
                    for tb in (2 * pair, 2 * pair + 1):
                        dve.wait_ge(*rows_ready(l, 1, tb, NP))
                        for h in range(2):
                            xs = X[:, tb, h * S:(h + 1) * S]
                            ins = nc.vector.tensor_tensor(xs, xs, bank[2 * tb + h][:], ALU.add)
                        ins.then_inc(y_resid.sem, 1)
                        dve.wait_ge(y_resid.sem, y_resid.at(l, tb + 1))
                        half_stats(ch, tb, 0)
                        half_stats(ch, tb, 1)
                    layer_norm(ch, pair, root_out.at(l, 5 + pair), ln_in.at(l, 32))
                    if pair == 0:
                        low_parts([0, 1], TURN_LOW, lambda n: xt_high.at(l, 3 * TB + n))

        @block.tensor
        def _(pe):
            def product(dst, sth, stl, mvh, mvl, first, last):
                nc.tensor.matmul(dst, sth, mvh, start=first, stop=False)
                nc.tensor.matmul(dst, sth, mvl, start=False, stop=False)
                return nc.tensor.matmul(dst, stl, mvh, start=False, stop=last)

            def turn_x(tbs, banks, normed, low=None):
                for i in range(2 * len(tbs)):
                    tb, h = tbs[i // 2], i % 2
                    if h == 0:
                        pe.wait_ge(x_normed.sem, normed(tb + 1))
                    if low is not None:
                        pe.wait_ge(xt_low.sem, low(i))
                    for k in range(4):
                        c = 4 * h + k
                        ins = nc.tensor.transpose(bank[banks[i]][:, k * P:(k + 1) * P],
                                                  X[:, tb, c * P:(c + 1) * P], ident)
                    ins.then_inc(xt_bank.sem, 1)

            pe.wait_ge(const_in, 16)
            turn_x([0, 1], TURN_LOW, lambda n: n)

            with pe.Fori(0, DEPTH) as l:
                def piece(n, slot, half=0):
                    pe.wait_ge(split.sem, split.at(l, 2 * n + (half + 1)))
                    return part_h[slot], part_l[slot]

                def columns(n, banks, kc, movh, movl):
                    for c, b in enumerate(banks):
                        if c % (len(banks) // 2) == 0:
                            ph, pl = piece(n, n % 2, c // (len(banks) // 2))
                        for k in range(kc):
                            w = slice((c * kc + k) * P, (c * kc + k + 1) * P)
                            ins = product(b[:], ph[:, w], pl[:, w], movh[:, k, :], movl[:, k, :],
                                          k == 0, k == kc - 1)
                    ins.then_inc(used.sem, 1)

                for pair in range(2):
                    if pair == 1:
                        turn_x([2, 3], TURN_HIGH, lambda n: x_normed.at(l, n - TB))
                    for n in range(2):
                        ph, pl = piece(P_Q + n, (P_Q + n) % 2)
                        for tb in (2 * pair, 2 * pair + 1):
                            pe.wait_ge(xt_low.sem, xt_low.at(l, 2 * tb + 2 - TB))
                            for k in range(4):
                                if k == 2:
                                    piece(P_Q + n, (P_Q + n) % 2, 1)
                                kk, ts, w = 4 * n + k, slice(tb * P, (tb + 1) * P), slice(k * S, (k + 1) * S)
                                ins = product(bank[tb][:], XTh[:, kk, ts], XTl[:, kk, ts], ph[:, w], pl[:, w],
                                              kk == 0, kk == KD - 1)
                        if pair == 1:
                            ins.then_inc(used.sem, 1)
                for n in range(2):
                    columns(P_XF + n, [bank[XF_BANK[2 * n]], bank[XF_BANK[2 * n + 1]]], KD, XTh, XTl)
                for tb in range(TB):
                    pe.wait_ge(q_copied.sem, q_copied.at(l, tb // 2 + 1))
                    for k in range(KD):
                        if k % (KD // 2) == 0:
                            ph, pl = piece(P_KV, P_KV % 2, k // (KD // 2))
                        ts, w = slice(tb * P, (tb + 1) * P), slice(k * 256, (k + 1) * 256)
                        ins = product(bank[tb // 2][:, (tb % 2) * 256:(tb % 2 + 1) * 256], XTh[:, k, ts],
                                      XTl[:, k, ts], ph[:, w], pl[:, w], k == 0, k == KD - 1)
                ins.then_inc(used.sem, 1)
                pe.wait_ge(xf_copied.sem, xf_copied.at(l, GROUPS))
                for g in range(GROUPS):
                    ins = nc.tensor.matmul(bank[CHAN_BANK[0]][0:1, g * P:(g + 1) * P], xfT[:, g, HALF:HALF + 1],
                                           dft[:, 0:P], start=True, stop=True)
                ins.then_inc(chan_done.sem, 1)
                pe.wait_ge(q_copied.sem, q_copied.at(l, TB))
                for g in range(GROUPS):
                    pe.wait_ge(folded.sem, folded.at(l, g + 1))
                    for a in range(4):
                        ins = nc.tensor.matmul(bank[CHAN_BANK[g + 1]][:, a * P:(a + 1) * P],
                                               even_odd[:, g, a // 2, (a % 2) * P:(a % 2 + 1) * P],
                                               dft[:, (a // 2) * P:(a // 2 + 1) * P], start=True, stop=True)
                    ins.then_inc(chan_done.sem, 1)
                pe.wait_ge(kv_copied.sem, kv_copied.at(l, 2))
                ph, pl = piece(P_DFT, P_DFT % 2, 1)
                for g in range(GROUPS):
                    pe.wait_ge(chan_low.sem, chan_low.at(l, g + 2))
                    yc, ys = bank[COS_BANK[g]][:, 0:NCOS], bank[SIN_BANK[g]][:, 0:HALF]
                    for a in range(2):
                        w = slice(a * NCOS, (a + 1) * NCOS)
                        product(yc, Zh[:, g, a, :], Zl[:, g, a, :], ph[:, w], pl[:, w], a == 0, False)
                    w = slice(T_MID, T_MID + NCOS)
                    product(yc, mid_h[0:1, g, :], mid_l[0:1, g, :], ph[0:1, w], pl[0:1, w], False, True)
                    for a in range(2):
                        w = slice(T_SIN + a * HALF, T_SIN + (a + 1) * HALF)
                        ins = product(ys, Zh[:, g, 2 + a, :], Zl[:, g, 2 + a, :], ph[:, w], pl[:, w], a == 0, a == 1)
                    ins.then_inc(y_done.sem if g < GROUPS - 1 else used.sem, 1)

                def scores(u):
                    h, tb = u // TB, u % TB
                    q, g = stacked(h)[:, tb * P:(tb + 1) * P], h // PAIRS
                    if u >= 2:
                        pe.wait_ge(exped.sem, exped.at(l, u - 1))
                    nc.tensor.matmul(bank[u % 2][:], q, k_stack[g][:], start=True, stop=False)
                    nc.tensor.matmul(bank[u % 2][:], q[0:HD, :], k_low[g][0:HD, :], start=False,
                                     stop=True).then_inc(scored.sem, 1)

                def turn_probs(u):
                    pe.wait_ge(prob_ready.sem, prob_ready.at(l, u + 1))
                    if u >= 2:
                        pe.wait_ge(p_copied.sem, p_copied.at(l, u - 1))
                    for s in range(TB):
                        ins = nc.tensor.transpose(bank[2 + u % 2][:, s * P:(s + 1) * P],
                                                  prob[:, u % 2, s * P:(s + 1) * P], ident)
                    ins.then_inc(p_turned.sem, 1)

                def values(h):
                    pe.wait_ge(p_copied.sem, p_copied.at(l, TB * (h + 1)))
                    if h >= 2:
                        pe.wait_ge(o_low.sem, o_low.at(l, h - 1))
                    for s in range(TB):
                        ins = nc.tensor.matmul(bank[4 + h % 2][:], qkv[:, s, NORMED * HD:QKV], PT[:, h % 2, s, :],
                                               start=(s == 0), stop=(s == TB - 1))
                    ins.then_inc(pv_done.sem, 1)

                def filler():
                    n = P_GF
                    for i, (kind, m) in enumerate(FILL):
                        per = FILL_PER[kind]
                        kc = FILL_LEN[kind]
                        mvh, mvl = (yTh, yTl) if kind == "wf" else (XTh, XTl)
                        if i < 2:
                            pe.wait_ge(y_summed.sem, y_summed.at(l, 2 - i))
                        if kind == "wf" and m == 0:
                            pe.wait_ge(y_low.sem, y_low.at(l, GROUPS))
                        if m % (per // 2) == 0:
                            ph, pl = piece(n, n % 2, m % per // (per // 2))
                        if i >= 2:
                            k2, m2 = FILL[i - 2]
                            done = {"gf": gatef, "wf": yf_gated, "ga": gatea}[k2]
                            pe.wait_ge(done.sem, done.at(l, m2 + 1))
                        for k in range(kc):
                            w = slice((m % per * kc + k) * P, (m % per * kc + k + 1) * P)
                            ins = product(bank[6 + i % 2][:], ph[:, w], pl[:, w], mvh[:, k, :], mvl[:, k, :],
                                          k == 0, k == kc - 1)
                            if k == kc - 1:
                                ins.then_inc(used.sem if m % per == per - 1 else fill_done.sem, 1)
                            yield
                        n += m % per == per - 1

                fill = filler()
                for _ in range(FILL_DFT):
                    next(fill)
                pe.wait_ge(y_summed.sem, y_summed.at(l, GROUPS))
                pe.wait_ge(qk_low.sem, qk_low.at(l, TB))
                for i in range(HEADS + 4):
                    if i == HEADS:
                        for _ in range(FILL_Q):
                            next(fill)
                        pe.wait_ge(qk_low.sem, qk_low.at(l, TB + 1))
                    if i >= 6:
                        pe.wait_ge(qk_copied.sem, qk_copied.at(l, i - 5))
                    for tb in range(TB):
                        if i < HEADS:
                            src = q_split[:, tb, 2 * (i % PAIRS) + i // PAIRS, :, :].rearrange("p a d -> p (a d)")
                        else:
                            g, low = (i - HEADS) // 2, (i - HEADS) % 2
                            src = k_split[:, tb, g, 1 - low:3 - low, :].rearrange("p a d -> p (a d)")
                        ins = nc.tensor.transpose(bank[i % 6][:, tb * P:(tb + 1) * P], src.bitcast(F32), ident)
                    ins.then_inc(qk_turned.sem, 1)
                for _ in range(FILL_QK):
                    next(fill)
                pe.wait_ge(qk_copied.sem, qk_copied.at(l, HEADS + 4))
                scores(0)
                for u in range(32):
                    if u + 1 < 32:
                        scores(u + 1)
                    for _ in range(FILL_STEP[u]):
                        next(fill)
                    turn_probs(u)
                    if u % TB == 1 and u > TB:
                        values(u // TB - 1)
                for _ in range(FILL_TURNED):
                    next(fill)
                values(HEADS - 1)
                for _ in range(FILL_VALUES):
                    next(fill)
                assert next(fill, "all") == "all"

                pe.wait_ge(p_copied.sem, p_copied.at(l, 32))
                pe.wait_ge(o_low.sem, o_low.at(l, HEADS))
                for m in range(KD):
                    n = P_WA + m // 4
                    if m % 2 == 0:
                        ph, pl = piece(n, n % 2, m % 4 // 2)
                    if m >= 4:
                        pe.wait_ge(ya_gated.sem, ya_gated.at(l, m - 3))
                    for k in range(PAIRS):
                        w = slice((m % 4 * PAIRS + k) * P, (m % 4 * PAIRS + k + 1) * P)
                        ins = product(bank[m % 4][:], ph[:, w], pl[:, w], oTh[:, k, :], oTl[:, k, :],
                                      k == 0, k == PAIRS - 1)
                    ins.then_inc(wa_done.sem if m % 4 < 3 else used.sem, 1)
                def out_rows(dst, n, tb):
                    ph, pl = piece(P_OUT + n, (P_OUT + n) % 2)
                    for k in range(KD):
                        if k == KD // 2:
                            piece(P_OUT + n, (P_OUT + n) % 2, 1)
                        if n == 0 and tb == 0:
                            pe.wait_ge(mixed_low.sem, mixed_low.at(l, k + 1))
                        ts, w = slice(tb * P, (tb + 1) * P), slice(k * 256, (k + 1) * 256)
                        ins = product(dst, XTh[:, k, ts], XTl[:, k, ts], ph[:, w], pl[:, w], k == 0, k == KD - 1)
                    return ins

                pe.wait_ge(ya_gated.sem, ya_gated.at(l, KD))
                for n in range(2):
                    for tb in range(TB):
                        ins = out_rows(bank[4 + 2 * n + tb // 2][:, (tb % 2) * 256:(tb % 2 + 1) * 256], n, tb)
                    ins.then_inc(used.sem, 1)
                for tb, n in BLOCK_ORDER:
                    ins = out_rows(bank[tb][:, n * 256:(n + 1) * 256], 2 + n, tb)
                    if tb == TB - 1:
                        ins.then_inc(used.sem, 1)
                    elif n == 1:
                        ins.then_inc(rows_done.sem, 1)
                pe.wait_ge(resid.sem, resid.at(l, 4))
                for pair in range(2):
                    tbs = [2 * pair, 2 * pair + 1]
                    turn_x(tbs, [4, 5, 6, 7], lambda n: x_normed.at(l, n),
                           None if pair == 0 else lambda i: xt_low.at(l, TB + i + 1))
                    pe.wait_ge(xt_low.sem, xt_low.at(l, 2 * TB + TB * pair))
                    for h in range(2):
                        if pair == 0 and h == 1:
                            pe.wait_ge(resid.sem, resid.at(l, 4 + TB))
                        ts = slice(pair * 2 * P, (pair + 1) * 2 * P)
                        for f in range(2):
                            ph, pl = piece(P_QUERY + h, (P_QUERY + h) % 2, f)
                            for k in range(KD):
                                w = slice((f * KD + k) * P, (f * KD + k + 1) * P)
                                ins = product(bank[2 * h + f][:, ts], ph[:, w], pl[:, w], XTh[:, k, ts], XTl[:, k, ts],
                                              k == 0, k == KD - 1)
                        if pair == 1:
                            ins.then_inc(used.sem, 1)

                def early_product(i, base, j, first):
                    c, k = divmod(j, KD)
                    slot = (2 * i + c) % 4
                    if k == 0:
                        piece(base + (P_TAB + i), i % 2, c)
                    if k == 0 and not (first and 2 * i + c < 4):
                        pe.wait_ge(early_out.sem, early_out.at(l, 2 * base + (2 * i + c - 3)))
                    w = slice(j * P, (j + 1) * P)
                    ins = product(bank[slot][:], part_h[i % 2][:, w], part_l[i % 2][:, w], XTh[:, k, :],
                                  XTl[:, k, :], k == 0, k == KD - 1)
                    if k == KD - 1:
                        ins.then_inc(early_first.sem if c == 0 else used.sem, 1)

                def key_scores(h):
                    if h == 0:
                        pe.wait_ge(key_in.sem, key_in.at(l, 16))
                    pe.wait_ge(qr_copied.sem, qr_copied.at(l, h + 1))
                    if h >= 2:
                        pe.wait_ge(ks_copied.sem, ks_copied.at(l, h - 1))
                    for f in range(2):
                        for tb in range(TB):
                            ins = nc.tensor.matmul(bank[4 + 2 * (h % 2) + f][:, tb * P:(tb + 1) * P],
                                                   qrT[:, h % 2, f, tb * P:(tb + 1) * P], keyT[:, 2 * h + f, :],
                                                   start=True, stop=True)
                    ins.then_inc(key_scored.sem, 1)

                key_scores(0)
                for h in range(2, RH):
                    pe.wait_ge(qr_copied.sem, qr_copied.at(l, h - 1))
                    columns(P_QUERY + h, [bank[2 * (h % 2)], bank[2 * (h % 2) + 1]], KD, XTh, XTl)
                    if h < RH - 1:
                        key_scores(h - 1)
                pe.wait_ge(qr_copied.sem, qr_copied.at(l, RH - 1))
                for i in range(E_BEFORE - 1):
                    for j in range(2 * KD):
                        if i == 0 and j == KD:
                            pe.wait_ge(qr_copied.sem, qr_copied.at(l, RH))
                        early_product(i, 0, j, True)
                    if i in KEYS_BESIDE:
                        key_scores(RH - 2 + KEYS_BESIDE.index(i))
                pe.wait_ge(ks_copied.sem, ks_copied.at(l, RH))
                for j in range(KD):
                    early_product(E_BEFORE - 1, 0, j, True)
                for tb in range(TB):
                    pe.wait_ge(routed.sem, routed.at(l, tb + 1))
                    for a in range(3):
                        ins = nc.tensor.transpose(bank[4 + tb][:, a * P:(a + 1) * P], route[:, tb, a, :], ident)
                    ins.then_inc(route_turned.sem, 1)
                for j in range(KD, 2 * KD):
                    early_product(E_BEFORE - 1, 0, j, True)

                def dense_gates(b, first):
                    for q in range(16):
                        if q % 2 == 0:
                            pe.wait_ge(hots.sem, hots.at(l, 8 * b + (q // 2 + 1)))
                        if not (first and q < 4):
                            pe.wait_ge(gate_copied.sem, gate_copied.at(l, 16 * b + (q - 3)))
                        for t in range(4):
                            dst = bank[4 + q % 4][:, t * P:(t + 1) * P]
                            at = (slice(None), q // 2 % 2, q % 2, slice(None), t)
                            nc.tensor.matmul(dst, hot1[at], hot2h[at], start=True, stop=False)
                            ins = nc.tensor.matmul(dst, hot1[at], hot2l[at], start=False, stop=True)
                        ins.then_inc(gated.sem, 1)
                        for j in range(2):
                            early_product(E_BEFORE + q // 8, 2 * b, 2 * (q % 8) + j, False)

                pe.wait_ge(route_copied.sem, route_copied.at(l, TB))
                pe.wait_ge(w_split.sem, w_split.at(l, TB))
                dense_gates(0, True)
                with pe.Fori(1, S // 64) as b:
                    dense_gates(b, False)
                for i in range(E_AFTER):
                    for j in range(2 * KD):
                        early_product(E_BEFORE + E_WITHIN + i, 0, j, False)
                pe.wait_ge(gate_copied.sem, gate_copied.at(l, S // 4))

                def up(g, half, n, slot, first):
                    for c in (2 * half, 2 * half + 1):
                        ph, pl = piece(n, slot, c % 2)
                        if not first:
                            pe.wait_ge(act_out.sem, act_out.at(l, CG * g + (c - 3 - CG * EG)))
                        for k in range(KD):
                            w = slice(((c % 2) * KD + k) * P, ((c % 2) * KD + k + 1) * P)
                            ins = product(bank[c][:], ph[:, w], pl[:, w], XTh[:, k, :], XTl[:, k, :],
                                          k == 0, k == KD - 1)
                        ins.then_inc(u_first.sem if c % 2 == 0 else used.sem, 1)

                def weighed_rows(dst, par, n, slot, tb):
                    ph, pl = piece(n, slot)
                    for c in range(CG):
                        if c == CG // 2:
                            piece(n, slot, 1)
                        ts, w = slice(tb * P, (tb + 1) * P), slice(c * S, (c + 1) * S)
                        ins = product(dst[:], Wh[:, par, c, ts], Wl[:, par, c, ts], ph[:, w], pl[:, w],
                                      c == 0, c == CG - 1)
                    return ins

                def down(g, par, half, n, slot, first):
                    pe.wait_ge(w_low.sem, w_low.at(l, CG * g + CG))
                    for s in range(2):
                        if not first:
                            pe.wait_ge(y_added.sem, y_added.at(l, 4 * g + (2 * half + s - 1)))
                        for tb in (2 * s, 2 * s + 1):
                            ins = weighed_rows(bank[4 + tb], par, n, slot, tb)
                        ins.then_inc(v_first.sem if s == 0 else used.sem, 1)

                def down_group(g, par, n, first):
                    down(g, par, 0, n, 0, first)
                    down(g, par, 1, n + 1, 1, False)

                def both_group(g, par, n, first):
                    up(g + 1, 0, n, 0, first)
                    down(g, par, 0, n + 1, 1, False)
                    up(g + 1, 1, n + 2, 0, first)
                    down(g, par, 1, n + 3, 1, False)

                down_group(0, 0, P_VA, True)
                with pe.Fori(0, EG // 2 - 1) as m:
                    down_group(2 * m + 1, 1, 4 * m + (P_VA + 2), False)
                    down_group(2 * m + 2, 0, 4 * m + (P_VA + 4), False)
                pe.wait_ge(early_out.sem, early_out.at(l, CG * EG))
                both_group(EG - 1, 1, P_UV, True)
                both_group(EG, 0, P_UV + 4, False)
                with pe.Fori(EG // 2, NG // 2 - 1) as m:
                    both_group(2 * m + 1, 1, 8 * m + (P_UV - 4 * (EG - 2)), False)
                    both_group(2 * m + 2, 0, 8 * m + (P_UV - 4 * (EG - 3)), False)
                pe.wait_ge(w_low.sem, w_low.at(l, CG * NG))
                for tb, n in BLOCK_ORDER:
                    if tb == 2:
                        pe.wait_ge(y_added.sem, y_added.at(l, 4 * NG - 4))
                    ins = weighed_rows(bank[2 * tb + n], 1, V_LAST + n, n, tb)
                    if tb == TB - 1:
                        ins.then_inc(used.sem, 1)
                    elif n == 1:
                        ins.then_inc(rows_done.sem, 1)
                turn_x([0, 1], TURN_LOW, lambda n: x_normed.at(l, TB + n))


def token_order():
    import numpy as np
    return np.concatenate([np.arange(HALF + 1), np.arange(S - 1, HALF, -1)])


def shape_tables():
    import numpy as np
    c = np.zeros((P, N_CONST), np.float64)
    c[:, C_IDENT:C_IDENT + P] = np.eye(P)
    c[:, C_IOTA:C_IOTA + P] = np.arange(P)
    a = 2 * np.pi * (np.outer(np.arange(P), np.arange(P)) % P) / P
    c[:, C_DFT:C_DFT + P], c[:, C_DFT + P:C_DFT + 2 * P] = np.cos(a), np.sin(a)
    pos = token_order()
    inv = (1.0 / (np.float32(10000.0) ** (np.arange(0, HD // 2, 2, dtype=np.float32) / np.float32(HD // 2))))
    inv = inv.astype(np.float32)
    row = (pos // 64).astype(np.float32)[:, None] * inv
    col = (pos % 64).astype(np.float32)[:, None] * inv
    ang = np.concatenate([row, row, col, col], 1).astype(np.float64)
    sign = np.tile(np.repeat([-1.0, 1.0], HD // 4), 2)
    c[:, C_COS:C_COS + TB * HD] = np.cos(ang).reshape(TB, P, HD).transpose(1, 0, 2).reshape(P, -1)
    c[:, C_SIN:C_SIN + TB * HD] = (np.sin(ang) * sign).reshape(TB, P, HD).transpose(1, 0, 2).reshape(P, -1)
    b = 2 * np.pi * (np.outer(np.arange(HALF), np.arange(HALF + 1)) % S) / S
    scale = 1.0 / np.sqrt(float(S * P))
    pos_dft = np.zeros((P, PIECE))
    for a in range(2):
        rows = b[a * P:(a + 1) * P]
        pos_dft[:, a * NCOS:a * NCOS + HALF + 1] = np.cos(rows) * scale
        pos_dft[:, T_SIN + a * HALF:T_SIN + (a + 1) * HALF] = np.sin(rows[:, :HALF]) * scale
    pos_dft[0, T_MID:T_MID + HALF + 1] = scale * (1 - 2 * (np.arange(HALF + 1) % 2))
    return c.astype(np.float32), pos_dft.astype(np.float32)


def chunk_pieces(w, per):
    k, m = w.shape[0] // P, w.shape[1] // P
    return w.reshape(k, P, m // per, per, P).transpose(2, 1, 3, 0, 4).reshape(m // per, P, PIECE)


def kernel(x, ln0_g, ln0_b, w_in, b_gate, q_norm_g, k_norm_g, w_branch_fourier, w_branch_attn, w_out,
           ln1_g, ln1_b, peer_w_query, peer_sub_keys, peer_u, peer_v, ln2_g, ln2_b):
    import numpy as np
    import concourse.bacc as bacc
    from concourse.bass_utils import run_bass_kernel_spmd as run

    consts, pos_dft = shape_tables()
    order = [g * PAIRS + j for j in range(PAIRS) for g in range(KV_HEADS)]
    DF = GROUPS * P
    stream = np.zeros((DEPTH, NP, P, PIECE), np.float32)
    for l in range(DEPTH):
        w = np.asarray(w_in[l])
        st = stream[l]
        st[P_XF:P_XF + 2] = chunk_pieces(w[:, 0:DF], 2)
        wq = w[:, DF:DF + S].reshape(D, HEADS, HD)[:, order].reshape(2, 4, P, S)
        st[P_Q:P_Q + 2] = wq.transpose(0, 2, 1, 3).reshape(2, P, PIECE)
        st[P_KV] = w[:, DF + S:DF + S + 256].reshape(KD, P, 256).transpose(1, 0, 2).reshape(P, PIECE)
        st[P_DFT] = pos_dft
        g0 = DF + S + 256
        st[P_GF:P_GF + 4] = chunk_pieces(w[:, g0:g0 + D], 2)
        st[P_GA:P_GA + 4] = chunk_pieces(w[:, g0 + D:g0 + 2 * D], 2)
        st[P_WF:P_WF + 2] = chunk_pieces(np.asarray(w_branch_fourier[l]), 4)
        wa = np.asarray(w_branch_attn[l]).reshape(HEADS, HD, D)[order].reshape(DF, D)
        st[P_WA:P_WA + 2] = chunk_pieces(wa, 4)
        wo = np.asarray(w_out[l]).reshape(KD, P, 4, 256)
        st[P_OUT:P_OUT + 4] = wo.transpose(2, 1, 0, 3).reshape(4, P, PIECE)
        st[P_QUERY:P_QUERY + RH] = chunk_pieces(np.asarray(peer_w_query[l]), 2)
        u = np.asarray(peer_u[l]).reshape(KEYS, 2 * NG, 2, KD, P).transpose(1, 4, 2, 3, 0).reshape(2 * NG, P, PIECE)
        v = np.asarray(peer_v[l]).reshape(KEYS, NG, CG, 2, S).transpose(1, 3, 0, 2, 4).reshape(2 * NG, P, PIECE)
        st[P_TAB:P_VA] = u[0:2 * EG]
        st[P_VA:P_UV] = v[0:2 * (EG - 1)]
        st[P_UV:V_LAST:2] = u[2 * EG:]
        st[P_UV + 1:V_LAST:2] = v[2 * (EG - 1):-2]
        st[V_LAST:] = v[-2:]
    keys = np.asarray(peer_sub_keys).reshape(DEPTH, 2 * RH, KEYS, P).transpose(0, 3, 1, 2)
    arrays = {
        "x": np.asarray(x).reshape(S, D)[token_order()],
        "stream": stream,
        "keys": np.ascontiguousarray(keys),
        "ln0": np.stack([np.asarray(ln0_g), np.asarray(ln0_b)]),
        "ln1": np.stack([np.asarray(ln1_g), np.asarray(ln1_b)], 1),
        "ln2": np.stack([np.asarray(ln2_g), np.asarray(ln2_b)], 1),
        "qk_gain": np.stack([np.asarray(q_norm_g), np.asarray(k_norm_g)], 1),
        "gate_bias": np.ascontiguousarray(np.asarray(b_gate).reshape(DEPTH, 2, KD, P).transpose(0, 3, 1, 2)),
        "consts": consts,
    }
    nc = bacc.Bacc("TRN2", target_bir_lowering=False, num_devices=1)
    args = [nc.dram_tensor(n, a.shape, F32, kind="ExternalInput").ap() for n, a in arrays.items()]
    out = nc.dram_tensor("out", (S, D), F32, kind="ExternalOutput").ap()
    build(nc, *args, out)
    r = run(nc, [arrays], core_ids=[0])
    y = np.empty((S, D), np.float32)
    y[token_order()] = np.asarray(r.results[0]["out"])
    return y.reshape(1, S, D)
```
